# Optimizing a Trainium2 kernel written in Bass

```python
import jax
import jax.numpy as jnp
from jax import lax
import numpy as np
import math
import jax, jax.numpy as jnp

D_MODEL = 1024
BATCH = 1
SEQ = 1024
DEPTH = 1

N_BRANCH = 4
HEADS = 4
BRANCH_WIDTH = D_MODEL // 4
HEAD_DV = BRANCH_WIDTH // HEADS
RET_DK = HEAD_DV // 2
GLA_DK = HEAD_DV // 2
HGRN_DK = HEAD_DV
RWKV_N = HEAD_DV
RWKV_W_LORA = 64
RWKV_A_LORA = 64
RWKV_G_LORA = 128
GLA_GATE_LORA = 16
GLA_GATE_TEMP = 16.0
CHUNK = 64
RET_ROPE_BASE = 10000.0
RWKV_DECAY_SCALE = 0.6065306597126334
D_FF = 2816
FFN_CONV_WIDTH = 3
PLE_DIM = 256
LN_EPS = 1e-5
HEAD_EPS = 1e-6
RWKV_GN_EPS = 64e-5
ALPHA = (2.0 * DEPTH) ** 0.25
BETA = (8.0 * DEPTH) ** -0.25

RET_COLS = (HEADS * RET_DK, HEADS * RET_DK, BRANCH_WIDTH, BRANCH_WIDTH)
RWKV_COLS = (BRANCH_WIDTH, BRANCH_WIDTH, BRANCH_WIDTH, RWKV_W_LORA, RWKV_A_LORA, RWKV_G_LORA)
GLA_COLS = (HEADS * GLA_DK, HEADS * GLA_DK, BRANCH_WIDTH, GLA_GATE_LORA, BRANCH_WIDTH)
HGRN_COLS = (HEADS * HGRN_DK, HEADS * HGRN_DK, BRANCH_WIDTH, BRANCH_WIDTH)
GROUP_COLS = (sum(RET_COLS), sum(RWKV_COLS), sum(GLA_COLS), sum(HGRN_COLS), N_BRANCH * D_MODEL)
N_IN = sum(GROUP_COLS)


def split_cols(a, sizes):
    return jnp.split(a, [int(c) for c in np.cumsum(sizes)[:-1]], axis=-1)

def heads(a, n_heads=HEADS):
    return a.reshape(*a.shape[:-1], n_heads, a.shape[-1] // n_heads)

def bhsd(a):
    return a.transpose(0, 2, 1, 3)

def shift_right(a):
    return jnp.pad(a, ((0, 0), (1, 0), (0, 0)))[:, :-1]

def layer_norm(x, w, b):
    x32 = x.astype(jnp.float32)
    mu = jnp.mean(x32, -1, keepdims=True)
    var = jnp.mean(jnp.square(x32 - mu), -1, keepdims=True)
    return ((x32 - mu) * lax.rsqrt(var + LN_EPS) * w + b).astype(x.dtype)

def head_norm(y, eps):
    y = y.astype(jnp.float32)
    mu = jnp.mean(y, -1, keepdims=True)
    var = jnp.mean(jnp.square(y - mu), -1, keepdims=True)
    return (y - mu) * lax.rsqrt(var + eps)

def head_rms(y, gain):
    y = y.astype(jnp.float32)
    return y * lax.rsqrt(jnp.mean(jnp.square(y), -1, keepdims=True) + HEAD_EPS) * gain

def rotary(x):
    S, d = x.shape[1], x.shape[-1]
    theta = 1.0 / (RET_ROPE_BASE ** jnp.linspace(0.0, 1.0, d // 2))
    ang = jnp.arange(S, dtype=jnp.float32)[:, None] * theta[None, :]
    cos, sin = jnp.cos(ang)[:, None, :], jnp.sin(ang)[:, None, :]
    xr = x.astype(jnp.float32).reshape(*x.shape[:-1], d // 2, 2)
    x1, x2 = xr[..., 0], xr[..., 1]
    return jnp.stack([x1 * cos - x2 * sin, x1 * sin + x2 * cos], -1).reshape(x.shape)

def to_chunks(a):
    B, H, T, d = a.shape
    return a.reshape(B, H, T // CHUNK, CHUNK, d).transpose(2, 0, 1, 3, 4)

def from_chunks(o):
    n, B, H, C, d = o.shape
    return o.transpose(1, 2, 0, 3, 4).reshape(B, H, n * C, d)

def retention_chunkwise(q, k, v, log_gamma):
    B, H, T, dk = q.shape
    dv = v.shape[-1]
    pos = jnp.arange(CHUNK, dtype=jnp.float32)
    causal = pos[:, None] >= pos[None, :]
    rel = jnp.where(causal, pos[:, None] - pos[None, :], 0.0)
    decay = jnp.where(causal[None], jnp.exp(log_gamma[:, None, None] * rel[None]), 0.0)
    xi = jnp.exp(log_gamma[:, None] * (pos + 1.0))[None, :, :, None]
    zeta = jnp.exp(log_gamma[:, None] * (CHUNK - 1.0 - pos))[None, :, :, None]
    gamma_c = jnp.exp(log_gamma * CHUNK)[None, :, None, None]

    def step(R, inp):
        qc, kc, vc = inp
        scores = jnp.einsum('bhtd,bhsd->bhts', qc, kc) * decay[None]
        o = jnp.einsum('bhts,bhse->bhte', scores, vc) + jnp.einsum('bhtd,bhde->bhte', qc, R) * xi
        R = gamma_c * R + jnp.einsum('bhsd,bhse->bhde', kc, vc * zeta)
        return R, o

    R0 = jnp.zeros((B, H, dk, dv), jnp.float32)
    _, o = lax.scan(step, R0, (to_chunks(q), to_chunks(k), to_chunks(v)))
    return from_chunks(o)

def chunk_gated_linear_attention(q, k, v, log_g):
    B, H, T, dk = q.shape
    dv = v.shape[-1]
    causal = jnp.tril(jnp.ones((CHUNK, CHUNK), bool))[:, :, None]

    def step(S, inp):
        qc, kc, vc, gc = inp
        b = jnp.cumsum(gc, axis=2)
        diff = b[:, :, :, None, :] - b[:, :, None, :, :]
        decay = jnp.where(causal, jnp.exp(jnp.where(causal, diff, 0.0)), 0.0)
        scores = jnp.einsum('bhtd,bhsd,bhtsd->bhts', qc, kc, decay)
        o = jnp.einsum('bhts,bhse->bhte', scores, vc) + jnp.einsum('bhtd,bhde->bhte', qc * jnp.exp(b), S)
        b_last = b[:, :, -1:, :]
        S = jnp.exp(b_last[:, :, 0, :, None]) * S + jnp.einsum('bhsd,bhse->bhde', kc * jnp.exp(b_last - b), vc)
        return S, o

    S0 = jnp.zeros((B, H, dk, dv), jnp.float32)
    _, o = lax.scan(step, S0, (to_chunks(q), to_chunks(k), to_chunks(v), to_chunks(log_g)))
    return from_chunks(o)

def rwkv7_recurrence(r, w, k, v, kk, a):
    B, S, H, N = r.shape
    seq = tuple(t.transpose(1, 0, 2, 3) for t in (r, w, k, v, kk, a))

    def step(state, inp):
        rt, wt, kt, vt, kkt, at = inp
        sa = jnp.einsum('bhvk,bhk->bhv', state, kkt)
        state = state * wt[:, :, None, :] - sa[..., None] * (kkt * at)[:, :, None, :] + vt[..., None] * kt[:, :, None, :]
        return state, jnp.einsum('bhvk,bhk->bhv', state, rt)

    _, y = lax.scan(step, jnp.zeros((B, H, N, N), jnp.float32), seq)
    return y.transpose(1, 0, 2, 3)

def retnet_branch(z):
    B, S, _ = z.shape
    q, k, v, g = split_cols(z.astype(jnp.float32), RET_COLS)
    q = rotary(heads(q))
    k = rotary(heads(k)) * RET_DK ** -0.5
    log_gamma = jnp.log1p(-jnp.exp2(-5.0 - jnp.arange(HEADS, dtype=jnp.float32)))
    o = retention_chunkwise(bhsd(q), bhsd(k), bhsd(heads(v)), log_gamma)
    o = head_norm(bhsd(o), HEAD_EPS).reshape(B, S, BRANCH_WIDTH)
    return (jax.nn.silu(g) * o).astype(z.dtype)

def rwkv7_branch(z, mu, w0, w2, a0, a2, g2, k_k, k_a, r_k, ln_w, ln_b):
    B, S, _ = z.shape
    z = z.astype(jnp.float32)
    z = z + (shift_right(z) - z) * mu
    r, k, v, wl, al, gl = split_cols(z, RWKV_COLS)
    w = jnp.exp(-RWKV_DECAY_SCALE * jax.nn.sigmoid(w0 + jnp.tanh(wl) @ w2))
    a = jax.nn.sigmoid(a0 + al @ a2)
    g = jax.nn.sigmoid(gl) @ g2
    kk = heads(k * k_k)
    kk = kk * lax.rsqrt(jnp.sum(jnp.square(kk), -1, keepdims=True) + 1e-12)
    k = k * (1.0 + (a - 1.0) * k_a)
    rh, kh, vh = heads(r), heads(k), heads(v)
    y = rwkv7_recurrence(rh, heads(w), kh, vh, kk, heads(a))
    y = head_norm(y, RWKV_GN_EPS).reshape(B, S, BRANCH_WIDTH) * ln_w + ln_b
    bonus = (jnp.sum(rh * kh * r_k, -1, keepdims=True) * vh).reshape(B, S, BRANCH_WIDTH)
    return ((y + bonus) * g).astype(z.dtype)

def gla_branch(z, w2, b, norm_w):
    B, S, _ = z.shape
    q, k, v, gl, g = split_cols(z.astype(jnp.float32), GLA_COLS)
    log_alpha = jax.nn.log_sigmoid(gl @ w2 + b) / GLA_GATE_TEMP
    o = chunk_gated_linear_attention(bhsd(heads(q) * GLA_DK ** -0.5), bhsd(heads(k)), bhsd(heads(v)), bhsd(heads(log_alpha)))
    o = head_rms(bhsd(o), norm_w).reshape(B, S, BRANCH_WIDTH)
    return (o * jax.nn.silu(g)).astype(z.dtype)

def hgrn2_branch(z, lb, norm_w):
    B, S, _ = z.shape
    q, fz, i, g = split_cols(z.astype(jnp.float32), HGRN_COLS)
    f = lb + (1.0 - lb) * jax.nn.sigmoid(fz)
    log_f = jnp.log(f)
    k = (1.0 - lb) * jax.nn.sigmoid(-fz)
    o = chunk_gated_linear_attention(bhsd(heads(q)), bhsd(heads(k)), bhsd(heads(i)), bhsd(heads(log_f)))
    o = head_rms(bhsd(o), norm_w).reshape(B, S, BRANCH_WIDTH)
    return (o * jax.nn.silu(g)).astype(z.dtype)

def conv_ffn(x, w_up, conv_w, w_down):
    S = x.shape[1]
    u, v = jnp.split(x @ w_up, 2, axis=-1)
    up = jnp.pad(u, ((0, 0), (FFN_CONV_WIDTH - 1, 0), (0, 0)))
    u = sum(conv_w[j] * up[:, j:j + S] for j in range(FFN_CONV_WIDTH))
    return (jax.nn.gelu(u) * v) @ w_down

def _normal(k, shape, scale):
    return scale * jax.random.normal(k, shape, jnp.float32)

def first_inputs(seed: int = 0) -> dict:
    key = jax.random.key(seed)
    k = jax.random.split(key, 32)
    L, D, W = DEPTH, D_MODEL, BRANCH_WIDTH
    return {
        'x': _normal(k[0], (BATCH, SEQ, D), 1.0),
        'p': _normal(k[1], (DEPTH, BATCH, SEQ, PLE_DIM), 1.0),
        'ln_in_w': 1.0 + _normal(k[2], (D,), 0.02),
        'ln_in_b': _normal(k[3], (D,), 0.02),
        'w_in': _normal(k[4], (L, D, N_IN), D ** -0.5),
        'rwkv_mu': jax.random.uniform(k[5], (L, sum(RWKV_COLS)), jnp.float32),
        'rwkv_w0': _normal(k[6], (L, W), 0.5),
        'rwkv_w2': _normal(k[7], (L, RWKV_W_LORA, W), 0.5 * RWKV_W_LORA ** -0.5),
        'rwkv_a0': _normal(k[8], (L, W), 0.1),
        'rwkv_a2': _normal(k[9], (L, RWKV_A_LORA, W), 0.5 * RWKV_A_LORA ** -0.5),
        'rwkv_g2': _normal(k[10], (L, RWKV_G_LORA, W), RWKV_G_LORA ** -0.5),
        'rwkv_k_k': 0.85 + _normal(k[11], (L, W), 0.05),
        'rwkv_k_a': 1.0 + _normal(k[12], (L, W), 0.05),
        'rwkv_r_k': _normal(k[13], (L, HEADS, RWKV_N), 0.1),
        'rwkv_ln_w': 1.0 + _normal(k[14], (L, W), 0.02),
        'rwkv_ln_b': _normal(k[15], (L, W), 0.02),
        'gla_w2': _normal(k[16], (L, GLA_GATE_LORA, HEADS * GLA_DK), GLA_GATE_LORA ** -0.5),
        'gla_b': _normal(k[17], (L, HEADS * GLA_DK), 0.1),
        'gla_norm_w': 1.0 + _normal(k[18], (L, HEAD_DV), 0.02),
        'hgrn_lb_logits': _normal(k[19], (L, HEADS * HGRN_DK), 0.1),
        'hgrn_norm_w': 1.0 + _normal(k[20], (L, HEAD_DV), 0.02),
        'w_branch': _normal(k[21], (L, N_BRANCH, W, D), W ** -0.5),
        'w_mix_out': _normal(k[22], (L, D, D), BETA * D ** -0.5),
        'ln_mix_w': 1.0 + _normal(k[23], (L, D), 0.02),
        'ln_mix_b': _normal(k[24], (L, D), 0.02),
        'w_ffn_up': _normal(k[25], (L, D, 2 * D_FF), D ** -0.5),
        'ffn_conv': _normal(k[26], (L, FFN_CONV_WIDTH, D_FF), FFN_CONV_WIDTH ** -0.5),
        'w_ffn_down': _normal(k[27], (L, D_FF, D), BETA * D_FF ** -0.5),
        'w_ple_gate': _normal(k[28], (L, D, D), D ** -0.5),
        'w_ple_proj': _normal(k[29], (L, PLE_DIM, D), BETA * PLE_DIM ** -0.5),
        'ln_ffn_w': 1.0 + _normal(k[30], (L, D), 0.02),
        'ln_ffn_b': _normal(k[31], (L, D), 0.02),
    }

def first_block(x, p, ln_in_w, ln_in_b, w_in, rwkv_mu, rwkv_w0, rwkv_w2, rwkv_a0, rwkv_a2, rwkv_g2,
              rwkv_k_k, rwkv_k_a, rwkv_r_k, rwkv_ln_w, rwkv_ln_b, gla_w2, gla_b, gla_norm_w,
              hgrn_lb_logits, hgrn_norm_w, w_branch, w_mix_out, ln_mix_w, ln_mix_b,
              w_ffn_up, ffn_conv, w_ffn_down, w_ple_gate, w_ple_proj, ln_ffn_w, ln_ffn_b):
    lb_prob = jax.nn.softmax(hgrn_lb_logits.astype(jnp.float32), axis=0)
    lb_all = jnp.concatenate([jnp.zeros_like(lb_prob[:1]), jnp.cumsum(lb_prob[1:], axis=0)], axis=0)

    x = layer_norm(x, ln_in_w, ln_in_b)
    for i in range(DEPTH):
        z = x @ w_in[i]
        z_ret, z_rwkv, z_gla, z_hgrn, z_gate = split_cols(z, GROUP_COLS)
        branches = (
            retnet_branch(z_ret),
            rwkv7_branch(z_rwkv, rwkv_mu[i], rwkv_w0[i], rwkv_w2[i], rwkv_a0[i], rwkv_a2[i], rwkv_g2[i],
                         rwkv_k_k[i], rwkv_k_a[i], rwkv_r_k[i], rwkv_ln_w[i], rwkv_ln_b[i]),
            gla_branch(z_gla, gla_w2[i], gla_b[i], gla_norm_w[i]),
            hgrn2_branch(z_hgrn, lb_all[i], hgrn_norm_w[i]),
        )
        merged = jnp.zeros_like(x)
        for n in range(N_BRANCH):
            gate = jax.nn.sigmoid(z_gate[..., n * D_MODEL:(n + 1) * D_MODEL])
            merged = merged + gate * (branches[n] @ w_branch[i, n])
        x = layer_norm(ALPHA * x + merged @ w_mix_out[i], ln_mix_w[i], ln_mix_b[i])
        ffn = conv_ffn(x, w_ffn_up[i], ffn_conv[i], w_ffn_down[i])
        ple = jax.nn.sigmoid(x @ w_ple_gate[i]) * (p[i] @ w_ple_proj[i])
        x = layer_norm(ALPHA * x + ffn + ple, ln_ffn_w[i], ln_ffn_b[i])
    return x


_first_inputs = first_inputs


def first_inputs(seed=0):
    import zlib

    import numpy as np

    out = dict(_first_inputs(seed))
    spreads = {}
    factors = {'rwkv_w2': 6.547,
     'rwkv_a0': 7.585,
     'rwkv_k_k': 8.0,
     'rwkv_k_a': 6.548,
     'rwkv_ln_w': 8.0,
     'rwkv_ln_b': 8.0,
     'gla_w2': 3.53,
     'gla_b': 7.9,
     'gla_norm_w': 8.0,
     'hgrn_norm_w': 8.0,
     'ln_mix_w': 2.844,
     'ln_mix_b': 2.779,
     'ln_ffn_w': 2.771,
     'ln_ffn_b': 2.898}
    for name, (base, spread) in spreads.items():
        noise = np.random.default_rng([zlib.crc32(name.encode()), seed]).standard_normal(out[name].shape)
        drawn = base * np.exp(spread * noise) if base else spread * noise
        out[name] = jnp.asarray(drawn.astype(out[name].dtype))
    for name, factor in factors.items():
        out[name] = (out[name] * factor).astype(out[name].dtype)
    return out


_narrow_inputs = first_inputs


def first_inputs(seed=0):

    out = dict(_narrow_inputs(seed))
    wider = {'rwkv_k_k': 8.54,
     'rwkv_ln_w': 5.28,
     'rwkv_ln_b': 6.04,
     'gla_norm_w': 4.79,
     'hgrn_norm_w': 5.05,
     'ln_ffn_w': 3.11,
     'ln_ffn_b': 3.12}
    for name, times in wider.items():
        mean = out[name].mean()
        out[name] = (mean + times * (out[name] - mean)).astype(out[name].dtype)
    return out


HEAD_DIM = 64
ATT_GROUPS = ((128, 1), (512, 4), (2048, 16))
HEADS_PER_GROUP = 4
N_ATT_HEADS = HEADS_PER_GROUP * len(ATT_GROUPS)
ATT_WIDTH = N_ATT_HEADS * HEAD_DIM
ATT_MERGED = HEADS_PER_GROUP * HEAD_DIM
BLK = 128
POOL_WINDOWS = (2, 4, 8, 16)
POOL_GROUP_WIDTH = 3 * D_MODEL // 16
POOL_WIDTH = POOL_GROUP_WIDTH * len(POOL_WINDOWS)
D_FF_2 = 4 * D_MODEL
N_IN_2 = 3 * ATT_WIDTH + POOL_WIDTH + 2 * D_MODEL
NORM_EPS = 1e-6
ALIBI_MAX_BIAS = 8.0


def _rmsnorm(x, g):
    xf = x.astype(jnp.float32)
    y = xf * lax.rsqrt(jnp.mean(xf * xf, axis=-1, keepdims=True) + NORM_EPS)
    return (y * g.astype(jnp.float32)).astype(x.dtype)

def _dilated_window_attention(q, k, v, dilation, n_steps, slopes):
    B, S, H, Dh = q.shape
    L = S // dilation
    nb = -(-L // BLK)
    Lp = nb * BLK
    Z = B * dilation

    def to_sub(t):
        t = t.reshape(B, L, dilation, H, Dh).transpose(0, 2, 1, 3, 4).reshape(Z, L, H, Dh)
        return jnp.pad(t, ((0, 0), (0, Lp - L), (0, 0), (0, 0)))

    def band(t):
        prev = jnp.pad(t, ((0, 0), (BLK, 0), (0, 0), (0, 0)))[:, :Lp]
        return jnp.concatenate([prev.reshape(Z, nb, BLK, H, Dh),
                                t.reshape(Z, nb, BLK, H, Dh)], axis=2)

    qb = to_sub(q).reshape(Z, nb, BLK, H, Dh).astype(jnp.float32)
    kb = band(to_sub(k)).astype(jnp.float32)
    vb = band(to_sub(v)).astype(jnp.float32)

    s = jnp.einsum('znqhd,znkhd->znhqk', qb, kb) * (Dh ** -0.5)
    steps = BLK + jnp.arange(BLK)[:, None] - jnp.arange(2 * BLK)[None, :]
    key_idx = (jnp.arange(nb)[:, None, None] * BLK
               + jnp.arange(2 * BLK)[None, None, :] - BLK)
    valid = (steps >= 0) & (steps <= n_steps) & (key_idx >= 0)
    bias = -(slopes[:, None, None] * (steps * dilation).astype(jnp.float32))
    s = jnp.where(valid[None, :, None], s + bias[None, None], -jnp.inf)
    lse = jax.nn.logsumexp(s, axis=-1)
    p = jnp.exp(s - lse[..., None])
    o = jnp.einsum('znhqk,znkhd->znqhd', p, vb).reshape(Z, Lp, H, Dh)[:, :L]
    lse = lse.transpose(0, 1, 3, 2).reshape(Z, Lp, H)[:, :L]
    o = o.reshape(B, dilation, L, H, Dh).transpose(0, 2, 1, 3, 4).reshape(B, S, H, Dh)
    lse = lse.reshape(B, dilation, L, H).transpose(0, 2, 1, 3).reshape(B, S, H)
    return o, lse

def _attention_branch(q, k, v):
    B, S, _ = q.shape
    q = q.reshape(B, S, N_ATT_HEADS, HEAD_DIM)
    k = k.reshape(B, S, N_ATT_HEADS, HEAD_DIM)
    v = v.reshape(B, S, N_ATT_HEADS, HEAD_DIM)
    slopes = 2.0 ** (-ALIBI_MAX_BIAS * (jnp.arange(N_ATT_HEADS, dtype=jnp.float32) + 1.0)
                     / N_ATT_HEADS)
    outs, lses = [], []
    for g, (window, dilation) in enumerate(ATT_GROUPS):
        hs = slice(g * HEADS_PER_GROUP, (g + 1) * HEADS_PER_GROUP)
        o, l = _dilated_window_attention(q[:, :, hs], k[:, :, hs], v[:, :, hs],
                                         dilation, window // dilation, slopes[hs])
        outs.append(o)
        lses.append(l)
    outs = jnp.stack(outs, axis=0)
    wts = jax.nn.softmax(jnp.stack(lses, axis=0), axis=0)
    merged = jnp.sum(wts[..., None] * outs, axis=0)
    return merged.reshape(B, S, ATT_MERGED)

def _pool_branch(pz, w_grp, scale):
    B, S, _ = pz.shape
    pf = pz.astype(jnp.float32).reshape(B, S, len(POOL_WINDOWS), POOL_GROUP_WIDTH)
    c0 = jnp.pad(jnp.cumsum(pf, axis=1), ((0, 0), (1, 0), (0, 0), (0, 0)))
    t = jnp.arange(S)
    pooled = []
    for g, w in enumerate(POOL_WINDOWS):
        lower = jnp.take(c0[:, :, g], jnp.maximum(t + 1 - w, 0), axis=1)
        count = jnp.minimum(t + 1, w).astype(jnp.float32)[None, :, None]
        pooled.append((c0[:, 1:, g] - lower) / count)
    pooled = jnp.stack(pooled, axis=2) - pf
    mixed = jnp.einsum('bsgc,gcd->bsgd', pooled, w_grp.astype(jnp.float32))
    return mixed.reshape(B, S, POOL_WIDTH) * scale.astype(jnp.float32)

def second_inputs(seed: int = 0) -> dict:
    key = jax.random.key(seed)
    ks = jax.random.split(key, 12)
    f32 = jnp.float32

    def nrm(k, shape, fan_in):
        return jax.random.normal(k, shape, f32) * (fan_in ** -0.5)

    def gain(k, shape):
        return 1.0 + 0.02 * jax.random.normal(k, shape, f32)

    return {
        "x": jax.random.normal(ks[0], (BATCH, SEQ, D_MODEL), f32),
        "norm_mix_g": gain(ks[1], (DEPTH, D_MODEL)),
        "w_in": nrm(ks[2], (DEPTH, D_MODEL, N_IN_2), D_MODEL),
        "w_att_out": nrm(ks[3], (DEPTH, ATT_MERGED, D_MODEL), ATT_MERGED),
        "w_pool_grp": nrm(ks[4], (DEPTH, len(POOL_WINDOWS), POOL_GROUP_WIDTH, POOL_GROUP_WIDTH),
                          POOL_GROUP_WIDTH),
        "pool_scale": 1.0 + 0.1 * jax.random.normal(ks[5], (DEPTH, POOL_WIDTH), f32),
        "w_pool_out": nrm(ks[6], (DEPTH, POOL_WIDTH, D_MODEL), POOL_WIDTH),
        "w_out": nrm(ks[7], (DEPTH, D_MODEL, D_MODEL), D_MODEL),
        "norm_mlp_g": gain(ks[8], (DEPTH, D_MODEL)),
        "w_mlp_in": nrm(ks[9], (DEPTH, D_MODEL, D_FF_2), D_MODEL),
        "w_mlp_out": nrm(ks[10], (DEPTH, D_FF_2, D_MODEL), D_FF_2),
        "norm_final_g": gain(ks[11], (D_MODEL,)),
    }

def second_block(x, norm_mix_g, w_in, w_att_out, w_pool_grp, pool_scale, w_pool_out, w_out,
              norm_mlp_g, w_mlp_in, w_mlp_out, norm_final_g):
    dt = x.dtype
    offs = np.cumsum([ATT_WIDTH, ATT_WIDTH, ATT_WIDTH, POOL_WIDTH, D_MODEL]).tolist()
    h = x
    for l in range(DEPTH):
        u = _rmsnorm(h, norm_mix_g[l])
        z = jnp.einsum('bsd,dn->bsn', u, w_in[l])
        q, k, v, pz, ga, gp = jnp.split(z, offs, axis=-1)
        a = _attention_branch(q, k, v).astype(dt)
        p = _pool_branch(pz, w_pool_grp[l], pool_scale[l]).astype(dt)
        merged = (jax.nn.sigmoid(ga) * jnp.einsum('bsc,cd->bsd', a, w_att_out[l])
                  + jax.nn.sigmoid(gp) * jnp.einsum('bsc,cd->bsd', p, w_pool_out[l]))
        h = h + jnp.einsum('bsd,de->bse', merged, w_out[l])
        m = _rmsnorm(h, norm_mlp_g[l])
        hid = jnp.square(jax.nn.relu(jnp.einsum('bsd,df->bsf', m, w_mlp_in[l])))
        h = h + jnp.einsum('bsf,fd->bsd', hid, w_mlp_out[l])
    return _rmsnorm(h, norm_final_g)


def setup_inputs(seed=0):
    out = dict(first_inputs(seed))
    for name, value in second_inputs(seed + 1).items():
        if name != "x":
            out[name + "_2"] = value
    return out


def reference(
    x, p, ln_in_w, ln_in_b, w_in, rwkv_mu, rwkv_w0, rwkv_w2, rwkv_a0, rwkv_a2, rwkv_g2,
    rwkv_k_k, rwkv_k_a, rwkv_r_k, rwkv_ln_w, rwkv_ln_b, gla_w2, gla_b, gla_norm_w,
    hgrn_lb_logits, hgrn_norm_w, w_branch, w_mix_out, ln_mix_w, ln_mix_b, w_ffn_up, ffn_conv,
    w_ffn_down, w_ple_gate, w_ple_proj, ln_ffn_w, ln_ffn_b, norm_mix_g_2, w_in_2, w_att_out_2,
    w_pool_grp_2, pool_scale_2, w_pool_out_2, w_out_2, norm_mlp_g_2, w_mlp_in_2, w_mlp_out_2,
    norm_final_g_2,
):
    x = first_block(
        x, p, ln_in_w, ln_in_b, w_in, rwkv_mu, rwkv_w0, rwkv_w2, rwkv_a0, rwkv_a2, rwkv_g2,
        rwkv_k_k, rwkv_k_a, rwkv_r_k, rwkv_ln_w, rwkv_ln_b, gla_w2, gla_b, gla_norm_w,
        hgrn_lb_logits, hgrn_norm_w, w_branch, w_mix_out, ln_mix_w, ln_mix_b, w_ffn_up,
        ffn_conv, w_ffn_down, w_ple_gate, w_ple_proj, ln_ffn_w, ln_ffn_b,
    )
    return second_block(
        x, norm_mix_g_2, w_in_2, w_att_out_2, w_pool_grp_2, pool_scale_2, w_pool_out_2, w_out_2,
        norm_mlp_g_2, w_mlp_in_2, w_mlp_out_2, norm_final_g_2,
    )


_drawn_inputs = setup_inputs


def setup_inputs(seed=0):
    import zlib

    import numpy as np

    out = dict(_drawn_inputs(seed))
    spreads = {}
    factors = {'norm_mix_g_2': 8.0, 'pool_scale_2': 3.346, 'norm_mlp_g_2': 5.903}
    for name, (base, spread) in spreads.items():
        noise = np.random.default_rng([zlib.crc32(name.encode()), seed]).standard_normal(out[name].shape)
        drawn = base * np.exp(spread * noise) if base else spread * noise
        out[name] = jnp.asarray(drawn.astype(out[name].dtype))
    for name, factor in factors.items():
        out[name] = (out[name] * factor).astype(out[name].dtype)
    return out
```

```python
from contextlib import ExitStack

import concourse.bass as bass
import numpy as np
from concourse import mybir

F32 = mybir.dt.float32
F32R = mybir.dt.float32r
I32 = mybir.dt.int32
ACT = mybir.ActivationFunctionType
ALU = mybir.AluOpType
AX = mybir.AxisListType.X

P = 128
T = 1024
D = 1024
KT = D // P
C = 128
NC = T // C
ALPHA = 2.0 ** 0.25
RWKV_DECAY = 0.6065306597126334
FF = 2816
FF2 = 4096
NEG = -1e30
RET0, RWKV0, GLA0, HGRN0, GATE0 = 0, 768, 1792, 2576, 3600
ATT_W = 768
DIL = (1, 4, 16)
POOL_WIN = (2, 4, 8, 16)
PG = 96

BASE = 16512
KB = 1024
OFF_XH, OFF_XL, OFF_A, OFF_WR, OFF_WH, OFF_WL, OFF_S = (
    BASE, BASE + 32 * KB, BASE + 64 * KB, BASE + 96 * KB, BASE + 104 * KB, BASE + 112 * KB, BASE + 120 * KB)
OFF_T = OFF_S + 64 * KB
END = 229344


class Space:

    def __init__(self, nc, name, *stretches):
        self.nc, self.name, self.free = nc, name, [list(s) for s in stretches]

    def __call__(self, name, shape, dtype=F32):
        size = int(np.prod(shape[1:])) * 4
        size = (size + 31) // 32 * 32
        for s in self.free:
            if s[1] - s[0] >= size:
                at = s[0]
                s[0] += size
                return self.nc.alloc_sbuf_tensor_at(f"{self.name}_{name}", list(shape), dtype, offset=at)
        raise ValueError(f"no room for {self.name}_{name}: {size} in {self.free}")


class Signals(ExitStack):

    def __init__(self, nc, phase):
        super().__init__()
        self.nc, self.phase, self.made = nc, phase, {}

    def __getitem__(self, name):
        if name not in self.made:
            self.made[name] = self.nc.alloc_semaphore(f"{self.phase}_{name}")
        return self.made[name]

    def __exit__(self, *details):
        self.nc.clear_and_free_semaphores(list(self.made.values()))
        self.nc.all_engine_barrier()
        return super().__exit__(*details)


def bc(ap, n):
    return ap.unsqueeze(1).to_broadcast([ap.shape[0], n, ap.shape[1]])


def bcl(ap, n):
    return ap.unsqueeze(2).to_broadcast([ap.shape[0], ap.shape[1], n])


class Core:

    def __init__(self, nc):
        self.nc = nc
        at = nc.alloc_sbuf_tensor_at
        self.xh = at("x_hi", [P, KT, T], F32R, offset=OFF_XH)
        self.xl = at("x_lo", [P, KT, T], F32R, offset=OFF_XL)
        self.a = at("acc", [P, KT, T], F32, offset=OFF_A)
        self.wr = at("w_raw", [P, 2, KT, P], F32, offset=OFF_WR)
        self.wh = at("w_hi", [P, 2, KT, P], F32R, offset=OFF_WH)
        self.wl = at("w_lo", [P, 2, KT, P], F32R, offset=OFF_WL)
        self.ps = nc.alloc_psum_tensor("psum", [P, 8, 512], F32)

    def slot(self, s):
        return self.ps[:, 2 * s:2 * s + 2, :].rearrange("p a b -> p (a b)")


class Run:

    def __init__(self, n, src, hi, lo, nk=(KT, KT), rows=P, m=P, ready=()):
        self.n, self.src, self.nk, self.m, self.ready = n, src, nk, m, ready
        self.rows = rows if isinstance(rows, tuple) else (rows, rows)
        self.hi = hi if isinstance(hi, tuple) else (hi, hi)
        self.lo = lo if isinstance(lo, tuple) else (lo, lo)


class Strips:

    def __init__(self, core, sig, runs):
        self.c, self.sig, self.runs = core, sig, runs
        self.turns = [sum(r.n for r in runs[:i]) for i in range(len(runs))]

    def load(self, sp):
        for run, base in zip(self.runs, self.turns):
            def turn(j, g, warm, run=run):
                if warm:
                    sp.wait_ge(self.sig["w_lo0"], g)
                    sp.wait_ge(self.sig["w_lo1"], g)
                for s in range(2):
                    sp.dma_start(self.c.wr[0:run.rows[s], s, 0:run.nk[s], 0:run.m], run.src(j, s)
                                 ).then_inc(self.sig[f"w_raw{s}"], 16)
            self._turns(sp, run.n, base, turn, peel=(base == 0))

    def _turns(self, eng, n, base, turn, peel=False, last=None):
        first = 1 if peel else 0
        stop = n - 1 if last is not None else n
        if peel and stop > 0:
            turn(0, base, False)
        if stop > first:
            with eng.Fori(first, stop) as j:
                turn(j, j + base, True)
        if last is not None:
            last(n - 1, base + n - 1)

    def split_hi(self, act, g, s, run, warm=True):
        act.wait_ge(self.sig[f"w_raw{s}"], g * 16 + 16)
        if warm:
            act.wait_ge(self.sig[f"mm{s}"], g)
        act.activation(self.c.wh[0:run.rows[s], s, 0:run.nk[s], 0:run.m],
                       self.c.wr[0:run.rows[s], s, 0:run.nk[s], 0:run.m], ACT.Copy).then_inc(self.sig[f"w_hi{s}"], 1)

    def split_lo(self, pool, g, s, run):
        pool.wait_ge(self.sig[f"w_hi{s}"], g + 1)
        pool.tensor_tensor(self.c.wl[0:run.rows[s], s, 0:run.nk[s], 0:run.m],
                           self.c.wr[0:run.rows[s], s, 0:run.nk[s], 0:run.m],
                           self.c.wh[0:run.rows[s], s, 0:run.nk[s], 0:run.m].bitcast(F32), ALU.subtract
                           ).then_inc(self.sig[f"w_lo{s}"], 1)

    def follow(self, eng, split, out):
        if split:
            for s in range(2):
                split(eng, 0, s, self.runs[0], False)
        for r, (run, base) in enumerate(zip(self.runs, self.turns)):
            after = self.runs[r + 1] if r + 1 < len(self.runs) else None

            def turn(j, g, warm, run=run, r=r):
                for s in range(2):
                    if split:
                        split(eng, g + 1, s, run, True)
                    if out:
                        out(r, j, g, s)

            def last(j, g, run=run, r=r, after=after):
                for s in range(2):
                    if split and after is not None:
                        split(eng, g + 1, s, after, True)
                    if out:
                        out(r, j, g, s)
            self._turns(eng, run.n, base, turn, last=last)

    def hi_split(self, act, g, s, run, warm):
        self.split_hi(act, g, s, run, warm)

    def lo_split(self, pool, g, s, run, warm):
        self.split_lo(pool, g, s, run)

    def products(self, pe):
        wh, wl = self.c.wh, self.c.wl
        for run, base in zip(self.runs, self.turns):
            for sem, value in run.ready:
                pe.wait_ge(sem, value)

            def turn(j, g, warm, run=run):
                for s in range(2):
                    pe.wait_ge(self.sig[f"w_lo{s}"], g + 1)
                    if warm:
                        pe.wait_ge(self.sig[f"out{s}"], g)
                    nk = run.nk[s]
                    for k in range(nk):
                        for n, (w, x) in enumerate(((wh, run.hi[s]), (wh, run.lo[s]), (wl, run.hi[s]))):
                            for h in range(2):
                                last = pe.matmul(self.c.ps[0:run.m, 2 * s + h, :], w[0:run.rows[s], s, k, 0:run.m],
                                                 x(k)[:, 512 * h:512 * h + 512],
                                                 start=(k == 0 and n == 0), stop=(k == nk - 1 and n == 2))
                    last.then_inc(self.sig[f"mm{s}"], 1)
            self._turns(pe, run.n, base, turn, peel=(base == 0))


def col_strip(w, first, i, rows=D, row0=0, part=P, width=P):
    v = w[row0:row0 + rows, :].rearrange("(k p) n -> p k n", p=part)
    if isinstance(i, int):
        return v[:, :, first + i * width:first + i * width + width]
    return v[:, :, bass.ds(i * width + first, width)]


def flat(ap):
    return ap.rearrange("p a b -> p (a b)")


def at(buf, i):
    if isinstance(i, int):
        return buf[:, i, :]
    return flat(buf[:, bass.ds(i, 1), :])


def colat(buf, i):
    return buf[:, i:i + 1] if isinstance(i, int) else buf[:, bass.ds(i, 1)]


def norm_phase(nc, core, name, ones, w, b, eps, x_in=None, keep=ALPHA, out=None, spill=None,
               split=True):
    mem = Space(nc, name, (OFF_S, END))
    one, wc, bcol = mem("ones", [P, P]), mem("w", [P, KT]), mem("b", [P, KT])
    sq, sd, rstd, epst = mem("sq", [P, 2, T]), mem("sd", [P, T]), mem("rstd", [P, T]), mem("eps", [P, 1])
    y = mem("y", [P, 2, T])
    a, ps = core.a, core.ps
    centre = b is not None
    with ExitStack() as ctx:
        sig = ctx.enter_context(Signals(nc, name))
        block = ctx.enter_context(nc.Block())

        @block.sync
        def _(sp):
            sp.dma_start(one[:, :], ones).then_inc(sig["consts"], 16)
            sp.dma_start(wc[:, :], w).then_inc(sig["consts"], 16)
            if centre:
                sp.dma_start(bcol[:, :], b).then_inc(sig["consts"], 16)
            if x_in is not None:
                for k in range(KT):
                    sp.dma_start(a[:, k, :], x_in[k * P:k * P + P, :]).then_inc(sig[f"x{k}"], 16)
            if spill is not None:
                sp.dma_start(spill.rearrange("(k p) t -> p k t", p=P), a[:, :, :]).then_inc(sig["spilled"], 16)
                sp.wait_ge(sig["spilled"], 16)
            if out is not None:
                for k in range(KT):
                    sp.wait_ge(sig["affine"], k + 1)
                    sp.dma_start(out[k * P:k * P + P, :], y[:, k % 2, :] if keep is None else a[:, k, :]
                                 ).then_inc(sig[f"stored{k}"], 16)
                for k in range(KT):
                    sp.wait_ge(sig[f"stored{k}"], 16)

        nconst = 48 if centre else 32

        @block.tensor
        def _(pe):
            pe.wait_ge(sig["consts"], nconst)
            if centre:
                for k in range(KT):
                    if x_in is not None:
                        pe.wait_ge(sig[f"x{k}"], 16)
                    for h in range(2):
                        last = pe.matmul(ps[:, h, :], one[:, :], a[:, k, 512 * h:512 * h + 512],
                                         start=(k == 0), stop=(k == KT - 1))
                last.then_inc(sig["mean"], 1)
            for k in range(KT):
                pe.wait_ge(sig["sq"], k + 1)
                for h in range(2):
                    last = pe.matmul(ps[:, 2 + h, :], one[:, :], sq[:, k % 2, 512 * h:512 * h + 512],
                                     start=(k == 0), stop=(k == KT - 1))
                last.then_inc(sig["sq_summed"], 1)

        @block.scalar
        def _(act):
            for k in range(KT):
                if centre:
                    act.wait_ge(sig["centred"], k + 1)
                if k >= 2:
                    act.wait_ge(sig["sq_summed"], k - 1)
                act.activation(sq[:, k % 2, :], a[:, k, :], ACT.Square).then_inc(sig["sq"], 1)
            act.wait_ge(sig["sq_summed"], KT)
            act.wait_ge(sig["eps"], 1)
            act.activation(sd[:, :], core.slot(1), ACT.Sqrt, bias=epst[:, 0:1]).then_inc(sig["sd"], 1)
            act.wait_ge(sig["consts"], nconst)
            for k in range(KT):
                dst = y[:, k % 2, :] if keep is None else a[:, k, :]
                act.wait_ge(sig["scaled"], k + 1)
                if centre:
                    act.activation(dst, dst, ACT.Identity, bias=bcol[:, k:k + 1], scale=wc[:, k:k + 1]
                                   ).then_inc(sig["affine"], 1)
                else:
                    act.activation(dst, dst, ACT.Copy, scale=wc[:, k:k + 1]).then_inc(sig["affine"], 1)
                if out is None and split:
                    act.wait_ge(sig["affine"], k + 1)
                    act.activation(core.xh[:, k, :], dst, ACT.Copy).then_inc(sig["hi"], 1)

        @block.vector
        def _(dve):
            dve.memset(epst[:, :], eps).then_inc(sig["eps"], 1)
            if centre:
                dve.wait_ge(sig["mean"], 1)
                for k in range(KT):
                    dve.tensor_tensor(a[:, k, :], a[:, k, :], core.slot(0), ALU.subtract).then_inc(sig["centred"], 1)
            dve.wait_ge(sig["sd"], 1)
            dve.reciprocal(rstd[:, :], sd[:, :]).then_inc(sig["rstd"], 1)
            dve.wait_ge(sig["rstd"], 1)
            for k in range(KT):
                dst = y[:, k % 2, :] if keep is None else a[:, k, :]
                if centre:
                    dve.wait_ge(sig["centred"], k + 1)
                if keep is None and k >= 2:
                    if out is None:
                        dve.wait_ge(sig["lo"], k - 1)
                    else:
                        dve.wait_ge(sig[f"stored{k - 2}"], 16)
                dve.tensor_tensor(dst, a[:, k, :], rstd[:, :], ALU.mult).then_inc(sig["scaled"], 1)

        @block.gpsimd
        def _(pool):
            if out is None and split:
                for k in range(KT):
                    dst = y[:, k % 2, :] if keep is None else a[:, k, :]
                    pool.wait_ge(sig["hi"], k + 1)
                    pool.tensor_tensor(core.xl[:, k, :], dst, core.xh[:, k, :].bitcast(F32), ALU.subtract
                                       ).then_inc(sig["lo"], 1)
                    if keep is not None and keep != 1.0:
                        pool.wait_ge(sig["lo"], k + 1)
                        pool.tensor_scalar(a[:, k, :], a[:, k, :], keep, None, ALU.mult)


def x_parts(core):
    return (lambda k: core.xh[:, k, :]), (lambda k: core.xl[:, k, :])


def mix_out_phase(nc, core, name, w, residual=None):
    mem = Space(nc, name, (OFF_S, END))
    mh, ml = mem("m_hi", [P, KT, T], F32R), mem("m_lo", [P, KT, T], F32R)
    a = core.a
    with ExitStack() as ctx:
        sig = ctx.enter_context(Signals(nc, name))
        st = Strips(core, sig, [Run(KT // 2, lambda j, s: col_strip(w, s * P, j * 2), lambda k: mh[:, k, :],
                                    lambda k: ml[:, k, :], ready=[(sig["m_lo"], KT)])])
        block = ctx.enter_context(nc.Block())

        @block.sync
        def _(sp):
            st.load(sp)

        @block.scalar
        def _(act):
            for k in range(KT):
                act.activation(mh[:, k, :], a[:, k, :], ACT.Copy).then_inc(sig["m_hi"], 1)
            if residual is not None:
                act.wait_ge(sig["m_lo"], KT)
                act.dma_start(a[:, :, :], residual.rearrange("(k p) t -> p k t", p=P)).then_inc(sig["residual"], 16)
            st.follow(act, st.hi_split, None)

        @block.gpsimd
        def _(pool):
            st.follow(pool, st.lo_split, None)

        @block.tensor
        def _(pe):
            st.products(pe)

        @block.vector
        def _(dve):
            for k in range(KT):
                dve.wait_ge(sig["m_hi"], k + 1)
                dve.tensor_tensor(ml[:, k, :], a[:, k, :], mh[:, k, :].bitcast(F32), ALU.subtract
                                  ).then_inc(sig["m_lo"], 1)
            if residual is None:
                for k in range(KT):
                    dve.wait_ge(sig["m_lo"], k + 1)
                    dve.tensor_scalar(a[:, k, :], core.xl[:, k, :].bitcast(F32), ALPHA, None, ALU.mult
                                      ).then_inc(sig["x_lo"], 1)
                    dve.wait_ge(sig["x_lo"], k + 1)
                    dve.scalar_tensor_tensor(out=a[:, k, :], in0=core.xh[:, k, :].bitcast(F32), scalar=ALPHA,
                                             in1=a[:, k, :], op0=ALU.mult, op1=ALU.add).then_inc(sig["x"], 1)
                dve.wait_ge(sig["x"], KT)
            else:
                dve.wait_ge(sig["residual"], 16)

            def out(r, j, g, s):
                dve.wait_ge(sig[f"mm{s}"], g + 1)
                dst = at(a, j * 2 + s)
                dve.tensor_tensor(dst, dst, core.slot(s), ALU.add).then_inc(sig[f"out{s}"], 1)
            st.follow(dve, None, out)


def gated_phase(nc, core, name, mem, branches, fresh, p_in=None):
    gate = mem("gate", [P, T])
    xh, xl = x_parts(core)
    if p_in is not None:
        raw, ph, pl = mem("p", [P, 2, T]), mem("p_hi", [P, 2, T], F32R), mem("p_lo", [P, 2, T], F32R)
    with ExitStack() as ctx:
        sig = ctx.enter_context(Signals(nc, name))
        runs = []
        for gw, g0, w, rows, pt, yh, yl in branches:
            if p_in is not None:
                yh, yl = (lambda k: ph[:, k, :]), (lambda k: pl[:, k, :])

            def src(j, s, gw=gw, g0=g0, w=w, rows=rows, pt=pt):
                if s == 0:
                    return col_strip(gw, g0, j)
                return col_strip(w, 0, j, rows=rows, part=pt)
            runs.append(Run(KT, src, (xh, yh), (xl, yl), nk=(KT, rows // pt), rows=(P, pt),
                            ready=[(sig["p_lo"], 1)] if p_in is not None else ()))
        st = Strips(core, sig, runs)
        block = ctx.enter_context(nc.Block())

        @block.sync
        def _(sp):
            if p_in is not None:
                sp.dma_start(raw[:, :, :], p_in.rearrange("(k p) t -> p k t", p=P)).then_inc(sig["p"], 16)
            st.load(sp)

        @block.scalar
        def _(act):
            if p_in is not None:
                act.wait_ge(sig["p"], 16)
                act.activation(ph[:, :, :], raw[:, :, :], ACT.Copy).then_inc(sig["p_hi"], 1)

            def out(r, j, g, s):
                if s == 0:
                    act.wait_ge(sig["mm0"], g + 1)
                    if isinstance(g, int) and g == 0:
                        pass
                    else:
                        act.wait_ge(sig["added"], g)
                    act.activation(gate[:, :], core.slot(0), ACT.Sigmoid).then_inc(sig["out0"], 1)
            st.follow(act, st.hi_split, out)

        @block.gpsimd
        def _(pool):
            st.follow(pool, st.lo_split, None)

        @block.tensor
        def _(pe):
            st.products(pe)

        @block.vector
        def _(dve):
            if p_in is not None:
                dve.wait_ge(sig["p_hi"], 1)
                dve.tensor_tensor(pl[:, :, :], raw[:, :, :], ph[:, :, :].bitcast(F32), ALU.subtract
                                  ).then_inc(sig["p_lo"], 1)

            def out(r, j, g, s):
                if s == 0:
                    return
                dve.wait_ge(sig["out0"], g + 1)
                dve.wait_ge(sig["mm1"], g + 1)
                dst = at(core.a, j)
                dve.tensor_tensor(gate[:, :], core.slot(1), gate[:, :], ALU.mult).then_inc(sig["out1"], 1)
                dve.wait_ge(sig["out1"], g + 1)
                if fresh and r == 0:
                    dve.tensor_copy(dst, gate[:, :]).then_inc(sig["added"], 1)
                else:
                    dve.tensor_tensor(dst, dst, gate[:, :], ALU.add).then_inc(sig["added"], 1)
            st.follow(dve, None, out)


def mlp_phase(nc, core, name, w_in, w_out):
    mem = Space(nc, name, (OFF_S, END))
    hh, hl = mem("h_hi", [P, KT, T], F32R), mem("h_lo", [P, KT, T], F32R)
    relu, h = mem("relu", [P, 2, T]), mem("h", [P, 2, T])
    xh, xl = x_parts(core)
    chunks = FF2 // (KT * P)
    with ExitStack() as ctx:
        sig = ctx.enter_context(Signals(nc, name))
        runs = []
        for i in range(chunks):
            runs.append(Run(KT // 2, lambda j, s, i=i: col_strip(w_in, i * D + s * P, j * 2), xh, xl))
            runs.append(Run(KT // 2, lambda j, s, i=i: col_strip(w_out, s * P, j * 2, rows=D, row0=i * D),
                            lambda k: hh[:, k, :], lambda k: hl[:, k, :], ready=[(sig["h_lo"], KT * (i + 1))]))
        st = Strips(core, sig, runs)
        block = ctx.enter_context(nc.Block())

        def hidden(r, j, s):
            return j * 2 + (s + KT * (r // 2))

        @block.sync
        def _(sp):
            st.load(sp)

        @block.tensor
        def _(pe):
            st.products(pe)

        @block.scalar
        def _(act):
            def out(r, j, g, s):
                if r % 2:
                    return
                f = hidden(r, j, s)
                act.wait_ge(sig[f"mm{s}"], g + 1)
                act.activation(relu[:, s, :], core.slot(s), ACT.Relu).then_inc(sig[f"out{s}"], 1)
                act.wait_ge(sig["squared"], f + 1)
                act.activation(at(hh, j * 2 + s), h[:, s, :], ACT.Copy).then_inc(sig["h_hi"], 1)
            st.follow(act, st.hi_split, out)

        @block.vector
        def _(dve):
            def out(r, j, g, s):
                if r % 2:
                    dve.wait_ge(sig[f"mm{s}"], g + 1)
                    dst = at(core.a, j * 2 + s)
                    dve.tensor_tensor(dst, dst, core.slot(s), ALU.add).then_inc(sig[f"out{s}"], 1)
                    return
                f = hidden(r, j, s)
                dve.wait_ge(sig[f"out{s}"], g + 1)
                dve.wait_ge(sig["h_lo"], f)
                dve.tensor_tensor(h[:, s, :], relu[:, s, :], relu[:, s, :], ALU.mult).then_inc(sig["squared"], 1)
            st.follow(dve, None, out)

        @block.gpsimd
        def _(pool):
            def out(r, j, g, s):
                if r % 2:
                    return
                f = hidden(r, j, s)
                pool.wait_ge(sig["h_hi"], f + 1)
                pool.tensor_tensor(at(hl, j * 2 + s), h[:, s, :], at(hh, j * 2 + s).bitcast(F32), ALU.subtract
                                   ).then_inc(sig["h_lo"], 1)
            st.follow(pool, st.lo_split, out)


def ffn_phase(nc, core, name, w_up, conv, w_down):
    mem = Space(nc, name, (OFF_S, END))
    hh, hl = mem("h_hi", [P, KT, T], F32R), mem("h_lo", [P, KT, T], F32R)
    u, gate = mem("conv", [P, 2, T]), mem("h", [P, 2, T])
    taps = mem("taps", [P, 3, FF // P])
    xh, xl = x_parts(core)
    chunks = [(0, 8), (8, 8), (16, 6)]
    with ExitStack() as ctx:
        sig = ctx.enter_context(Signals(nc, name))
        runs = []
        for f0, n in chunks:
            runs.append(Run(n, lambda j, s, f0=f0: col_strip(w_up, f0 * P + s * FF, j), xh, xl))
            runs.append(Run(KT // 2, lambda j, s, f0=f0, n=n: col_strip(w_down, s * P, j * 2, rows=n * P, row0=f0 * P),
                            lambda k: hh[:, k, :], lambda k: hl[:, k, :], nk=(n, n),
                            ready=[(sig["h_lo"], f0 + n)]))
        st = Strips(core, sig, runs)
        block = ctx.enter_context(nc.Block())

        @block.sync
        def _(sp):
            sp.dma_start(taps[:, :, :], conv).then_inc(sig["taps"], 16)
            st.load(sp)

        @block.tensor
        def _(pe):
            st.products(pe)

        def tile_no(r, j):
            return j + chunks[r // 2][0]

        @block.scalar
        def _(act):
            act.wait_ge(sig["taps"], 16)

            def out(r, j, g, s):
                if r % 2:
                    return
                f = tile_no(r, j)
                if s == 0:
                    act.wait_ge(sig["mm0"], g + 1)
                    act.activation(u[:, 0, :], core.slot(0), ACT.Copy, scale=colat(taps[:, 2, :], f)
                                   ).then_inc(sig["tap2"], 1)
                else:
                    act.wait_ge(sig["out0"], g + 1)
                    act.activation(u[:, 1, :], u[:, 0, :], ACT.Gelu_apprx_tanh).then_inc(sig["gelu"], 1)
                    act.wait_ge(sig["out1"], g + 1)
                    act.activation(at(hh, j), gate[:, 0, :], ACT.Copy).then_inc(sig["h_hi"], 1)
            st.follow(act, st.hi_split, out)

        @block.vector
        def _(dve):
            def out(r, j, g, s):
                if r % 2:
                    dve.wait_ge(sig[f"mm{s}"], g + 1)
                    dst = at(core.a, j * 2 + s)
                    dve.tensor_tensor(dst, dst, core.slot(s), ALU.add).then_inc(sig[f"out{s}"], 1)
                    return
                f = tile_no(r, j)
                if s == 0:
                    dve.wait_ge(sig["tap2"], f + 1)
                    dve.scalar_tensor_tensor(out=u[:, 0, 1:T], in0=core.slot(0)[:, 0:T - 1],
                                             scalar=colat(taps[:, 1, :], f), in1=u[:, 0, 1:T],
                                             op0=ALU.mult, op1=ALU.add).then_inc(sig["tap1"], 1)
                    dve.wait_ge(sig["tap1"], f + 1)
                    dve.scalar_tensor_tensor(out=u[:, 0, 2:T], in0=core.slot(0)[:, 0:T - 2],
                                             scalar=colat(taps[:, 0, :], f), in1=u[:, 0, 2:T],
                                             op0=ALU.mult, op1=ALU.add).then_inc(sig["out0"], 1)
                else:
                    dve.wait_ge(sig["mm1"], g + 1)
                    dve.wait_ge(sig["gelu"], f + 1)
                    dve.wait_ge(sig["h_lo"], f)
                    dve.tensor_tensor(gate[:, 0, :], core.slot(1), u[:, 1, :], ALU.mult).then_inc(sig["out1"], 1)
            st.follow(dve, None, out)

        @block.gpsimd
        def _(pool):
            def out(r, j, g, s):
                if r % 2 or s == 0:
                    return
                f = tile_no(r, j)
                pool.wait_ge(sig["h_hi"], f + 1)
                pool.tensor_tensor(at(hl, j), gate[:, 0, :], at(hh, j).bitcast(F32), ALU.subtract
                                   ).then_inc(sig["h_lo"], 1)
            st.follow(pool, st.lo_split, out)


def project_phase(nc, core, name, runs, outs, w_tok=None, zv=None, tokens=None, consts=None, last_vector=None):
    ps = core.ps
    with ExitStack() as ctx:
        sig = ctx.enter_context(Signals(nc, name))
        feat = list(runs)
        turns = sum(r.n for r in feat)
        st = Strips(core, sig, feat + ([Run(1, lambda j, s: w_tok(s), None, None)] if w_tok else []))
        pe_st = Strips(core, sig, feat)
        block = ctx.enter_context(nc.Block())
        tokens = tokens or (lambda buf, k, j: buf[:, k, j * P:j * P + P])

        @block.sync
        def _(sp):
            if consts:
                consts[0](sp, sig)
            st.load(sp)

        @block.scalar
        def _(act):
            if consts:
                act.wait_ge(sig["ready"], 1)

            def out(r, j, g, s):
                if r >= len(feat):
                    return
                act.wait_ge(sig[f"mm{s}"], g + 1)
                outs[r](act, j, s, core.slot(s)).then_inc(sig[f"taken{s}" if last_vector else f"out{s}"], 1)
            st.follow(act, st.hi_split, out)
            if w_tok:
                for b in range(4):
                    act.wait_ge(sig["tok"], b + 1)
                    act.activation(zv[:, 2 * b:2 * b + 2, :], ps[:, 4 + b, :].rearrange("p (j n) -> p j n", j=2),
                                   ACT.Copy)

        @block.gpsimd
        def _(pool):
            st.follow(pool, st.lo_split, None)

        @block.vector
        def _(dve):
            if consts:
                consts[1](dve, sig).then_inc(sig["ready"], 1)
            if last_vector:
                def out(r, j, g, s):
                    dve.wait_ge(sig[f"taken{s}"], g + 1)
                    last_vector(dve, r, j, s, core.slot(s)).then_inc(sig[f"out{s}"], 1)
                pe_st.follow(dve, None, out)

        @block.tensor
        def _(pe):
            pe_st.products(pe)
            if w_tok:
                for s in range(2):
                    pe.wait_ge(sig[f"w_lo{s}"], turns + 1)
                for j in range(NC):
                    for k in range(KT):
                        for n, (x, w) in enumerate(((core.xh, core.wh), (core.xl, core.wh), (core.xh, core.wl))):
                            last = pe.matmul(ps[:, 4 + j // 2, 256 * (j % 2):256 * (j % 2) + 256],
                                             tokens(x, k, j), w[:, 0:2, k, :],
                                             start=(k == 0 and n == 0), stop=(k == KT - 1 and n == 2))
                    if j % 2:
                        last.then_inc(sig["tok"], 1)


class Ring:

    def __init__(self, core, sig, steps):
        self.c, self.sig, self.steps = core, sig, steps

    def bank(self, name, unit):
        i = unit * len(self.steps) + self.steps.index(name)
        return self.c.ps[:, 2 * (i % 4):2 * (i % 4) + 2, :].rearrange("p a b -> p (a b)")

    def start(self, pe, name, unit):
        back = unit * len(self.steps) + self.steps.index(name) - 4
        if back >= 0:
            pe.wait_ge(self.sig["out_" + self.steps[back % len(self.steps)]], back // len(self.steps) + 1)
        return self.bank(name, unit)

    def full(self, eng, name, unit):
        eng.wait_ge(self.sig["pe"], unit * len(self.steps) + self.steps.index(name) + 1)
        return self.bank(name, unit)


LEVELS = (64, 32, 16, 8, 4, 2, 1)


def linear_mixer(nc, core, name, kind, mem, z, zv, yh, yl, y0, k):
    H = 512
    ret, gla, hgrn = kind == "ret", kind == "gla", kind == "hgrn"
    sc, dd = mem("scores", [P, 8, P]), mem("d", [P, 2, H])
    if ret:
        rot, sel = mem("rot", [P, 2, H]), mem("sel", [P, 4, P])
    if gla:
        sel = mem("sel", [P, 4, P])
    q, kk, c = mem("q", [P, H]), mem("k", [P, H]), None if ret else mem("c", [P, H])
    qe, ke = (mem("qe", [P, 2, H]), mem("ke", [P, 2, H])) if not ret else (mem("qe", [P, 1, H]), mem("ke", [P, 1, H]))
    kt, xs = mem("k_tok", [P, 4, P]), mem("state", [P, 5, P])
    psi = kk[:, :].rearrange("p (j t) -> p j t", t=P) if ret else mem("state_new", [P, 4, P])
    ident, bd, bdm = mem("ident", [P, P]), mem("heads", [P, P]), mem("head_mean", [P, P])
    gain, eend, epst = mem("gain", [P, 2]), mem("end", [P, 4]), mem("eps", [P, 1])
    if not ret:
        masks, onesr = mem("masks", [P, 8, P], I32), mem("ones", [P, P])
    if ret:
        dec, xz = mem("decay", [P, 2, P]), mem("xi_zeta", [P, 2, P])
        gend = mem("chunk_decay", [P, 2])
    if gla:
        w2e, bcol = mem("w2", [16, 2, P]), mem("b", [P, 2])
    units = [(u, hf) for u in range(2) for hf in range(2)]
    steps = (["qs", "ks", "score"] if ret else (["qk", "gate"] if gla else []) + [f"l{i}" for i in range(8)]) + \
        ["kt", "psi", "y"] + (["mean"] if ret else []) + ["var"]
    nconst = 16 * {"ret": 4, "gla": 7, "hgrn": 6}[kind]
    with ExitStack() as ctx:
        sig = ctx.enter_context(Signals(nc, name))
        ring = Ring(core, sig, steps)
        block = ctx.enter_context(nc.Block())

        def tk(buf, j):
            return buf[:, j * P:j * P + P]

        @block.sync
        def _(sp):
            sp.dma_start(ident[:, :], k["ident"]).then_inc(sig["consts"], 16)
            sp.dma_start(bd[:, :], k["heads"]).then_inc(sig["consts"], 16)
            sp.dma_start(bdm[:, :], k["head_mean"]).then_inc(sig["consts"], 16)
            if ret:
                sp.dma_start(gend[:, :], k["ret_end"]).then_inc(sig["consts"], 16)
            else:
                sp.dma_start(gain[:, :], k[kind + "_gain"]).then_inc(sig["consts"], 16)
                sp.dma_start(masks[:, :, :], k["levels"]).then_inc(sig["consts"], 16)
                sp.dma_start(onesr[:, :], k["ones"]).then_inc(sig["consts"], 16)
            if gla:
                sp.dma_start(sel[:, :, :], k["gla_sel"]).then_inc(sig["consts"], 16)
                sp.wait_ge(sig["zeroed"], 2)
                for h in range(4):
                    u, o = h // 2, 64 * (h % 2)
                    sp.dma_start(w2e[:, u, o:o + 32], k["gla_w2"][:, 32 * h:32 * h + 32]).then_inc(sig["w2"], 16)
                    sp.dma_start(bcol[o:o + 32, u:u + 1], k["gla_b"][32 * h:32 * h + 32, :]).then_inc(sig["w2"], 16)
            if ret:
                for n, (u, hf) in enumerate(units):
                    if n:
                        sp.wait_ge(sig["unit"], n)
                    sp.dma_start(rot[:, :, :], k["rot"][:, :, hf * H:hf * H + H]).then_inc(sig["unit_consts"], 16)
                    sp.dma_start(sel[:, :, :], k["ret_sel"][:, 4 * u:4 * u + 4, :]).then_inc(sig["unit_consts"], 16)
                    sp.dma_start(dec[:, :, :], k["ret_decay"][:, 2 * u:2 * u + 2, :]).then_inc(sig["unit_consts"], 16)
                    sp.dma_start(xz[:, :, :], k["ret_xz"][:, 2 * u:2 * u + 2, :]).then_inc(sig["unit_consts"], 16)

        @block.tensor
        def _(pe):
            pe.wait_ge(sig["consts"], nconst)
            if gla:
                pe.wait_ge(sig["w2"], 128)
            for n, (u, hf) in enumerate(units):
                t0 = hf * H
                cols = slice(t0, t0 + H)
                if n:
                    pe.wait_ge(sig["unit"], n)
                if ret:
                    pe.wait_ge(sig["unit_consts"], 64 * (n + 1))
                    for i, s in enumerate(("qs", "ks")):
                        b = ring.start(pe, s, n)
                        pe.matmul(b[:, 0:H], sel[:, 2 * i, :], z[:, i, cols], start=True, stop=True)
                        pe.matmul(b[:, H:2 * H], sel[:, 2 * i + 1, :], z[:, i, cols], start=True, stop=True
                                  ).then_inc(sig["pe"], 1)
                if gla:
                    b = ring.start(pe, "qk", n)
                    pe.matmul(b[:, 0:H], sel[:, u, :], z[:, 0, cols], start=True, stop=True)
                    pe.matmul(b[:, H:2 * H], sel[:, 2 + u, :], z[:, 1, cols], start=True, stop=True
                              ).then_inc(sig["pe"], 1)
                    b = ring.start(pe, "gate", n)
                    pe.matmul(b[:, 0:H], w2e[:, u, :], z[0:16, 2, cols], start=True, stop=True).then_inc(sig["pe"], 1)
                for i, s in enumerate(["score"] if ret else [f"l{i}" for i in range(8)]):
                    b = ring.start(pe, s, n)
                    if ret or i == 7:
                        pe.wait_ge(sig["q"], n + 1)
                        pe.wait_ge(sig["k"], n + 1)
                        qa, ka = (q[:, :], kk[:, :])
                        if hgrn:
                            qa = z[:, u, cols]
                    else:
                        pe.wait_ge(sig["level"], 7 * n + i + 1)
                        qa, ka = qe[:, i % 2, :], ke[:, i % 2, :]
                    for h in range(2):
                        for j in range(4):
                            o = (4 * h + j) * P
                            last = pe.matmul(b[:, o:o + P], tk(ka, j)[64 * h:64 * h + 64, :],
                                             tk(qa, j)[64 * h:64 * h + 64, :], start=True, stop=True)
                    last.then_inc(sig["pe"], 1)
                b = ring.start(pe, "kt", n)
                pe.wait_ge(sig["kd"], n + 1)
                for j in range(4):
                    last = pe.transpose(tk(b, j), tk(ke[:, 0, :], j), ident[:, :])
                last.then_inc(sig["pe"], 1)
                b = ring.start(pe, "psi", n)
                pe.wait_ge(sig["out_kt"], n + 1)
                for j in range(4):
                    last = pe.matmul(tk(b, j), kt[:, j, :], zv[:, 4 * hf + j, u * P:u * P + P], start=True, stop=True)
                last.then_inc(sig["pe"], 1)
                b = ring.start(pe, "y", n)
                pe.wait_ge(sig["states"], 4 * n + 4)
                pe.wait_ge(sig["scores"], n + 1)
                pe.wait_ge(sig["qd"], n + 1)
                for j in range(4):
                    for h in range(2):
                        dst = b[64 * h:64 * h + 64, j * P:j * P + P]
                        pe.matmul(dst, xs[:, j, 64 * h:64 * h + 64], tk(qe[:, 0, :], j), start=True, stop=False)
                        last = pe.matmul(dst, zv[:, 4 * hf + j, u * P + 64 * h:u * P + 64 * h + 64],
                                         sc[:, 4 * h + j, :], start=False, stop=True)
                last.then_inc(sig["pe"], 1)
                if ret:
                    b = ring.start(pe, "mean", n)
                    pe.wait_ge(sig["out_y"], n + 1)
                    pe.matmul(b[:, 0:H], bdm[:, :], dd[:, 0, :], start=True, stop=True).then_inc(sig["pe"], 1)
                b = ring.start(pe, "var", n)
                pe.wait_ge(sig["sq"], n + 1)
                pe.matmul(b[:, 0:H], bdm[:, :], qe[:, 0, :], start=True, stop=True).then_inc(sig["pe"], 1)

        @block.scalar
        def _(act):
            for n, (u, hf) in enumerate(units):
                cols = slice(hf * H, hf * H + H)
                if n:
                    act.wait_ge(sig["unit"], n)
                d0, d1 = dd[:, 0, :], dd[:, 1, :]
                if gla:
                    b = ring.full(act, "qk", n)
                    act.activation(q[:, :], b[:, 0:H], ACT.Copy).then_inc(sig["q"], 1)
                    act.activation(kk[:, :], b[:, H:2 * H], ACT.Copy).then_inc(sig["out_qk"], 1)
                    act.wait_ge(sig["out_qk"], n + 1)
                    act.wait_ge(sig["consts"], nconst)
                    act.wait_ge(sig["w2"], 128)
                    b = ring.full(act, "gate", n)
                    act.activation(c[:, :], b[:, 0:H], ACT.Identity, bias=bcol[:, u:u + 1]).then_inc(sig["out_gate"], 1)
                    act.wait_ge(sig["out_gate"], n + 1)
                    x = c[:, :]
                if hgrn:
                    x = z[:, 2 + u, cols]
                if not ret:
                    act.activation(d0, x, ACT.Abs).then_inc(sig["abs"], 1)
                    act.wait_ge(sig["abs"], n + 1)
                    act.activation(d0, d0, ACT.Exp, scale=-1.0).then_inc(sig["expabs"], 1)
                    act.wait_ge(sig["expabs"], n + 1)
                    act.activation(d1, d0, ACT.Ln, bias=1.0).then_inc(sig["ln"], 1)
                    if hgrn:
                        act.wait_ge(sig["lwx"], n + 1)
                        act.activation(kk[:, :], kk[:, :], ACT.Exp).then_inc(sig["k"], 1)
                    for i in range(7):
                        act.wait_ge(sig["dist"], 7 * n + i + 1)
                        act.activation(dd[:, i % 2, :], dd[:, i % 2, :], ACT.Exp).then_inc(sig["e"], 1)
                    act.wait_ge(sig["todecay"], n + 1)
                    act.activation(d0, d0, ACT.Exp).then_inc(sig["ekd"], 1)
                    act.activation(d1, c[:, :], ACT.Exp).then_inc(sig["eqd"], 1)
                    act.activation(eend[:, :], c[:, :].rearrange("p (j t) -> p j t", t=P)[:, :, P - 1], ACT.Exp
                                   ).then_inc(sig["eend"], 1)
                b = ring.full(act, "y", n)
                act.wait_ge(sig["qd"], n + 1)
                act.wait_ge(sig["kd"], n + 1)
                act.activation(d0, b[:, 0:H], ACT.Copy).then_inc(sig["out_y"], 1)
                if ret:
                    act.wait_ge(sig["out_mean"], n + 1)
                else:
                    act.wait_ge(sig["out_y"], n + 1)
                act.activation(qe[:, 0, :], d0, ACT.Square).then_inc(sig["sq"], 1)
                b = ring.full(act, "var", n)
                act.wait_ge(sig["eps"], 1)
                act.activation(d1, b[:, 0:H], ACT.Sqrt, bias=epst[:, 0:1]).then_inc(sig["out_var"], 1)
                act.wait_ge(sig["outv"], n + 1)
                act.activation(yh[:, y0 + u, cols], d0, ACT.Copy).then_inc(sig["yh"], 1)

        @block.vector
        def _(dve):
            dve.memset(epst[:, :], 1e-6).then_inc(sig["eps"], 1)
            if gla:
                dve.memset(w2e[:, :, :], 0.0).then_inc(sig["zeroed"], 1)
                dve.memset(bcol[:, :], 0.0).then_inc(sig["zeroed"], 1)
            dve.memset(sc[:, :, :], 0.0).then_inc(sig["sc0"], 1)
            dve.wait_ge(sig["sc0"], 1)
            dve.wait_ge(sig["consts"], nconst)
            for n, (u, hf) in enumerate(units):
                cols = slice(hf * H, hf * H + H)
                d0, d1 = dd[:, 0, :], dd[:, 1, :]
                if n:
                    dve.wait_ge(sig["unit"], n)
                if hf:
                    dve.tensor_copy(xs[:, 0, :], xs[:, 4, :]).then_inc(sig["carried"], 1)
                else:
                    dve.memset(xs[:, 0, :], 0.0).then_inc(sig["carried"], 1)
                if ret:
                    dve.wait_ge(sig["unit_consts"], 64 * (n + 1))
                    for s, dst, nm in (("qs", q, "q"), ("ks", kk, "k")):
                        b = ring.full(dve, s, n)
                        dve.tensor_tensor(dst[:, :], b[:, 0:H], rot[:, 0, :], ALU.mult).then_inc(sig[nm + "cos"], 1)
                        if nm == "k":
                            dve.wait_ge(sig["q"], n + 1)
                        dve.tensor_tensor(d0, b[:, H:2 * H], rot[:, 1, :], ALU.mult).then_inc(sig["out_" + s], 1)
                        dve.wait_ge(sig[nm + "cos"], n + 1)
                        dve.wait_ge(sig["out_" + s], n + 1)
                        dve.tensor_tensor(dst[:, :], dst[:, :], d0, ALU.add).then_inc(sig[nm], 1)
                    b = ring.full(dve, "score", n)
                    for h in range(2):
                        last = dve.tensor_tensor(sc[:, 4 * h:4 * h + 4, :], b[:, h * H:h * H + H].rearrange(
                            "p (j t) -> p j t", t=P), bc(dec[:, h, :], 4), ALU.mult)
                        if h == 0:
                            last.then_inc(sig["score_h0"], 1)
                    last.then_inc(sig["out_score"], 1)
                    dve.wait_ge(sig["out_score"], n + 1)
                    dve.sem_inc(sig["scores"], 1)
                else:
                    if hgrn:
                        x = z[:, 2 + u, cols]
                    else:
                        dve.wait_ge(sig["out_gate"], n + 1)
                        x = c[:, :]
                    dve.wait_ge(sig["ln"], n + 1)
                    dve.scalar_tensor_tensor(out=d0, in0=x, scalar=0.0, in1=d1, op0=ALU.min,
                                             op1=ALU.subtract).then_inc(sig["lw"], 1)
                    dve.wait_ge(sig["lw"], n + 1)
                    if hgrn:
                        dve.tensor_tensor(kk[:, :], d0, x, ALU.subtract).then_inc(sig["lwx"], 1)
                    else:
                        dve.tensor_scalar(d0, d0, 1.0 / 16.0, None, ALU.mult).then_inc(sig["lw16"], 1)
                        dve.wait_ge(sig["lw16"], n + 1)
                    for j in range(4):
                        dve.tensor_tensor_scan(out=tk(c, j), data0=onesr[:, :], data1=tk(d0, j), initial=0.0,
                                               op0=ALU.mult, op1=ALU.add).then_inc(sig["scan"], 1)
                    dve.wait_ge(sig["scan"], 4 * n + 4)
                    if hgrn:
                        dve.wait_ge(sig["lwx"], n + 1)

                    def take(i):
                        b = ring.full(dve, f"l{i}", n)
                        if n or i:
                            dve.wait_ge(sig["taken"], 8 * n + i)
                        dve.copy_predicated(sc[:, :, :], bc(masks[:, i, :], 8),
                                            b.rearrange("p (j t) -> p j t", t=P)).then_inc(sig[f"out_l{i}"], 1)
                        dve.wait_ge(sig[f"out_l{i}"], n + 1)
                        dve.sem_inc(sig["taken"], 1)
                    for i, L in enumerate(LEVELS):
                        if i >= 2:
                            dve.wait_ge(sig["level"], 7 * n + i - 1)
                        c3 = c[:, :].rearrange("p (n t) -> p n t", t=2 * L)
                        e3 = dd[:, i % 2, :].rearrange("p (n t) -> p n t", t=2 * L)
                        ref = bcl(c3[:, :, L - 1], L)
                        dve.tensor_tensor(e3[:, :, L:2 * L], c3[:, :, L:2 * L], ref, ALU.subtract
                                          ).then_inc(sig["dist_up"], 1)
                        dve.wait_ge(sig["dist_up"], 7 * n + i + 1)
                        dve.tensor_tensor(e3[:, :, 0:L], ref, c3[:, :, 0:L], ALU.subtract
                                          ).then_inc(sig["dist"], 1)
                        if i >= 2:
                            take(i - 2)
                    dve.wait_ge(sig["level"], 7 * n + 7)
                    c3 = c[:, :].rearrange("p (n t) -> p n t", t=P)
                    dve.tensor_tensor(d0.rearrange("p (n t) -> p n t", t=P), bcl(c3[:, :, P - 1], P), c3,
                                      ALU.subtract).then_inc(sig["todecay"], 1)
                    for i in range(5, 8):
                        take(i)
                    dve.wait_ge(sig["out_l7"], n + 1)
                    dve.sem_inc(sig["scores"], 1)
                b = ring.full(dve, "kt", n)
                dve.tensor_copy(flat(kt[:, :, :]), b[:, 0:H]).then_inc(sig["out_kt"], 1)
                b = ring.full(dve, "psi", n)
                dve.tensor_tensor(psi[:, :, :], b[:, 0:H].rearrange("p (j t) -> p j t", t=P), bc(bd[:, :], 4),
                                  ALU.mult).then_inc(sig["out_psi"], 1)
                dve.wait_ge(sig["out_psi"], n + 1)
                dve.wait_ge(sig["carried"], n + 1)
                if not ret:
                    dve.wait_ge(sig["eend"], n + 1)
                for j in range(4):
                    if j:
                        dve.wait_ge(sig["states"], 4 * n + j)
                    dve.scalar_tensor_tensor(out=xs[:, j + 1, :], in0=xs[:, j, :],
                                             scalar=gend[:, u:u + 1] if ret else eend[:, j:j + 1],
                                             in1=psi[:, j, :], op0=ALU.mult, op1=ALU.add).then_inc(sig["states"], 1)
                if ret:
                    dve.wait_ge(sig["out_y"], n + 1)
                    b = ring.full(dve, "mean", n)
                    dve.tensor_tensor(d0, d0, b[:, 0:H], ALU.subtract).then_inc(sig["out_mean"], 1)
                dve.wait_ge(sig["out_var"], n + 1)
                dve.reciprocal(d1, d1).then_inc(sig["rstd"], 1)
                dve.wait_ge(sig["rstd"], n + 1)
                dve.wait_ge(sig["sq"], n + 1)
                if ret:
                    dve.tensor_tensor(d1, d0, d1, ALU.mult).then_inc(sig["yn"], 1)
                else:
                    dve.scalar_tensor_tensor(out=d1, in0=d0, scalar=gain[:, u:u + 1], in1=d1, op0=ALU.mult,
                                             op1=ALU.mult).then_inc(sig["yn"], 1)
                dve.wait_ge(sig["yn"], n + 1)
                g = z[:, (2 if ret else 3 if gla else 4) + u, cols]
                dve.tensor_tensor(d0, d1, g, ALU.mult).then_inc(sig["outv"], 1)

        @block.gpsimd
        def _(pool):
            for n, (u, hf) in enumerate(units):
                cols = slice(hf * H, hf * H + H)
                d0, d1 = dd[:, 0, :], dd[:, 1, :]
                if n:
                    pool.wait_ge(sig["unit"], n)
                qin = z[:, u, cols] if hgrn else q[:, :]
                if gla:
                    pool.wait_ge(sig["q"], n + 1)
                    pool.wait_ge(sig["out_qk"], n + 1)
                    pool.engine_nop().then_inc(sig["k"], 1)
                if hgrn:
                    pool.wait_ge(sig["k"], n + 1)
                    pool.engine_nop().then_inc(sig["q"], 1)
                if ret:
                    pool.wait_ge(sig["unit_consts"], 64 * (n + 1))
                    pool.wait_ge(sig["q"], n + 1)
                    pool.wait_ge(sig["k"], n + 1)
                    v4 = lambda x: x.rearrange("p (j t) -> p j t", t=P)
                    pool.tensor_tensor(v4(ke[:, 0, :]), v4(kk[:, :]), bc(xz[:, 1, :], 4), ALU.mult
                                       ).then_inc(sig["kd"], 1)
                    pool.tensor_tensor(v4(qe[:, 0, :]), v4(q[:, :]), bc(xz[:, 0, :], 4), ALU.mult
                                       ).then_inc(sig["qd"], 1)
                else:
                    for i in range(7):
                        pool.wait_ge(sig["e"], 7 * n + i + 1)
                        if i >= 2:
                            ring.full(pool, f"l{i - 2}", n)
                        pool.tensor_tensor(qe[:, i % 2, :], qin, dd[:, i % 2, :], ALU.mult).then_inc(sig["qe"], 1)
                        pool.tensor_tensor(ke[:, i % 2, :], kk[:, :], dd[:, i % 2, :], ALU.mult
                                           ).then_inc(sig["ke"], 1)
                        pool.wait_ge(sig["qe"], 7 * n + i + 1)
                        pool.wait_ge(sig["ke"], 7 * n + i + 1)
                        pool.sem_inc(sig["level"], 1)
                    ring.full(pool, "l6", n)
                    pool.wait_ge(sig["ekd"], n + 1)
                    pool.tensor_tensor(ke[:, 0, :], kk[:, :], d0, ALU.mult).then_inc(sig["kd"], 1)
                    pool.wait_ge(sig["eqd"], n + 1)
                    pool.tensor_tensor(qe[:, 0, :], qin, d1, ALU.mult).then_inc(sig["qd"], 1)
                pool.wait_ge(sig["yh"], n + 1)
                pool.tensor_tensor(yl[:, y0 + u, cols], d0, yh[:, y0 + u, cols].bitcast(F32), ALU.subtract
                                   ).then_inc(sig["unit"], 1)


def rwkv_mixer(nc, core, mem, z, yh, yl, y0, k):
    H = 512
    r_, k_, v_, wa_, gl_ = 0, 2, 4, 6, 7
    cst = mem("masks", [P, 7, P])
    ident, heads, hmean, ones = (mem(n, [P, P]) for n in ("ident", "heads", "head_mean", "ones"))
    wa2, g2, pc, epst = mem("wa2", [P, 256]), mem("g2", [P, 256]), mem("params", [P, 2, 8]), mem("eps", [P, 2])
    em, ecm, eend = mem("e_mid", [P, 4]), mem("e_mid_end", [P, 4]), mem("e_end", [P, 4])
    mt, rk, rb = mem("m_t", [P, 8, P]), mem("rho_kappa", [P, 8, P]), mem("rho_beta", [P, 8, P])
    l16, l32, l64 = mem("l16", [P, 8, P]), mem("l32", [P, 8, P]), mem("l64", [P, 8, P])
    jj, jt, j2, j2t = mem("j", [P, 8, P]), mem("jt", [P, 8, P]), mem("j2", [P, 8, P]), mem("j2t", [P, 8, P])
    xx, j4, j4t = mem("x", [P, 8, P]), mem("j4", [P, 8, P]), mem("j4t", [P, 8, P])
    at_, bt, kt, vt = (mem(n, [P, 4, P]) for n in ("a_tok", "b_tok", "k_tok", "v_tok"))
    xs = mem("state", [P, 5, P])

    def halves(buf):
        f = flat(buf[:, :, :])
        return f[:, 0:H], f[:, H:2 * H]
    lw, c = halves(jj)
    a, kk = halves(jt)
    kp, e1 = halves(j2)
    e3, e2 = halves(j2t)
    tmp, _ = halves(xx)
    al, be = halves(j4)
    ka, rh = halves(j4t)
    a0f, b0f, k0f = e3, e1, e2
    xt, ww, j8t = jj, jt, j2
    ta, mv = halves(j4)
    tat, tmv = halves(j4t)
    phi, psi = halves(j2t)
    uu, _ = halves(jj)
    dg, _ = halves(mt)
    y, sq = halves(l16)
    sd, fin = halves(l32)
    bv, _ = halves(l64)
    M_JT, M_L16, M_L32, M_L64, M_J, M_SU, M_IU = range(7)
    W0, A0, K_K, K_A, R_K, LN_W, LN_B, OMKA = range(8)
    steps = ["wa", "norm", "tr1", "tr2", "L", "N", "M", "RK", "RB", "J2", "J2t", "X2", "J4", "J4t", "X4", "J8t", "X8"]
    for lv in (16, 32, 64):
        steps += [f"T{lv}", f"W{lv}", f"Y{lv}"]
    steps += ["TA", "TAt", "PP", "c0", "c1", "c2", "c3", "U", "y", "bg", "mean", "var"]
    units = [(u, hf) for u in range(2) for hf in range(2)]
    name = "rwkv"
    NCONST = 16 * 9

    def tk(buf, j):
        return buf[:, j * P:j * P + P]

    def j4v(x):
        return x.rearrange("p (j t) -> p j t", t=P)

    with ExitStack() as ctx:
        sig = ctx.enter_context(Signals(nc, name))
        ring = Ring(core, sig, steps)
        block = ctx.enter_context(nc.Block())

        def need(eng, n, *names):
            for x in names:
                eng.wait_ge(sig[x], n + 1)

        @block.sync
        def _(sp):
            for dst, src in ((cst[:, :, :], k["rwkv_masks"]), (ident[:, :], k["ident"]), (heads[:, :], k["heads"]),
                             (hmean[:, :], k["head_mean"]), (ones[:, :], k["ones"]), (wa2[0:64, :], k["w2"]),
                             (wa2[64:128, :], k["a2"]), (g2[:, :], k["g2"]), (pc[:, :, 0:7], k["params"])):
                sp.dma_start(dst, src).then_inc(sig["consts"], 16)

        @block.tensor
        def _(pe):
            pe.wait_ge(sig["consts"], NCONST)
            pe.wait_ge(sig["squashed"], 2)
            for n, (u, hf) in enumerate(units):
                cols = slice(hf * H, hf * H + H)
                feat = slice(u * P, u * P + P)
                if n:
                    pe.wait_ge(sig["unit"], n)

                def step(s, *needs):
                    b = ring.start(pe, s, n)
                    need(pe, n, *needs)
                    return b

                def each(b, lhs, rhs):
                    for h in range(2):
                        for j in range(4):
                            o = (4 * h + j) * P
                            last = pe.matmul(b[:, o:o + P], lhs(h, j), rhs(h, j), start=True, stop=True)
                    last.then_inc(sig["pe"], 1)

                def mats(s, lhs, rhs, *needs):
                    each(step(s, *needs), lambda h, j: lhs[:, 4 * h + j, :], lambda h, j: rhs[:, 4 * h + j, :])

                def feats(s, lhs, rhs, *needs):
                    each(step(s, *needs), lambda h, j: tk(lhs, j)[64 * h:64 * h + 64, :],
                         lambda h, j: tk(rhs, j)[64 * h:64 * h + 64, :])

                b = step("wa")
                pe.matmul(b[:, 0:H], wa2[0:64, feat], z[0:64, wa_, cols], start=True, stop=True)
                pe.matmul(b[:, H:2 * H], wa2[64:128, feat], z[64:128, wa_, cols], start=True, stop=True
                          ).then_inc(sig["pe"], 1)
                b = step("norm", "sqk")
                pe.matmul(b[:, 0:H], heads[:, :], tmp, start=True, stop=True).then_inc(sig["pe"], 1)
                for s, (x0, x1), needs in (("tr1", (a0f, b0f), ("a0f", "b0f")), ("tr2", (k0f, z[:, v_ + u, cols]), ("k0f",))):
                    b = step(s, *needs)
                    for j in range(4):
                        pe.transpose(tk(b, j), tk(x0, j), ident[:, :])
                    for j in range(4):
                        last = pe.transpose(tk(b, 4 + j), tk(x1, j), ident[:, :])
                    last.then_inc(sig["pe"], 1)
                feats("L", al, be, "al", "be")
                feats("N", be, al)
                feats("M", ka, al, "ka")
                feats("RK", ka, rh, "rh")
                feats("RB", be, rh)
                mats("J2", jt, jj, "out_L", "out_J")
                mats("J2t", jj, jt)
                mats("X2", j2t, xx, "out_J2t", "out_N")
                mats("J4", j2t, j2, "out_J2")
                mats("J4t", j2, j2t)
                mats("X4", j4t, xx, "out_J4t", "out_X2")
                mats("J8t", j4, j4t, "out_J4")
                mats("X8", j8t, xx, "out_J8t", "out_X4")
                before = "out_X8"
                for lv, lm in ((16, l16), (32, l32), (64, l64)):
                    b = step(f"T{lv}", before)
                    for i in range(8):
                        last = pe.transpose(b[:, i * P:i * P + P], xx[:, i, :], ident[:, :])
                    last.then_inc(sig["pe"], 1)
                    mats(f"W{lv}", lm, xx)
                    mats(f"Y{lv}", xt, ww, f"out_T{lv}", f"out_W{lv}")
                    before = f"out_Y{lv}"

                def heads64(b, half, lhs, rhs):
                    for j in range(4):
                        for h in range(2):
                            o = half * H + j * P + 64 * h
                            last = pe.matmul(b[:, o:o + 64], lhs[:, 4 * h + j, :], rhs(j, h), start=True, stop=True)
                    return last
                b = step("TA", before, "out_tr1", "out_tr2", "out_M")
                heads64(b, 0, xx, lambda j, h: at_[:, j, 64 * h:64 * h + 64])
                heads64(b, 1, mt, lambda j, h: vt[:, j, 64 * h:64 * h + 64]).then_inc(sig["pe"], 1)
                b = step("TAt", "out_TA")
                for j in range(4):
                    for h in range(2):
                        pe.matmul(b[64 * h:64 * h + 64, j * P:j * P + P], at_[:, j, 64 * h:64 * h + 64],
                                  xx[:, 4 * h + j, :], start=True, stop=True)
                heads64(b, 1, xx, lambda j, h: tk(mv, j)[:, 64 * h:64 * h + 64]).then_inc(sig["pe"], 1)
                b = step("PP", "out_TAt")
                for j in range(4):
                    pe.matmul(tk(b, j), tk(ta, j), bt[:, j, :], start=True, stop=True)
                for j in range(4):
                    pe.matmul(tk(b, 4 + j), kt[:, j, :], vt[:, j, :], start=True, stop=False)
                    last = pe.matmul(tk(b, 4 + j), bt[:, j, :], tk(tmv, j), start=False, stop=True)
                last.then_inc(sig["pe"], 1)
                for j in range(4):
                    b = step(f"c{j}", "phi", "psi", "carried" if j == 0 else f"out_c{j - 1}")
                    pe.matmul(b[:, 0:P], tk(phi, j), xs[:, j, :], start=True, stop=True).then_inc(sig["pe"], 1)
                b = step("U")
                for j in range(4):
                    last = pe.matmul(tk(b, j), tk(tat, j), xs[:, j, :], start=True, stop=True)
                last.then_inc(sig["pe"], 1)
                b = step("y", "out_U", "out_RK", "out_RB", "r0")
                for j in range(4):
                    for h in range(2):
                        dst = b[64 * h:64 * h + 64, j * P:j * P + P]
                        hc = slice(64 * h, 64 * h + 64)
                        pe.matmul(dst, xs[:, j, hc], tk(z[:, k_ + u, cols], j), start=True, stop=False)
                        pe.matmul(dst, vt[:, j, hc], rk[:, 4 * h + j, :], start=False, stop=False)
                        last = pe.matmul(dst, tk(uu, j)[:, hc], rb[:, 4 * h + j, :], start=False, stop=True)
                last.then_inc(sig["pe"], 1)
                b = step("bg", "bonus")
                pe.matmul(b[:, 0:H], heads[:, :], z[:, r_ + u, cols], start=True, stop=True)
                pe.matmul(b[:, H:2 * H], g2[:, feat], z[:, gl_, cols], start=True, stop=True).then_inc(sig["pe"], 1)
                b = step("mean", "out_y")
                pe.matmul(b[:, 0:H], hmean[:, :], y, start=True, stop=True).then_inc(sig["pe"], 1)
                b = step("var", "sqy")
                pe.matmul(b[:, 0:H], hmean[:, :], sq, start=True, stop=True).then_inc(sig["pe"], 1)

        @block.scalar
        def _(act):
            act.activation(z[0:64, wa_, :], z[0:64, wa_, :], ACT.Tanh).then_inc(sig["squashed"], 1)
            act.activation(z[:, gl_, :], z[:, gl_, :], ACT.Sigmoid).then_inc(sig["squashed"], 1)
            act.wait_ge(sig["consts"], NCONST)
            act.wait_ge(sig["eps"], 2)
            for n, (u, hf) in enumerate(units):
                cols = slice(hf * H, hf * H + H)
                if n:
                    act.wait_ge(sig["unit"], n)

                def copy(s, dst, lo=0, hi=2 * H, signal=None, scale=1.0):
                    b = ring.full(act, s, n)
                    act.activation(dst, b[:, lo:hi], ACT.Copy, scale=scale).then_inc(sig[signal or "out_" + s], 1)

                b = ring.full(act, "wa", n)
                act.activation(lw, b[:, 0:H], ACT.Sigmoid, bias=pc[:, u, W0:W0 + 1]).then_inc(sig["w_sig"], 1)
                act.activation(a, b[:, H:2 * H], ACT.Sigmoid, bias=pc[:, u, A0:A0 + 1]).then_inc(sig["out_wa"], 1)
                need(act, n, "kk0")
                act.activation(tmp, kk, ACT.Square).then_inc(sig["sqk"], 1)
                b = ring.full(act, "norm", n)
                act.activation(tmp, b[:, 0:H], ACT.Sqrt, bias=epst[:, 0:1]).then_inc(sig["out_norm"], 1)
                need(act, n, "d1", "d3", "dm")
                act.activation(e1, e1, ACT.Exp).then_inc(sig["e1"], 1)
                act.activation(e2, e3, ACT.Exp, scale=-1.0).then_inc(sig["e2"], 1)
                act.wait_ge(sig["e2"], n + 1)
                act.activation(e3, e3, ACT.Exp).then_inc(sig["e3"], 1)
                c3 = j4v(c)
                act.activation(em[:, :], c3[:, :, P // 2 - 1], ACT.Exp).then_inc(sig["em"], 1)
                act.activation(ecm[:, :], ecm[:, :], ACT.Exp).then_inc(sig["ecm"], 1)
                act.activation(eend[:, :], c3[:, :, P - 1], ACT.Exp).then_inc(sig["eend"], 1)
                copy("tr1", flat(at_[:, :, :]), 0, H, "at")
                copy("tr1", flat(bt[:, :, :]), H, 2 * H, scale=-1.0)
                copy("tr2", flat(kt[:, :, :]), 0, H, "kt")
                copy("tr2", flat(vt[:, :, :]), H, 2 * H)
                copy("J2", flat(j2[:, :, :]))
                copy("J2t", flat(j2t[:, :, :]))
                copy("J4", flat(j4[:, :, :]))
                copy("J4t", flat(j4t[:, :, :]))
                copy("J8t", flat(j8t[:, :, :]))
                for lv in (16, 32, 64):
                    copy(f"T{lv}", flat(xt[:, :, :]))
                    copy(f"W{lv}", flat(ww[:, :, :]))
                copy("TA", flat(j4[:, :, :]))
                copy("TAt", flat(j4t[:, :, :]))
                copy("y", y, 0, H)
                need(act, n, "out_mean")
                act.activation(sq, y, ACT.Square).then_inc(sig["sqy"], 1)
                b = ring.full(act, "var", n)
                act.activation(sd, b[:, 0:H], ACT.Sqrt, bias=epst[:, 1:2]).then_inc(sig["out_var"], 1)
                need(act, n, "fin")
                act.activation(yh[:, y0 + u, cols], fin, ACT.Copy).then_inc(sig["yh"], 1)

        @block.vector
        def _(dve):
            dve.memset(epst[:, 0:1], 1e-12).then_inc(sig["eps"], 1)
            dve.memset(epst[:, 1:2], 64e-5).then_inc(sig["eps"], 1)
            dve.wait_ge(sig["consts"], NCONST)
            dve.tensor_scalar(pc[:, :, OMKA], pc[:, :, K_A], -1.0, 1.0, ALU.mult, ALU.add).then_inc(sig["omka"], 1)
            dve.wait_ge(sig["omka"], 1)
            for n, (u, hf) in enumerate(units):
                cols = slice(hf * H, hf * H + H)
                r, kin, v = z[:, r_ + u, cols], z[:, k_ + u, cols], z[:, v_ + u, cols]
                if n:
                    dve.wait_ge(sig["unit"], n)

                def par(i):
                    return pc[:, u, i:i + 1]

                def mul(out, x, y_, signal, *needs):
                    need(dve, n, *needs)
                    dve.tensor_tensor(out, x, y_, ALU.mult).then_inc(sig[signal], 1)

                if hf:
                    dve.tensor_copy(xs[:, 0, :], xs[:, 4, :]).then_inc(sig["carried"], 1)
                else:
                    dve.memset(xs[:, 0, :], 0.0).then_inc(sig["carried"], 1)
                dve.tensor_scalar(kk, kin, par(K_K), None, ALU.mult).then_inc(sig["kk0"], 1)
                need(dve, n, "w_sig", "out_wa")
                dve.tensor_scalar(lw, lw, -RWKV_DECAY, None, ALU.mult).then_inc(sig["lw"], 1)
                dve.tensor_scalar(kp, a, par(K_A), par(OMKA), ALU.mult, ALU.add).then_inc(sig["ka_"], 1)
                need(dve, n, "lw")
                for j in range(4):
                    last = dve.tensor_tensor_scan(out=tk(c, j), data0=ones[:, :], data1=tk(lw, j), initial=0.0,
                                                  op0=ALU.mult, op1=ALU.add)
                    last.then_inc(sig["scan"], 1)
                mul(kp, kp, kin, "kp", "ka_")
                dve.wait_ge(sig["scan"], 4 * n + 4)
                c3 = j4v(c)
                mid = bcl(c3[:, :, P // 2 - 1], P)
                dve.tensor_tensor(e1, c, lw, ALU.subtract).then_inc(sig["d1_"], 1)
                dve.tensor_tensor(j4v(e3), c3, mid, ALU.subtract).then_inc(sig["d3"], 1)
                dve.tensor_tensor(ecm[:, :], c3[:, :, P - 1], c3[:, :, P // 2 - 1], ALU.subtract).then_inc(sig["dm"], 1)
                need(dve, n, "d1_")
                dve.tensor_tensor(j4v(e1), j4v(e1), mid, ALU.subtract).then_inc(sig["d1"], 1)
                need(dve, n, "out_norm")
                dve.reciprocal(tmp, tmp).then_inc(sig["rn"], 1)
                mul(kk, kk, tmp, "kk", "rn")
                mul(al, kk, e1, "al", "kk", "e1")
                mul(a, kk, a, "kka")
                mul(be, a, e2, "be", "kka", "e2")
                mul(ka, kp, e2, "ka", "kp")
                mul(rh, r, e3, "rh", "e3")
                need(dve, n, "ecm", "be", "ka", "al")
                dve.tensor_tensor(j4v(b0f), j4v(be), bcl(ecm[:, :], P), ALU.mult).then_inc(sig["b0f"], 1)
                dve.tensor_tensor(j4v(k0f), j4v(ka), bcl(ecm[:, :], P), ALU.mult).then_inc(sig["k0f"], 1)
                need(dve, n, "em", "rh")
                dve.tensor_tensor(j4v(a0f), j4v(al), bcl(em[:, :], P), ALU.mult).then_inc(sig["a0f"], 1)

                def masked(s, dst, m, signal=None):
                    b = ring.full(dve, s, n)
                    dve.tensor_tensor(dst[:, :, :], b.rearrange("p (j t) -> p j t", t=P), bc(cst[:, m, :], 8),
                                      ALU.mult).then_inc(sig[signal or "out_" + s], 1)
                need(dve, n, "a0f", "b0f", "k0f", "bonus", "eend")
                masked("L", l16, M_L16, "l16")
                masked("L", l32, M_L32, "l32")
                masked("L", l64, M_L64, "l64")
                masked("L", jt, M_JT)
                masked("N", jj, M_J, "out_J")
                need(dve, n, "out_J")
                dve.tensor_tensor(xx[:, :, :], bc(ident[:, :], 8), jj[:, :, :], ALU.subtract).then_inc(sig["out_N"], 1)
                masked("M", mt, M_SU)
                masked("RK", rk, M_IU)
                masked("RB", rb, M_IU)
                need(dve, n, "out_N")
                x = flat(xx[:, :, :])

                def update(s, op):
                    b = ring.full(dve, s, n)
                    dve.tensor_tensor(x, x, b, op).then_inc(sig["out_" + s], 1)
                    need(dve, n, "out_" + s)
                for s in ("X2", "X4", "X8"):
                    update(s, ALU.add)
                for lv in (16, 32, 64):
                    update(f"Y{lv}", ALU.subtract)
                b = ring.full(dve, "PP", n)
                dve.tensor_tensor(j4v(phi), j4v(b[:, 0:H]), bc(heads[:, :], 4), ALU.mult).then_inc(sig["phi_"], 1)
                dve.tensor_tensor(j4v(psi), j4v(b[:, H:2 * H]), bc(heads[:, :], 4), ALU.mult).then_inc(sig["psi"], 1)
                need(dve, n, "phi_", "psi", "dg")
                dve.tensor_tensor(phi, phi, dg, ALU.add).then_inc(sig["phi"], 1)
                need(dve, n, "phi")
                dve.sem_inc(sig["out_PP"], 1)
                for j in range(4):
                    b = ring.full(dve, f"c{j}", n)
                    dve.tensor_tensor(xs[:, j + 1, :], b[:, 0:P], tk(psi, j), ALU.add).then_inc(sig[f"out_c{j}"], 1)
                b = ring.full(dve, "U", n)
                need(dve, n, "out_TAt")
                dve.scalar_tensor_tensor(out=uu, in0=b[:, 0:H], scalar=-1.0, in1=tmv, op0=ALU.mult,
                                         op1=ALU.subtract).then_inc(sig["out_U"], 1)
                b = ring.full(dve, "bg", n)
                dve.tensor_tensor(bv, b[:, 0:H], v, ALU.mult).then_inc(sig["bv"], 1)
                need(dve, n, "out_y")
                b2 = ring.full(dve, "mean", n)
                dve.tensor_tensor(y, y, b2[:, 0:H], ALU.subtract).then_inc(sig["out_mean"], 1)
                need(dve, n, "out_var", "out_mean")
                dve.reciprocal(sd, sd).then_inc(sig["rsd"], 1)
                need(dve, n, "sqy")
                mul(y, y, sd, "yn", "rsd")
                need(dve, n, "yn")
                dve.tensor_scalar(y, y, par(LN_W), par(LN_B), ALU.mult, ALU.add).then_inc(sig["yw"], 1)
                need(dve, n, "yw", "bv")
                dve.tensor_tensor(y, y, bv, ALU.add).then_inc(sig["yb"], 1)
                need(dve, n, "yb")
                dve.tensor_tensor(fin, y, b[:, H:2 * H], ALU.mult).then_inc(sig["fin"], 1)
                need(dve, n, "fin")
                dve.sem_inc(sig["out_bg"], 1)

        @block.gpsimd
        def _(pool):
            for n, (u, hf) in enumerate(units):
                cols = slice(hf * H, hf * H + H)
                r = z[:, r_ + u, cols]
                if n:
                    pool.wait_ge(sig["unit"], n)
                need(pool, n, "rh", "em", "kp", "kk0")
                pool.tensor_tensor(j4v(z[:, k_ + u, cols]), j4v(rh), bcl(em[:, :], P), ALU.mult).then_inc(sig["r0"], 1)
                pool.tensor_scalar(r, r, pc[:, u, R_K:R_K + 1], None, ALU.mult).then_inc(sig["rrk"], 1)
                need(pool, n, "rrk")
                pool.tensor_tensor(r, r, kp, ALU.mult).then_inc(sig["bonus"], 1)
                ring.full(pool, "TA", n)
                need(pool, n, "eend")
                pool.tensor_tensor(j4v(dg), bc(ident[:, :], 4), bcl(eend[:, :], P), ALU.mult).then_inc(sig["dg"], 1)
                need(pool, n, "yh")
                pool.tensor_tensor(yl[:, y0 + u, cols], fin, yh[:, y0 + u, cols].bitcast(F32), ALU.subtract
                                   ).then_inc(sig["unit"], 1)


def attention_phase(nc, core, mem, qks, vs, scratch, k):
    ob, bias = mem("out", [P, 2, NC, 4, 66]), mem("bias", [P, 2, 2, P])
    sb, pt = mem("scores", [P, 2, 4, 2 * P]), mem("probs_t", [P, 2, 8, P])
    ident, neg = mem("ident", [P, P]), mem("neg_max", [P, 2, 4])
    ps = core.ps
    units = [(g, h, hf) for g in range(3) for h in range(4) for hf in range(2)]
    N = len(units)

    def before(g, j):
        return (g == 0 and j > 0) or (g == 1 and j % 2 == 1)

    def spans(g, hf):
        return {0: [(slice(1, 4), slice(0, 1)), (slice(0, 4), None)][hf], 1: (slice(1, 4, 2), slice(0, 4, 2)),
                2: (None, slice(0, 4))}[g]

    def blocks(g, hf):
        return [(i, b) for i in range(4) for b in range(2) if b or before(g, 4 * hf + i)]

    def tokens(g, buf, tile, row, first, n=1):
        x = buf[row:row + 64, tile, :]
        if g == 0:
            return x[:, first * P:(first + n) * P]
        if g == 1:
            z, nb = first // 2, first % 2
            return x.rearrange("p (l z) -> p z l", z=4)[:, z, nb * P:(nb + n) * P]
        return x.rearrange("p (l z) -> p z l", z=8)[:, first, :]

    with ExitStack() as ctx:
        sig = ctx.enter_context(Signals(nc, "att"))
        block = ctx.enter_context(nc.Block())

        def s_bank(n):
            return ps[:, 2 * (n % 2):2 * (n % 2) + 2, :].rearrange("p a (b c) -> p (a b) c", b=2)

        t_bank = ps[:, 4:6, :].rearrange("p a (b c) -> p (a b) c", b=4)

        def o_bank(n):
            return ps[:, 6 + n % 2, 0:256].rearrange("p (j e) -> p j e", j=4)

        @block.sync
        def _(sp):
            sp.dma_start(ident[:, :], k["ident"]).then_inc(sig["ident"], 16)
            for h in range(14):
                if h >= 2:
                    sp.wait_ge(sig["scored"], 2 * min(h - 1, 12))
                if h < 12:
                    sp.dma_start(bias[:, h % 2], k["att_bias"][:, h]).then_inc(sig[f"bias{h % 2}"], 16)
                if h % 4 == 1 and h > 1:
                    g = h // 4 - 1
                    sp.wait_ge(sig["o_out"], 8 * (g + 1))
                    sp.wait_ge(sig["exp"], 8 * (g + 1))
                    src = ob[:, g % 2].rearrange("p j h e -> p j (h e)")
                    dst = scratch[:, g, :]
                    if g == 0:
                        sp.dma_start(dst.rearrange("(j p) c -> p j c", p=P), src).then_inc(sig["stored0"], 16)
                    elif g == 1:
                        v = dst.rearrange("(b p z) c -> z b p c", b=2, z=4)
                        for j in range(NC):
                            sp.dma_start(v[j // 2, j % 2], src[:, j]).then_inc(sig["stored1"], 16)
                    else:
                        sp.dma_start(dst.rearrange("(p j) c -> p j c", j=NC), src).then_inc(sig["stored2"], 16)
            sp.wait_ge(sig["stored0"], 16)
            sp.wait_ge(sig["stored1"], 16 * NC)
            sp.wait_ge(sig["stored2"], 16)

        @block.tensor
        def _(pe):
            def scores(n):
                g, h, hf = units[n]
                row, tile = 64 * (h % 2), h // 2
                if n >= 2:
                    pe.wait_ge(sig["scored"], n - 1)
                b = s_bank(n)
                for i in range(4):
                    j = 4 * hf + i
                    q = tokens(g, qks[g], tile, row, j)
                    if before(g, j):
                        last = pe.matmul(b[:, i, :], q, tokens(g, qks[g], 2 + tile, row, j - 1, 2), start=True, stop=True)
                    else:
                        last = pe.matmul(b[:, i, P:2 * P], q, tokens(g, qks[g], 2 + tile, row, j), start=True, stop=True)
                last.then_inc(sig["s"], 1)

            pe.wait_ge(sig["ident"], 16)
            scores(0)
            for n, (g, h, hf) in enumerate(units):
                if n + 1 < N:
                    scores(n + 1)
                pe.wait_ge(sig["exp"], n + 1)
                if n:
                    pe.wait_ge(sig["t_out"], n)
                for i, b in blocks(g, hf):
                    last = pe.transpose(t_bank[:, 2 * i + b, :], sb[:, n % 2, i, b * P:b * P + P], ident[:, :])
                last.then_inc(sig["t"], 1)
                pe.wait_ge(sig["t_out"], n + 1)
                if n >= 2:
                    pe.wait_ge(sig["o_out"], n - 1)
                for i in range(4):
                    j = 4 * hf + i
                    have = [b for ii, b in blocks(g, hf) if ii == i]
                    for b in have:
                        last = pe.matmul(o_bank(n)[:, i, :], pt[:, n % 2, 2 * i + b, :],
                                         vs[g][:, j - 1 + b, 64 * h:64 * h + 64], start=(b == have[0]), stop=(b == 1))
                last.then_inc(sig["o"], 1)

        def tout(dve, n):
            g, h, hf = units[n]
            full, own = spans(g, hf)
            dve.wait_ge(sig["t"], n + 1)
            if n >= 2:
                dve.wait_ge(sig["o"], n - 1)
            tb = t_bank.rearrange("p (i b) c -> p i b c", b=2)
            pv = pt[:, n % 2].rearrange("p (i b) c -> p i b c", b=2)
            if full is not None:
                last = dve.tensor_copy(pv[:, full], tb[:, full])
                if own is not None:
                    last.then_inc(sig["t_part"], 1)
            if own is not None:
                last = dve.tensor_copy(pv[:, own, 1, :], tb[:, own, 1, :])
            last.then_inc(sig["t_out"], 1)

        @block.vector
        def _(dve):
            for n, (g, h, hf) in enumerate(units):
                head = 4 * g + h
                full, own = spans(g, hf)
                dve.wait_ge(sig[f"bias{head % 2}"], 16 * (head // 2 + 1))
                dve.wait_ge(sig["s"], n + 1)
                if n >= 2:
                    dve.wait_ge(sig["t"], n - 1)
                if own is not None and g < 2:
                    dve.memset(sb[:, n % 2, own, 0:P], NEG).then_inc(sig["filled"], 1)
                else:
                    dve.sem_inc(sig["filled"], 1)
                b = s_bank(n)
                bi = bias[:, head % 2].rearrange("p a b -> p (a b)")
                last = None
                for part, c0 in ((full, 0), (own, P)):
                    if part is None:
                        continue
                    if last is not None:
                        last.then_inc(sig["scored_part"], 1)
                    m = len(range(*part.indices(4)))
                    last = dve.scalar_tensor_tensor(out=sb[:, n % 2, part, c0:2 * P], in0=b[:, part, c0:2 * P],
                                                    scalar=0.125, in1=bc(bi[:, c0:2 * P], m), op0=ALU.mult, op1=ALU.add)
                last.then_inc(sig["scored"], 1)
                dve.wait_ge(sig["scored"], n + 1)
                dve.wait_ge(sig["filled"], n + 1)
                c0 = P if g == 2 else 0
                if g == 2 and h == 0 and hf == 0:
                    dve.wait_ge(sig["stored0"], 16)
                mx = ob[:, g % 2, 4 * hf:4 * hf + 4, h, 64]
                dve.tensor_reduce(mx, sb[:, n % 2, :, c0:2 * P], AX, ALU.max).then_inc(sig["max"], 1)
                dve.wait_ge(sig["max"], n + 1)
                dve.tensor_scalar(neg[:, n % 2, :], mx, -1.0, None, ALU.mult).then_inc(sig["neg"], 1)
                if n:
                    tout(dve, n - 1)
            tout(dve, N - 1)

        @block.scalar
        def _(act):
            def o_out(n):
                g, h, hf = units[n]
                act.wait_ge(sig["o"], n + 1)
                act.activation(ob[:, g % 2, 4 * hf:4 * hf + 4, h, 0:64], o_bank(n), ACT.Copy).then_inc(sig["o_out"], 1)

            for n, (g, h, hf) in enumerate(units):
                act.wait_ge(sig["neg"], n + 1)
                c0 = P if g == 2 else 0
                for i in range(4):
                    ins = act.activation(sb[:, n % 2, i, c0:2 * P], sb[:, n % 2, i, c0:2 * P], ACT.Exp,
                                         bias=neg[:, n % 2, i:i + 1], accum_out=ob[:, g % 2, 4 * hf + i, h, 65:66])
                    ins.then_inc(sig["exp" if i == 3 else "exp_part"], 1)
                if n:
                    o_out(n - 1)
            o_out(N - 1)


def attention_merge(nc, core, mem, scratch, ah, al, k):
    mb, w, r = mem("groups", [P, NC, 3, 4 * 66]), mem("weights", [P, 3, NC, 4]), mem("sums", [P, 3, NC, 4])
    acc, tmp, ident = mem("merged", [P, NC, 256]), mem("term", [P, NC, 256]), mem("ident", [P, P])
    ps = core.ps
    with ExitStack() as ctx:
        sig = ctx.enter_context(Signals(nc, "attm"))
        block = ctx.enter_context(nc.Block())
        grp = mb[:, :, :, :].rearrange("p j g (h e) -> p j g h e", e=66)

        @block.sync
        def _(sp):
            sp.dma_start(mb[:, :, :, :], scratch.rearrange("(j p) g c -> p j g c", p=P)).then_inc(sig["in"], 16)
            sp.dma_start(ident[:, :], k["ident"]).then_inc(sig["in"], 16)

        @block.vector
        def _(dve):
            count = [0]

            def link(ins):
                count[0] += 1
                ins.then_inc(sig["chain"], 1)
                dve.wait_ge(sig["chain"], count[0])

            dve.wait_ge(sig["in"], 32)
            m = [grp[:, :, g, :, 64] for g in range(3)]
            s = [grp[:, :, g, :, 65] for g in range(3)]
            top = r[:, 0]
            link(dve.tensor_tensor(top, m[0], m[1], ALU.max))
            link(dve.tensor_tensor(top, top, m[2], ALU.max))
            for g in range(3):
                ins = dve.tensor_tensor(w[:, g], m[g], top, ALU.subtract)
                if g < 2:
                    link(ins)
            ins.then_inc(sig["diff"], 1)
            dve.wait_ge(sig["e"], 1)
            link(dve.tensor_tensor(r[:, 0], w[:, 0], s[0], ALU.mult))
            for g in (1, 2):
                link(dve.tensor_tensor(r[:, 1], w[:, g], s[g], ALU.mult))
                link(dve.tensor_tensor(r[:, 0], r[:, 0], r[:, 1], ALU.add))
            link(dve.reciprocal(r[:, 2], r[:, 0]))
            for g in range(3):
                link(dve.tensor_tensor(w[:, g], w[:, g], r[:, 2], ALU.mult))
            v4 = lambda x: x.rearrange("p j (h e) -> p j h e", e=64)
            for g in range(3):
                for j in range(NC):
                    dst = (acc if g == 0 else tmp)[:, j, :].rearrange("p (h e) -> p h e", e=64)
                    ins = dve.tensor_tensor(dst, grp[:, j, g, :, 0:64], bcl(w[:, g, j, :], 64), ALU.mult)
                    link(ins)
                if g:
                    link(dve.tensor_tensor(acc[:, :, :], acc[:, :, :], tmp[:, :, :], ALU.add))
            dve.sem_inc(sig["merged"], 1)
            dve.wait_ge(sig["hi"], 1)
            for h in range(2):
                dve.tensor_tensor(al[:, h, :], ps[:, 2 * h:2 * h + 2, :].rearrange("p a b -> p (a b)"),
                                  ah[:, h, :].bitcast(F32), ALU.subtract)

        @block.scalar
        def _(act):
            act.wait_ge(sig["diff"], 1)
            act.activation(w[:, :, :, :], w[:, :, :, :], ACT.Exp).then_inc(sig["e"], 1)
            act.wait_ge(sig["t"], 1)
            act.activation(ah[:, :, :], ps[:, 0:4, :].rearrange("p (h a) b -> p h (a b)", h=2), ACT.Copy
                           ).then_inc(sig["hi"], 1)

        @block.tensor
        def _(pe):
            pe.wait_ge(sig["merged"], 1)
            for h in range(2):
                for j in range(NC):
                    last = pe.transpose(ps[:, 2 * h + j // 4, (j % 4) * P:(j % 4) * P + P], acc[:, j, h * P:h * P + P],
                                        ident[:, :])
            last.then_inc(sig["t"], 1)


def pool_phase(nc, core, mem, pz, bufs, ph, pl, a, k):
    wg, sc, fix = mem("w_grp", [PG, 8, 2 * PG]), mem("scale", [PG, 8]), mem("fix", [PG, 4, 16])
    with ExitStack() as ctx:
        sig = ctx.enter_context(Signals(nc, "pool"))
        block = ctx.enter_context(nc.Block())

        @block.sync
        def _(sp):
            sp.dma_start(wg[:, :, :], a["w_pool_grp_2"]).then_inc(sig["consts"], 16)
            sp.dma_start(sc[:, :], a["pool_scale_2"]).then_inc(sig["consts"], 16)
            sp.dma_start(fix[:, :, :], k["pool_fix"]).then_inc(sig["consts"], 16)

        @block.vector
        def _(dve):
            count = [0]

            def link(ins):
                count[0] += 1
                ins.then_inc(sig["chain"], 1)
                dve.wait_ge(sig["chain"], count[0])

            dve.wait_ge(sig["consts"], 48)
            for tile in range(8):
                win = POOL_WIN[tile // 2]
                src, d, b = pz[:, tile, :], 1, 0
                while d < win:
                    dst = bufs[b][0:PG, :]
                    link(dve.tensor_tensor(dst[:, d:T], src[:, d:T], src[:, 0:T - d], ALU.add))
                    link(dve.tensor_copy(dst[:, 0:d], src[:, 0:d]))
                    src, d, b = dst, 2 * d, 1 - b
                link(dve.tensor_scalar(src[:, 0:16], src[:, 0:16], 1.0, None, ALU.mult))
                link(dve.tensor_tensor(src[:, 0:16], src[:, 0:16], fix[:, tile // 2, :], ALU.mult))
                link(dve.scalar_tensor_tensor(out=pz[:, tile, :], in0=src, scalar=1.0 / win, in1=pz[:, tile, :],
                                              op0=ALU.mult, op1=ALU.subtract))
            dve.sem_inc(sig["pooled"], 1)
            for o in range(8):
                dve.wait_ge(sig["hi"], o + 1)
                dve.scalar_tensor_tensor(out=pl[0:PG, o, :], in0=core.slot(o % 2)[0:PG, :], scalar=sc[:, o:o + 1],
                                         in1=ph[0:PG, o, :].bitcast(F32), op0=ALU.mult, op1=ALU.subtract
                                         ).then_inc(sig["lo"], 1)

        @block.scalar
        def _(act):
            for o in range(8):
                act.wait_ge(sig["mixed"], o + 1)
                act.activation(ph[0:PG, o, :], core.slot(o % 2)[0:PG, :], ACT.Copy, scale=sc[:, o:o + 1]
                               ).then_inc(sig["hi"], 1)

        @block.tensor
        def _(pe):
            pe.wait_ge(sig["pooled"], 1)
            for o in range(8):
                g, half = o // 2, o % 2
                if o >= 2:
                    pe.wait_ge(sig["lo"], o - 1)
                for h in range(2):
                    for kk in range(2):
                        last = pe.matmul(core.ps[0:PG, 2 * (o % 2) + h, :], wg[:, 2 * g + kk, half * PG:half * PG + PG],
                                         pz[:, 2 * g + kk, 512 * h:512 * h + 512], start=(kk == 0), stop=(kk == 1))
                last.then_inc(sig["mixed"], 1)


def second_block(nc, core, a, k, residual, out, phase):
    xh, xl = x_parts(core)
    w = a["w_in_2"]
    qks = [nc.alloc_sbuf_tensor_at(f"qk{g}", [P, 4, T], F32, offset=OFF_S + 16 * KB * g) for g in range(3)]
    vs = [nc.alloc_sbuf_tensor_at(f"v{g}", [P, NC, 256], F32, offset=OFF_S + (48 + 8 * g) * KB) for g in range(3)]

    def order(g):
        def tokens(buf, kt, j):
            x = buf[:, kt, :]
            if g == 0:
                return x[:, j * P:j * P + P]
            if g == 1:
                return x.rearrange("p (l z) -> p z l", z=4)[:, j // 2, (j % 2) * P:(j % 2) * P + P]
            return x.rearrange("p (l z) -> p z l", z=8)[:, j, :]
        return tokens
    for g in range(3):
        project_phase(nc, core, f"qkv{g}",
                      [Run(2, lambda j, s, g=g: col_strip(w, g * 256 + s * P, j * (ATT_W // P)), xh, xl)],
                      [into(qks[g], 0)], w_tok=lambda s, g=g: col_strip(w, 2 * ATT_W + g * 256, s), zv=vs[g],
                      tokens=order(g))
    scratch = nc.dram_tensor("attention", (T, 3, 4 * 66), F32, kind="Internal").ap()
    attention_phase(nc, core, Space(nc, "att", (OFF_A, OFF_A + 32 * KB), (OFF_T + 8 * KB, END)), qks, vs, scratch, k)
    ah = nc.alloc_sbuf_tensor_at("a_hi", [P, 2, T], F32R, offset=OFF_S)
    al = nc.alloc_sbuf_tensor_at("a_lo", [P, 2, T], F32R, offset=OFF_S + 8 * KB)
    attention_merge(nc, core, Space(nc, "attm", (OFF_S + 16 * KB, END)), scratch, ah, al, k)
    pz = nc.alloc_sbuf_tensor_at("pool_z", [PG, 8, T], F32, offset=OFF_A)
    ph = nc.alloc_sbuf_tensor_at("pool_hi", [PG, 8, T], F32R, offset=OFF_S + 16 * KB)
    pl = nc.alloc_sbuf_tensor_at("pool_lo", [PG, 8, T], F32R, offset=OFF_S + 48 * KB)
    bufs = [nc.alloc_sbuf_tensor_at(f"pool_sum{i}", [PG, T], F32, offset=OFF_S + (44 + 32 * i) * KB) for i in range(2)]
    project_phase(nc, core, "pool_in",
                  [Run(4, lambda j, s: col_strip(w, 3 * ATT_W + s * PG, j * 2, width=PG), xh, xl, m=PG)],
                  [lambda act, j, s, psum: act.activation(at(pz, j * 2 + s), psum[0:PG, :], ACT.Copy)])
    pool_phase(nc, core, Space(nc, "pool", (OFF_S + 80 * KB, END)), pz, bufs, ph, pl, a, k)
    gate0 = 3 * ATT_W + 768
    gated_phase(nc, core, "merge2", Space(nc, "merge2", (OFF_S + 80 * KB, END)),
                [(w, gate0, a["w_att_out_2"], 256, P, lambda kt: ah[:, kt, :], lambda kt: al[:, kt, :]),
                 (w, gate0 + D, a["w_pool_out_2"], 768, PG, lambda kt: ph[:, kt, :], lambda kt: pl[:, kt, :])], True)
    if phase("merge2"):
        return
    mix_out_phase(nc, core, "out2", a["w_out_2"], residual=residual)
    norm_phase(nc, core, "rms_mlp", k["mean"], a["norm_mlp_g_2"], None, 1e-6, keep=None)
    if phase("rms_mlp"):
        return
    mlp_phase(nc, core, "mlp", a["w_mlp_in_2"], a["w_mlp_out_2"])
    norm_phase(nc, core, "rms_out", k["mean"], a["norm_final_g_2"], None, 1e-6, keep=None, out=out)


def constants():
    i = np.arange(P)
    f = np.float32
    k = {"ident": np.eye(P, dtype=f), "ones": np.ones((P, P), f), "mean": np.full((P, P), 1.0 / D, f)}
    heads = (i[:, None] // 64 == i[None, :] // 64).astype(f)
    k["heads"], k["head_mean"] = heads, heads / f(64)
    s, t = i[:, None], i[None, :]
    lv = [((s // (2 * L) == t // (2 * L)) & (s % (2 * L) < L) & (t % (2 * L) >= L)) for L in LEVELS] + [s == t]
    k["levels"] = np.stack(lv, 1).astype(np.int32)
    slopes = np.exp2(-8.0 * (np.arange(12) + 1.0) / 12.0)
    bias = np.full((P, 12, 2, P), NEG)
    for h in range(12):
        dil = DIL[h // 4]
        if h < 8:
            for b in range(2):
                dist = s - t + P * (1 - b)
                bias[:, h, b] = np.where((dist >= 0) & (dist <= P), -slopes[h] * dist * dil, NEG)
        else:
            dist = s // 2 - t // 2
            bias[:, h, 1] = np.where((dist >= 0) & (s % 2 == t % 2), -slopes[h] * dist * dil, NEG)
    k["att_bias"] = bias.astype(f)
    k["pool_fix"] = np.broadcast_to(np.stack([w / np.minimum(np.arange(16) + 1.0, w) for w in POOL_WIN]), (PG, 4, 16)).astype(f)
    b16 = s // 16 == t // 16

    def low(L):
        return (s // (2 * L) == t // (2 * L)) & (s % (2 * L) >= L) & (t % (2 * L) < L)
    k["rwkv_masks"] = np.stack([(s > t) & b16, low(16), low(32), low(64), (s < t) & b16, s < t, s <= t], 1).astype(f)
    sel = np.zeros((2, P, P), f)
    swap = np.zeros((P, P), f)
    for h in range(4):
        for e in range(32):
            sel[h // 2, 32 * h + e, 64 * (h % 2) + e] = 1
    for e in range(0, P, 2):
        swap[e + 1, e], swap[e, e + 1] = -1, 1
    sc = f(32.0 ** -0.5)
    k["gla_sel"] = np.stack([sel[0] * sc, sel[1] * sc, sel[0], sel[1]], 1)
    k["ret_sel"] = np.stack([m for u in range(2) for m in (sel[u], swap @ sel[u], sel[u] * sc, swap @ sel[u] * sc)], 1)
    theta = (1.0 / (f(10000.0) ** np.linspace(0.0, 1.0, 16, dtype=f))).astype(f)
    ang = (np.arange(T, dtype=f)[:, None] * theta[None, :]).astype(f)
    rot = np.zeros((P, 2, T), f)
    for p in range(P):
        if p % 64 < 32:
            rot[p, 0], rot[p, 1] = np.cos(ang[:, p % 64 // 2]), np.sin(ang[:, p % 64 // 2])
    k["rot"] = rot
    lg = np.log1p(-np.exp2(-5.0 - np.arange(4)))
    k["ret_decay"] = np.stack([np.where(s <= t, np.exp(lg[h] * np.maximum(t - s, 0)), 0) for h in range(4)], 1).astype(f)
    lgp = np.stack([lg[2 * u + i // 64] for u in range(2)], 1)
    k["ret_xz"] = np.stack([np.exp(lgp[:, u:u + 1] * e) for u in range(2) for e in (t + 1.0, P - 1.0 - t)], 1).astype(f)
    k["ret_end"] = np.exp(lgp * P).astype(f)
    return k


def into(z, z0, func=ACT.Copy, rows=P):
    def out(act, j, s, psum):
        return act.activation(at(z, j * 2 + (z0 + s)), psum, func)
    return out


def program(nc, a, out, upto=None):
    core = Core(nc)
    k = {n[2:]: v for n, v in a.items() if n.startswith("k_")}
    xh, xl = x_parts(core)
    w = a["w_in"]

    def phase(name):
        return upto is not None and name == upto

    norm_phase(nc, core, "ln_in", k["mean"], a["ln_in_w"], a["ln_in_b"], 1e-5, x_in=a["x"], keep=None)
    yh = nc.alloc_sbuf_tensor_at("y_hi", [P, KT, T], F32R, offset=OFF_S)
    yl = nc.alloc_sbuf_tensor_at("y_lo", [P, KT, T], F32R, offset=OFF_S + 32 * KB)
    y_free = lambda lo, hi: [(OFF_S + 4 * KB * lo, OFF_S + 4 * KB * hi), (OFF_S + (32 + 4 * lo) * KB, OFF_S + (32 + 4 * hi) * KB)]

    z = nc.alloc_sbuf_tensor_at("rwkv_z", [P, 8, T], F32, offset=OFF_A)
    mem = Space(nc, "rwkv", (OFF_S, OFF_S + 8 * KB), (OFF_S + 16 * KB, OFF_S + 40 * KB), (OFF_S + 48 * KB, END))
    mu, om = (nc.alloc_sbuf_tensor_at(n, [P, 8], F32, offset=OFF_T + 32 * i) for i, n in enumerate(("mu", "one_mu")))

    def mu_load(sp, sig):
        sp.dma_start(mu[:, :], a["rwkv_mu"]).then_inc(sig["mu"], 16)

    def mu_prepare(dve, sig):
        dve.wait_ge(sig["mu"], 16)
        return dve.tensor_scalar(om[:, :], mu[:, :], -1.0, 1.0, ALU.mult, ALU.add)

    def shifted(dve, r, j, s, psum):
        dst = at(z, j * 2 + s)[:, 1:T]
        return dve.scalar_tensor_tensor(out=dst, in0=psum[:, 0:T - 1], scalar=colat(mu, j * 2 + s), in1=dst,
                                        op0=ALU.mult, op1=ALU.add)
    project_phase(nc, core, "rwkv_in", [Run(4, lambda j, s: col_strip(w, RWKV0 + s * P, j * 2), xh, xl)],
                  [lambda act, j, s, psum: act.activation(at(z, j * 2 + s), psum, ACT.Copy, scale=colat(om, j * 2 + s))],
                  consts=(mu_load, mu_prepare), last_vector=shifted)
    rwkv_mixer(nc, core, mem, z, yh, yl, 2,
               dict(k, w2=a["rwkv_w2"], a2=a["rwkv_a2"], g2=a["rwkv_g2"], params=a["rwkv_params"]))
    if phase("rwkv"):
        return

    z = nc.alloc_sbuf_tensor_at("hgrn_z", [P, 6, T], F32, offset=OFF_A)
    zv = nc.alloc_sbuf_tensor_at("hgrn_v", [P, NC, 256], F32, offset=OFF_A + 24 * KB)
    project_phase(nc, core, "hgrn_in",
                  [Run(2, lambda j, s: col_strip(w, HGRN0 + s * P, j * 2), xh, xl),
                   Run(1, lambda j, s: col_strip(w, HGRN0 + 768, s), xh, xl)],
                  [into(z, 0), into(z, 4, ACT.Silu)], w_tok=lambda s: col_strip(w, HGRN0 + 512, s), zv=zv)
    linear_mixer(nc, core, "hgrn", "hgrn", Space(nc, "hgrn", (OFF_T, END), *y_free(0, 2), *y_free(4, 6)),
                 z, zv, yh, yl, 6, k)
    if phase("hgrn"):
        return
    z = nc.alloc_sbuf_tensor_at("gla_z", [P, 6, T], F32, offset=OFF_A)
    zv = nc.alloc_sbuf_tensor_at("gla_v", [P, NC, 256], F32, offset=OFF_A + 24 * KB)
    project_phase(nc, core, "gla_in",
                  [Run(1, lambda j, s: col_strip(w, GLA0, s), xh, xl),
                   Run(1, lambda j, s: col_strip(w, GLA0 + 512, 0), xh, xl),
                   Run(1, lambda j, s: col_strip(w, GLA0 + 528, s), xh, xl)],
                  [into(z, 0), lambda act, j, s, psum: act.activation(z[:, 2 + 3 * s, :], psum, ACT.Copy),
                   into(z, 3, ACT.Silu)],
                  w_tok=lambda s: col_strip(w, GLA0 + 256, s), zv=zv)
    linear_mixer(nc, core, "gla", "gla", Space(nc, "gla", (OFF_T, END), *y_free(0, 2)), z, zv, yh, yl, 4,
                 dict(k, gla_w2=a["gla_w2"], gla_b=a["gla_b"]))
    if phase("gla"):
        return
    z = nc.alloc_sbuf_tensor_at("ret_z", [P, 4, T], F32, offset=OFF_A)
    zv = nc.alloc_sbuf_tensor_at("ret_v", [P, NC, 256], F32, offset=OFF_A + 16 * KB)
    project_phase(nc, core, "ret_in",
                  [Run(1, lambda j, s: col_strip(w, RET0, s), xh, xl),
                   Run(1, lambda j, s: col_strip(w, RET0 + 512, s), xh, xl)],
                  [into(z, 0), into(z, 2, ACT.Silu)], w_tok=lambda s: col_strip(w, RET0 + 256, s), zv=zv)
    linear_mixer(nc, core, "ret", "ret", Space(nc, "ret", (OFF_T, END), (OFF_A + 24 * KB, OFF_A + 32 * KB)),
                 z, zv, yh, yl, 0, k)
    if phase("ret"):
        return
    ytile = lambda buf, n: (lambda k: buf[:, 2 * n + k, :])
    gated_phase(nc, core, "merge", Space(nc, "merge", (OFF_T, END)),
                [(w, GATE0 + n * D, a["w_branch"][n], 256, P, ytile(yh, n), ytile(yl, n)) for n in range(4)], True)
    if phase("merge"):
        return
    mix_out_phase(nc, core, "mix_out", a["w_mix_out"])
    norm_phase(nc, core, "ln_mix", k["mean"], a["ln_mix_w"], a["ln_mix_b"], 1e-5)
    if phase("ln_mix"):
        return
    gated_phase(nc, core, "ple", Space(nc, "ple", (OFF_S, END)),
                [(a["w_ple_gate"], 0, a["w_ple_proj"], 256, P, None, None)], False, p_in=a["p"])
    ffn_phase(nc, core, "ffn", a["w_ffn_up"], a["ffn_conv"], a["w_ffn_down"])
    norm_phase(nc, core, "ln_ffn", k["mean"], a["ln_ffn_w"], a["ln_ffn_b"], 1e-5, keep=1.0, split=False)
    if phase("ln_ffn"):
        return
    residual = nc.dram_tensor("residual", (D, T), F32, kind="Internal").ap()
    norm_phase(nc, core, "rms_mix", k["mean"], a["norm_mix_g_2"], None, 1e-6, keep=None, spill=residual)
    if phase("rms_mix"):
        return
    second_block(nc, core, a, k, residual, out, phase)



def tiles_of(v, m=P):
    return np.ascontiguousarray(v.reshape(-1, m).T)


def layout(i):
    c = np.ascontiguousarray
    a = {"x": c(i["x"][0].T), "w_in": i["w_in"][0]}
    for n in ("ln_in_w", "ln_in_b", "norm_final_g_2"):
        a[n] = tiles_of(i[n])
    for n in ("ln_mix_w", "ln_mix_b", "ln_ffn_w", "ln_ffn_b", "norm_mix_g_2", "norm_mlp_g_2"):
        a[n] = tiles_of(i[n][0])
    for n in ("w_branch", "w_mix_out", "w_ffn_up", "w_ffn_down", "w_ple_gate", "w_ple_proj", "w_in_2", "w_att_out_2",
              "w_pool_out_2", "w_out_2", "w_mlp_in_2", "w_mlp_out_2"):
        a[n] = i[n][0]
    a["p"] = c(i["p"][0, 0].T)
    a["ffn_conv"] = c(i["ffn_conv"][0].reshape(3, FF // P, P).transpose(2, 0, 1))
    a["w_pool_grp_2"] = c(i["w_pool_grp_2"][0].reshape(8, PG, 2 * PG).transpose(1, 0, 2))
    a["pool_scale_2"] = tiles_of(i["pool_scale_2"][0], PG)
    for n in ("w2", "a2", "g2"):
        a["rwkv_" + n] = i["rwkv_" + n][0]
    a["rwkv_mu"] = tiles_of(i["rwkv_mu"][0])
    names = ("w0", "a0", "k_k", "k_a", "r_k", "ln_w", "ln_b")
    a["rwkv_params"] = c(np.stack([tiles_of(i["rwkv_" + n][0].reshape(-1)) for n in names], 2))
    a["gla_w2"], a["gla_b"] = i["gla_w2"][0], c(i["gla_b"][0].reshape(-1, 1))
    for n in ("gla", "hgrn"):
        g = i[n + "_norm_w"][0]
        a["k_" + n + "_gain"] = c(np.stack([np.concatenate([g, g])] * 2, 1))
    a.update({"k_" + n: v for n, v in constants().items()})
    return a


def kernel(**inputs):
    import concourse.bacc as bacc
    from concourse.bass_utils import run_bass_kernel_spmd

    arrays = {n: np.ascontiguousarray(v) for n, v in layout({n: np.asarray(v) for n, v in inputs.items()}).items()}
    nc = bacc.Bacc("TRN2", target_bir_lowering=False, num_devices=1)
    a = {n: nc.dram_tensor("in_" + n, v.shape, mybir.dt.from_np(v.dtype), kind="ExternalInput").ap()
         for n, v in arrays.items()}
    out = nc.dram_tensor("out", (D, T), F32, kind="ExternalOutput").ap()
    program(nc, a, out, upto=UPTO)
    r = run_bass_kernel_spmd(nc, [{"in_" + n: v for n, v in arrays.items()}], core_ids=[0])
    return r.results[0]["out"].T.reshape(1, T, D)
UPTO = None
```

```python
from contextlib import ExitStack

import concourse.bass as bass
import numpy as np
from concourse import mybir

F32 = mybir.dt.float32
F32R = mybir.dt.float32r
I32 = mybir.dt.int32
ACT = mybir.ActivationFunctionType
ALU = mybir.AluOpType
AX = mybir.AxisListType.X

P = 128
T = 1024
D = 1024
KT = D // P
C = 128
NC = T // C
ALPHA = 2.0 ** 0.25
RWKV_DECAY = 0.6065306597126334
FF = 2816
FF2 = 4096
NEG = -1e30
RET0, RWKV0, GLA0, HGRN0, GATE0 = 0, 768, 1792, 2576, 3600
ATT_W = 768
DIL = (1, 4, 16)
POOL_WIN = (2, 4, 8, 16)
PG = 96

BASE = 16512
KB = 1024
OFF_XH, OFF_XL, OFF_A, OFF_WR, OFF_WH, OFF_WL, OFF_S = (
    BASE, BASE + 32 * KB, BASE + 64 * KB, BASE + 96 * KB, BASE + 104 * KB, BASE + 112 * KB, BASE + 120 * KB)
OFF_T = OFF_S + 64 * KB
OFF_LOW = 2 * KB
OFF_TAIL = OFF_LOW + 8 * KB
END = 229344


class Space:

    def __init__(self, nc, name, *stretches):
        self.nc, self.name, self.free = nc, name, [list(s) for s in stretches]

    def __call__(self, name, shape, dtype=F32):
        size = int(np.prod(shape[1:])) * 4
        size = (size + 31) // 32 * 32
        for s in self.free:
            if s[1] - s[0] >= size:
                at = s[0]
                s[0] += size
                return self.nc.alloc_sbuf_tensor_at(f"{self.name}_{name}", list(shape), dtype, offset=at)
        raise ValueError(f"no room for {self.name}_{name}: {size} in {self.free}")


class Signals(ExitStack):

    def __init__(self, nc, phase):
        super().__init__()
        self.nc, self.phase, self.made = nc, phase, {}

    def __getitem__(self, name):
        if name not in self.made:
            self.made[name] = self.nc.alloc_semaphore(f"{self.phase}_{name}")
        return self.made[name]

    def __exit__(self, *details):
        self.nc.clear_and_free_semaphores(list(self.made.values()))
        self.nc.all_engine_barrier()
        return super().__exit__(*details)


def bc(ap, n):
    return ap.unsqueeze(1).to_broadcast([ap.shape[0], n, ap.shape[1]])


def bcl(ap, n):
    return ap.unsqueeze(2).to_broadcast([ap.shape[0], ap.shape[1], n])


class Core:

    def __init__(self, nc):
        self.nc = nc
        at = nc.alloc_sbuf_tensor_at
        self.xh = at("x_hi", [P, KT, T], F32R, offset=OFF_XH)
        self.xl = at("x_lo", [P, KT, T], F32R, offset=OFF_XL)
        self.a = at("acc", [P, KT, T], F32, offset=OFF_A)
        self.wr = at("w_raw", [P, 2, KT, P], F32, offset=OFF_WR)
        self.wh = at("w_hi", [P, 2, KT, P], F32R, offset=OFF_WH)
        self.wl = at("w_lo", [P, 2, KT, P], F32R, offset=OFF_WL)
        self.gate = at("gate", [P, 2, T], F32, offset=OFF_LOW)
        self.stat, self.square = self.gate[:, 0, :], self.gate[:, 1, :]
        self.ps = nc.alloc_psum_tensor("psum", [P, 8, 512], F32)

    def slot(self, s):
        return self.ps[:, 2 * s:2 * s + 2, :].rearrange("p a b -> p (a b)")


class Run:

    def __init__(self, n, src, hi, lo, nk=(KT, KT), rows=P, m=P,
                 each=None, second=None):
        self.second = second
        self.n, self.src, self.nk, self.m, self.each = n, src, nk, m, each
        self.rows = rows if isinstance(rows, tuple) else (rows, rows)
        self.hi = hi if isinstance(hi, tuple) else (hi, hi)
        self.lo = lo if isinstance(lo, tuple) else (lo, lo)


class Strips:

    def __init__(self, core, sig, runs, fetched=False, ahead=None):
        self.c, self.sig, self.runs, self.fetched, self.ahead = core, sig, runs, fetched, ahead
        self.turns = [sum(r.n for r in runs[:i]) for i in range(len(runs) + 1)]

    def load(self, sp):
        for run, base in zip(self.runs, self.turns):
            def turn(j, g, warm, run=run):
                if self.fetched and isinstance(g, int) and g == 0:
                    for s in range(2):
                        sp.sem_inc(self.sig[f"w_raw{s}"], 16)
                    return
                if warm:
                    sp.wait_ge(self.sig["w_lo0"], g)
                    sp.wait_ge(self.sig["w_lo1"], g)
                for s in range(2):
                    sp.dma_start(self.c.wr[0:run.rows[s], s, 0:run.nk[s], 0:run.m], run.src(j, s)
                                 ).then_inc(self.sig[f"w_raw{s}"], 16)
            self._turns(sp, run.n, base, turn, peel=(base == 0))
        if self.ahead:
            done, run = self.turns[-1], self.ahead
            for s in range(2):
                if done:
                    sp.wait_ge(self.sig[f"w_lo{s}"], done)
                sp.dma_start(self.c.wr[0:run.rows[s], s, 0:run.nk[s], 0:run.m], run.src(0, s)
                             ).then_inc(self.sig[f"w_raw{s}"], 16)
            sp.wait_ge(self.sig["w_raw1"], 16 * (done + 1))

    def split_ahead(self, act=None, pool=None):
        if act:
            self.split_hi(act, 0, 0, self.ahead, warm=False)
        if pool:
            self.split_lo(pool, 0, 0, self.ahead)

    def _turns(self, eng, n, base, turn, peel=False, last=None):
        first = 1 if peel else 0
        stop = n - 1 if last is not None else n
        if peel and stop > 0:
            turn(0, base, False)
        if stop > first:
            with eng.Fori(first, stop) as j:
                turn(j, j + base, True)
        if last is not None:
            last(n - 1, base + n - 1)

    def split_hi(self, act, g, s, run, warm=True):
        act.wait_ge(self.sig[f"w_raw{s}"], g * 16 + 16)
        if warm:
            act.wait_ge(self.sig[f"mm{s}"], g)
        act.activation(self.c.wh[0:run.rows[s], s, 0:run.nk[s], 0:run.m],
                       self.c.wr[0:run.rows[s], s, 0:run.nk[s], 0:run.m], ACT.Copy).then_inc(self.sig[f"w_hi{s}"], 1)

    def split_lo(self, pool, g, s, run):
        pool.wait_ge(self.sig[f"w_hi{s}"], g + 1)
        pool.tensor_tensor(self.c.wl[0:run.rows[s], s, 0:run.nk[s], 0:run.m],
                           self.c.wr[0:run.rows[s], s, 0:run.nk[s], 0:run.m],
                           self.c.wh[0:run.rows[s], s, 0:run.nk[s], 0:run.m].bitcast(F32), ALU.subtract
                           ).then_inc(self.sig[f"w_lo{s}"], 1)

    def follow(self, eng, split, out, before=None, ahead=True, out_first=False):
        def first():
            if split:
                for s in range(2):
                    split(eng, 0, s, self.runs[0], False)
        if before:
            before(first)
        else:
            first()
        for r, (run, base) in enumerate(zip(self.runs, self.turns)):
            after = self.runs[r + 1] if r + 1 < len(self.runs) else None
            ahead_of = self.ahead if r + 1 == len(self.runs) and ahead else None

            def turn(j, g, warm, run=run, r=r):
                for s in range(2):
                    if out and out_first:
                        out(r, j, g, s)
                    if split:
                        split(eng, g + 1, s, run, True)
                    if out and not out_first:
                        out(r, j, g, s)

            def last(j, g, run=run, r=r, after=after, ahead_of=ahead_of):
                for s in range(2):
                    if out and out_first:
                        out(r, j, g, s)
                    if split and after is not None:
                        split(eng, g + 1, s, after, True)
                    if split and ahead_of is not None and s == 0:
                        split(eng, g + 1, s, ahead_of, True)
                    if out and not out_first:
                        out(r, j, g, s)
            self._turns(eng, run.n, base, turn, last=last)

    def hi_split(self, act, g, s, run, warm):
        if self.fetched and not warm and s == 0:
            act.sem_inc(self.sig["w_hi0"], 1)
            return
        self.split_hi(act, g, s, run, warm)

    def lo_split(self, pool, g, s, run, warm):
        if self.fetched and not warm and s == 0:
            pool.sem_inc(self.sig["w_lo0"], 1)
            return
        self.split_lo(pool, g, s, run)

    def products(self, pe):
        wh, wl = self.c.wh, self.c.wl
        for run, base in zip(self.runs, self.turns):

            def turn(j, g, warm, run=run):
                for s in range(2):
                    pe.wait_ge(self.sig[f"w_lo{s}"], g + 1)
                    if not (isinstance(g, int) and g == 0):
                        pe.wait_ge(self.sig[f"out{s}"], g)
                    nk = run.nk[s]
                    if run.second is not None and isinstance(j, int) and j == 0 and s == 1:
                        pe.wait_ge(*run.second)
                    for k in range(nk):
                        if run.each is not None and isinstance(j, int) and j == 0 and s == 0:
                            pe.wait_ge(*run.each(k))
                        for n, (w, x) in enumerate(((wh, run.hi[s]), (wh, run.lo[s]), (wl, run.hi[s]))):
                            for h in range(2):
                                last = pe.matmul(self.c.ps[0:run.m, 2 * s + h, :], w[0:run.rows[s], s, k, 0:run.m],
                                                 x(k)[:, 512 * h:512 * h + 512],
                                                 start=(k == 0 and n == 0), stop=(k == nk - 1 and n == 2))
                    last.then_inc(self.sig[f"mm{s}"], 1)
            self._turns(pe, run.n, base, turn, peel=(base == 0 or run.each is not None))


def col_strip(w, first, i, rows=D, row0=0, part=P, width=P):
    v = w[row0:row0 + rows, :].rearrange("(k p) n -> p k n", p=part)
    if isinstance(i, int):
        return v[:, :, first + i * width:first + i * width + width]
    return v[:, :, bass.ds(i * width + first, width)]


def flat(ap):
    return ap.rearrange("p a b -> p (a b)")


def at(buf, i):
    if isinstance(i, int):
        return buf[:, i, :]
    return flat(buf[:, bass.ds(i, 1), :])


def colat(buf, i):
    return buf[:, i:i + 1] if isinstance(i, int) else buf[:, bass.ds(i, 1)]


class Norm:

    def __init__(self, core, sig, mem, ones, w, b, eps, x_in=None, keep=True, out=None, spill=None, split=True,
                 sum_squares=False):
        self.sum_squares = sum_squares
        self.core, self.sig, self.ones, self.w, self.b, self.eps_value = core, sig, ones, w, b, eps
        self.x_in, self.keep, self.out, self.spill, self.split = x_in, keep, out, spill, split and out is None
        self.centre = b is not None
        self.one, self.wc, self.bcol = mem("ones", [P, P]), mem("w", [P, KT]), mem("b", [P, KT])
        self.sq = mem("sq", [P, KT, T]) if self.centre else None
        self.sd, self.epst = mem("sd", [P, T]), mem("eps", [P, 1])
        self.rstd, self.y = mem("rstd", [P, T]), None if keep else mem("y", [P, 2, T])
        self.nconst = 48 if self.centre else 32

    def dst(self, k):
        return self.core.a[:, k, :] if self.keep else self.y[:, k % 2, :]

    def lo(self, k):
        return self.sig[f"x_lo{k % 2}"], k // 2 + 1

    def sync(self, sp):
        sig, a = self.sig, self.core.a
        if self.x_in is not None:
            for k in range(KT):
                sp.dma_start(a[:, k, :], self.x_in[k * P:k * P + P, :]).then_inc(sig[f"x{k}"], 16)
        sp.dma_start(self.one[:, :], self.ones).then_inc(sig["norm_consts"], 16)
        sp.dma_start(self.wc[:, :], self.w).then_inc(sig["norm_consts"], 16)
        if self.centre:
            sp.dma_start(self.bcol[:, :], self.b).then_inc(sig["norm_consts"], 16)

    def sync_end(self, sp):
        sig = self.sig
        if self.spill is not None:
            sp.dma_start(self.spill.rearrange("(k p) t -> p k t", p=P), self.core.a[:, :, :]).then_inc(sig["spilled"], 16)
            sp.wait_ge(sig["spilled"], 16)
        if self.out is not None:
            for k in range(KT):
                sp.wait_ge(sig["affine"], k + 1)
                sp.dma_start(self.out[k * P:k * P + P, :], self.dst(k)).then_inc(sig[f"stored{k}"], 16)
            for k in range(KT):
                sp.wait_ge(sig[f"stored{k}"], 16)

    def tensor(self, pe):
        sig, ps, a, one = self.sig, self.core.ps, self.core.a, self.one
        pe.wait_ge(sig["norm_consts"], self.nconst)
        if self.centre:
            if self.x_in is not None:
                pe.wait_ge(sig["tiles_added"], KT - 1)
            for h in range(2):
                last = pe.matmul(ps[:, h, :], one[:, :], self.core.stat[:, 512 * h:512 * h + 512],
                                 start=True, stop=True)
            last.then_inc(sig["mean"], 1)
        if not self.centre:
            for h in range(2):
                last = pe.matmul(ps[:, 2 + h, :], one[:, :], self.core.stat[:, 512 * h:512 * h + 512],
                                 start=True, stop=True)
            last.then_inc(sig["sq_summed"], 1)
            return
        for k in range(KT // 2 + 1):
            if k < KT // 2:
                pe.wait_ge(sig["sq"], k + 1)
                x = self.sq[:, k, :]
            else:
                pe.wait_ge(sig["sq_added"], KT // 2 - 1)
                x = self.core.stat
            for h in range(2):
                last = pe.matmul(ps[:, 2 + h, :], one[:, :], x[:, 512 * h:512 * h + 512],
                                 start=(k == 0), stop=(k == KT // 2))
        last.then_inc(sig["sq_summed"], 1)

    def scalar(self, act, first):
        sig, core = self.sig, self.core
        for k in range(KT if self.centre else 0):
            act.wait_ge(sig["centred"], k + 1)
            act.activation(self.sq[:, k, :], core.a[:, k, :], ACT.Square).then_inc(sig["sq"], 1)
        act.wait_ge(sig["norm_eps"], 1)
        act.wait_ge(sig["sq_summed"], 1)
        act.activation(self.sd[:, :], core.slot(1), ACT.Sqrt, bias=self.epst[:, 0:1]).then_inc(sig["sd"], 1)
        first()
        act.wait_ge(sig["norm_consts"], self.nconst)
        for k in range(KT):
            dst = self.dst(k)
            if self.centre:
                act.wait_ge(sig["scaled"], k + 1)
                act.activation(dst, dst, ACT.Identity, bias=self.bcol[:, k:k + 1], scale=self.wc[:, k:k + 1]
                               ).then_inc(sig["affine"], 1)
            if self.sum_squares:
                act.wait_ge(sig["affine"], k + 1)
                act.activation(self.sq[:, k, :], dst, ACT.Square).then_inc(sig["tile_squared"], 1)
            if self.split:
                act.wait_ge(sig["affine"], k + 1)
                act.activation(core.xh[:, k, :], dst, ACT.Copy).then_inc(sig["x_hi"], 1)

    def lo_part(self, eng, k):
        eng.wait_ge(self.sig["x_hi"], k + 1)
        eng.tensor_tensor(self.core.xl[:, k, :], self.dst(k), self.core.xh[:, k, :].bitcast(F32), ALU.subtract
                          ).then_inc(self.lo(k)[0], 1)

    def vector(self, dve):
        sig, core, a = self.sig, self.core, self.core.a
        dve.memset(self.epst[:, :], self.eps_value).then_inc(sig["norm_eps"], 1)
        stat = core.stat

        def add_up(tile, n, arrived, added):
            dve.wait_ge(*arrived(0))
            for k in range(1, n):
                dve.wait_ge(*arrived(k))
                if k > 1:
                    dve.wait_ge(sig[added], k - 1)
                dve.tensor_tensor(stat, tile(0) if k == 1 else stat, tile(k), ALU.add).then_inc(sig[added], 1)

        if self.x_in is not None:
            add_up(lambda k: a[:, k, :], KT, lambda k: (sig[f"x{k}"], 16), "tiles_added")
        if self.centre:
            dve.wait_ge(sig["mean"], 1)
            for k in range(KT):
                dve.tensor_tensor(a[:, k, :], a[:, k, :], core.slot(0), ALU.subtract).then_inc(sig["centred"], 1)
            half = KT // 2
            add_up(lambda k: self.sq[:, half + k, :], half, lambda k: (sig["sq"], half + k + 1), "sq_added")
        dve.wait_ge(sig["sd"], 1)
        dve.reciprocal(self.rstd[:, :], self.sd[:, :]).then_inc(sig["rstd"], 1)
        dve.wait_ge(sig["rstd"], 1)
        if not self.centre:
            dve.wait_ge(sig["norm_consts"], self.nconst)
        for k in range(KT):
            if self.centre:
                dve.wait_ge(sig["centred"], k + 1)
            if not self.keep and k >= 2:
                if self.out is None:
                    dve.wait_ge(*self.lo(k - 2))
                else:
                    dve.wait_ge(sig[f"stored{k - 2}"], 16)
            if self.centre:
                dve.tensor_tensor(self.dst(k), a[:, k, :], self.rstd[:, :], ALU.mult).then_inc(sig["scaled"], 1)
            else:
                dve.scalar_tensor_tensor(out=self.dst(k), in0=a[:, k, :], scalar=self.wc[:, k:k + 1],
                                         in1=self.rstd[:, :], op0=ALU.mult, op1=ALU.mult).then_inc(sig["affine"], 1)
            if self.split and k % 2 == 1:
                self.lo_part(dve, k - 1)

    def gpsimd(self, pool, first):
        first()
        if self.sum_squares:
            sig, stat = self.sig, self.core.stat
            pool.wait_ge(sig["sq_summed"], 1)
            pool.memset(stat, 0.0).then_inc(sig["tile_summed"], 1)
            for k in range(KT):
                pool.wait_ge(sig["tile_squared"], k + 1)
                pool.wait_ge(sig["tile_summed"], k + 1)
                pool.tensor_tensor(stat, stat, self.sq[:, k, :], ALU.add).then_inc(sig["tile_summed"], 1)
        if self.split:
            for k in range(1, KT, 2):
                self.lo_part(pool, k)


class TileSums:

    def __init__(self, core, sig, squares):
        self.core, self.sig, self.squares = core, sig, squares

    def start(self, pool):
        pool.memset(self.core.stat, 0.0).then_inc(self.sig["tile_summed"], 1)

    def scalar(self, act, j, g, s):
        if self.squares:
            act.wait_ge(self.sig[f"out{s}"], g + 1)
            act.wait_ge(self.sig["tile_summed"], j * 2 + (s + 1))
            act.activation(self.core.square, at(self.core.a, j * 2 + s), ACT.Square).then_inc(self.sig["tile_squared"], 1)

    def gpsimd(self, pool, j, g, s):
        if self.squares:
            pool.wait_ge(self.sig["tile_squared"], j * 2 + (s + 1))
            x = self.core.square
        else:
            pool.wait_ge(self.sig[f"out{s}"], g + 1)
            x = at(self.core.a, j * 2 + s)
        pool.wait_ge(self.sig["tile_summed"], j * 2 + (s + 1))
        pool.tensor_tensor(self.core.stat, self.core.stat, x, ALU.add).then_inc(self.sig["tile_summed"], 1)


def norm_phase(nc, core, name, *args, **more):
    with ExitStack() as ctx:
        sig = ctx.enter_context(Signals(nc, name))
        norm = Norm(core, sig, Space(nc, name, (OFF_S, END)), *args, **more)
        block = ctx.enter_context(nc.Block())

        @block.sync
        def _(sp):
            norm.sync(sp)
            norm.sync_end(sp)

        @block.tensor
        def _(pe):
            norm.tensor(pe)

        @block.scalar
        def _(act):
            norm.scalar(act, lambda: None)

        @block.vector
        def _(dve):
            norm.vector(dve)

        @block.gpsimd
        def _(pool):
            norm.gpsimd(pool, lambda: None)


def x_parts(core):
    return (lambda k: core.xh[:, k, :]), (lambda k: core.xl[:, k, :])


def mix_out_run(w):
    return Run(KT // 2, lambda j, s: col_strip(w, s * P, j * 2), None, None)


def mix_out_phase(nc, core, name, w, residual=None):
    mem = Space(nc, name, (OFF_S, END))
    mh, ml = mem("m_hi", [P, KT, T], F32R), mem("m_lo", [P, KT, T], F32R)
    a = core.a
    with ExitStack() as ctx:
        sig = ctx.enter_context(Signals(nc, name))
        st = Strips(core, sig, [Run(KT // 2, lambda j, s: col_strip(w, s * P, j * 2), lambda k: mh[:, k, :],
                                    lambda k: ml[:, k, :], each=lambda k: (sig["m_lo"], k + 1))], fetched=True)
        sums = TileSums(core, sig, residual is not None)
        block = ctx.enter_context(nc.Block())

        @block.sync
        def _(sp):
            st.load(sp)

        @block.scalar
        def _(act):
            act.activation(mh[:, 0, :], a[:, 0, :], ACT.Copy).then_inc(sig["m_hi"], 1)

            def before(first):
                first()
                for k in range(1, KT):
                    act.activation(mh[:, k, :], a[:, k, :], ACT.Copy).then_inc(sig["m_hi"], 1)
                if residual is not None:
                    act.wait_ge(sig["m_lo"], KT)
                    act.dma_start(a[:, :, :], residual.rearrange("(k p) t -> p k t", p=P)).then_inc(sig["residual"], 16)
            st.follow(act, st.hi_split, lambda r, j, g, s: sums.scalar(act, j, g, s), before)

        @block.gpsimd
        def _(pool):
            sums.start(pool)
            st.follow(pool, st.lo_split, lambda r, j, g, s: sums.gpsimd(pool, j, g, s))

        @block.tensor
        def _(pe):
            st.products(pe)

        @block.vector
        def _(dve):
            for k in range(KT):
                dve.wait_ge(sig["m_hi"], k + 1)
                dve.tensor_tensor(ml[:, k, :], a[:, k, :], mh[:, k, :].bitcast(F32), ALU.subtract
                                  ).then_inc(sig["m_lo"], 1)
            if residual is None:
                for k in range(KT):
                    dve.wait_ge(sig["m_lo"], k + 1)
                    dve.tensor_scalar(a[:, k, :], core.xl[:, k, :].bitcast(F32), ALPHA, None, ALU.mult
                                      ).then_inc(sig["x_lo"], 1)
                    dve.wait_ge(sig["x_lo"], k + 1)
                    dve.scalar_tensor_tensor(out=a[:, k, :], in0=core.xh[:, k, :].bitcast(F32), scalar=ALPHA,
                                             in1=a[:, k, :], op0=ALU.mult, op1=ALU.add).then_inc(sig["x"], 1)
                dve.wait_ge(sig["x"], KT)
            else:
                dve.wait_ge(sig["residual"], 16)

            def out(r, j, g, s):
                dve.wait_ge(sig[f"mm{s}"], g + 1)
                dst = at(a, j * 2 + s)
                dve.tensor_tensor(dst, dst, core.slot(s), ALU.add).then_inc(sig[f"out{s}"], 1)
            st.follow(dve, None, out)


def ple_phase(nc, core, name, p_in, w_gate, w_proj, norm_args, ahead):
    mem = Space(nc, name, (OFF_S, END))
    gate, raw, ph, pl = mem("gate", [P, T]), mem("p", [P, 2, T]), mem("p_hi", [P, 2, T], F32R), mem("p_lo", [P, 2, T], F32R)
    xh, xl = x_parts(core)
    with ExitStack() as ctx:
        sig = ctx.enter_context(Signals(nc, name))
        norm = Norm(core, sig, mem, *norm_args)

        def src(j, s):
            return col_strip(w_proj, 0, j, rows=2 * P) if s else col_strip(w_gate, 0, j)
        st = Strips(core, sig, [Run(KT, src, (xh, lambda k: ph[:, k, :]), (xl, lambda k: pl[:, k, :]), nk=(KT, 2),
                                    each=norm.lo, second=(sig["p_lo"], 1))], ahead=ahead)
        block = ctx.enter_context(nc.Block())

        @block.sync
        def _(sp):
            norm.sync(sp)
            sp.dma_start(raw[:, :, :], p_in.rearrange("(k p) t -> p k t", p=P)).then_inc(sig["p"], 16)
            st.load(sp)

        @block.scalar
        def _(act):
            def before(first):
                def splits():
                    first()
                    act.wait_ge(sig["p"], 16)
                    act.activation(ph[:, :, :], raw[:, :, :], ACT.Copy).then_inc(sig["p_hi"], 1)
                norm.scalar(act, splits)

            def out(r, j, g, s):
                if s:
                    return
                act.wait_ge(sig["mm0"], g + 1)
                if not (isinstance(g, int) and g == 0):
                    act.wait_ge(sig["added"], g)
                act.activation(gate[:, :], core.slot(0), ACT.Sigmoid).then_inc(sig["out0"], 1)
            st.follow(act, st.hi_split, out, before)

        @block.gpsimd
        def _(pool):
            def before(first):
                norm.gpsimd(pool, first)
                pool.wait_ge(sig["p_hi"], 1)
                pool.tensor_tensor(pl[:, :, :], raw[:, :, :], ph[:, :, :].bitcast(F32), ALU.subtract
                                   ).then_inc(sig["p_lo"], 1)
            st.follow(pool, st.lo_split, None, before)

        @block.tensor
        def _(pe):
            norm.tensor(pe)
            pe.wait_ge(sig["rstd"], 1)
            st.products(pe)

        @block.vector
        def _(dve):
            norm.vector(dve)

            def out(r, j, g, s):
                if not s:
                    return
                dve.wait_ge(sig["out0"], g + 1)
                dve.wait_ge(sig["mm1"], g + 1)
                dst = at(core.a, j)
                dve.tensor_tensor(gate[:, :], core.slot(1), gate[:, :], ALU.mult).then_inc(sig["out1"], 1)
                dve.wait_ge(sig["out1"], g + 1)
                dve.scalar_tensor_tensor(out=dst, in0=dst, scalar=ALPHA, in1=gate[:, :], op0=ALU.mult, op1=ALU.add
                                         ).then_inc(sig["added"], 1)
            st.follow(dve, None, out)


def merge_phase(nc, core, name, mem, branches, gates, fetched, ahead):
    raw, gate, prod = mem("raw", [P, 2, T]), core.gate, mem("product", [P, 2, T])
    with ExitStack() as ctx:
        sig = ctx.enter_context(Signals(nc, name))
        runs = [branch_run(*b) for b in branches]
        st = Strips(core, sig, runs, fetched, ahead)
        block = ctx.enter_context(nc.Block())

        @block.sync
        def _(sp):
            st.load(sp)

        @block.gpsimd
        def _(pool):
            st.follow(pool, st.lo_split, None)

        @block.tensor
        def _(pe):
            st.products(pe)

        def gate_rows(r, j, s):
            if isinstance(j, int):
                return gates[(KT * r + 2 * j + s) * P:(KT * r + 2 * j + s + 1) * P, :]
            return gates.rearrange("(n p) t -> n p t", p=P)[bass.ds(j * 2 + (KT * r + s), 1), :, :].rearrange(
                "n p t -> (n p) t")

        @block.scalar
        def _(act):
            def out(r, j, g, s):
                act.wait_ge(sig[f"g_raw{s}"], g * 16 + 16)
                if not (isinstance(g, int) and g == 0):
                    act.wait_ge(sig[f"out{s}"], g)
                act.activation(gate[:, s, :], raw[:, s, :], ACT.Sigmoid).then_inc(sig[f"g{s}"], 1)
                nxt(r, j, g, s)

            def fetch(r, j, s):
                act.dma_start(raw[:, s, :], gate_rows(r, j, s)).then_inc(sig[f"g_raw{s}"], 16)

            def nxt(r, j, g, s):
                if isinstance(j, int) and j == KT // 2 - 1:
                    if r + 1 < len(runs):
                        act.wait_ge(sig[f"g{s}"], g + 1)
                        fetch(r + 1, 0, s)
                    return
                act.wait_ge(sig[f"g{s}"], g + 1)
                fetch(r, j + 1, s)
            for s in range(2):
                fetch(0, 0, s)
            st.follow(act, st.hi_split, out, out_first=True)

        @block.vector
        def _(dve):
            def out(r, j, g, s):
                dve.wait_ge(sig[f"g{s}"], g + 1)
                dve.wait_ge(sig[f"mm{s}"], g + 1)
                dst = at(core.a, j * 2 + s)
                if r == 0:
                    dve.tensor_tensor(dst, core.slot(s), gate[:, s, :], ALU.mult).then_inc(sig[f"out{s}"], 1)
                    return
                dve.tensor_tensor(prod[:, s, :], core.slot(s), gate[:, s, :], ALU.mult).then_inc(sig[f"out{s}"], 1)
                dve.wait_ge(sig[f"out{s}"], g + 1)
                dve.tensor_tensor(dst, dst, prod[:, s, :], ALU.add).then_inc(sig["added"], 1)
            st.follow(dve, None, out)


def branch_run(w, yh, yl, rows=P):
    nk = w.shape[0] // rows
    return Run(KT // 2, lambda j, s: col_strip(w, s * P, j * 2, rows=w.shape[0], part=rows), yh, yl, nk=(nk, nk), rows=rows)


def mlp_phase(nc, core, name, w_in, w_out, norm_args):
    mem = Space(nc, name, (OFF_S, END))
    hh, hl = mem("h_hi", [P, KT, T], F32R), mem("h_lo", [P, KT, T], F32R)
    relu, h = mem("relu", [P, 2, T]), mem("h", [P, 2, T])
    xh, xl = x_parts(core)
    chunks = FF2 // (KT * P)
    with ExitStack() as ctx:
        sig = ctx.enter_context(Signals(nc, name))
        norm = Norm(core, sig, Space(nc, name + "_norm", (OFF_S + 32 * KB, END)), *norm_args, keep=False)
        runs = []
        for i in range(chunks):
            runs.append(Run(KT // 2, lambda j, s, i=i: col_strip(w_in, i * D + s * P, j * 2), xh, xl, each=norm.lo))
            runs.append(Run(KT // 2, lambda j, s, i=i: col_strip(w_out, s * P, j * 2, rows=D, row0=i * D),
                            lambda k: hh[:, k, :], lambda k: hl[:, k, :], each=lambda k, i=i: (sig["h_lo"], KT * i + k + 1)))
        st = Strips(core, sig, runs)
        sums = TileSums(core, sig, True)
        block = ctx.enter_context(nc.Block())

        def hidden(r, j, s):
            return j * 2 + (s + KT * (r // 2))

        @block.sync
        def _(sp):
            norm.sync(sp)
            st.load(sp)

        @block.tensor
        def _(pe):
            norm.tensor(pe)
            pe.wait_ge(sig["rstd"], 1)
            st.products(pe)

        @block.scalar
        def _(act):
            def out(r, j, g, s):
                if r == len(runs) - 1:
                    sums.scalar(act, j, g, s)
                if r % 2:
                    return
                f = hidden(r, j, s)
                act.wait_ge(sig[f"mm{s}"], g + 1)
                act.activation(relu[:, s, :], core.slot(s), ACT.Relu).then_inc(sig[f"out{s}"], 1)
                act.wait_ge(sig["squared"], f + 1)
                act.activation(at(hh, j * 2 + s), h[:, s, :], ACT.Copy).then_inc(sig["h_hi"], 1)
            st.follow(act, st.hi_split, out, lambda first: norm.scalar(act, first))

        @block.vector
        def _(dve):
            norm.vector(dve)

            def out(r, j, g, s):
                if r % 2:
                    dve.wait_ge(sig[f"mm{s}"], g + 1)
                    dst = at(core.a, j * 2 + s)
                    dve.tensor_tensor(dst, dst, core.slot(s), ALU.add).then_inc(sig[f"out{s}"], 1)
                    return
                f = hidden(r, j, s)
                dve.wait_ge(sig[f"out{s}"], g + 1)
                dve.wait_ge(sig["h_lo"], f)
                dve.tensor_tensor(h[:, s, :], relu[:, s, :], relu[:, s, :], ALU.mult).then_inc(sig["squared"], 1)
            st.follow(dve, None, out)

        @block.gpsimd
        def _(pool):
            pool.wait_ge(sig["sq_summed"], 1)
            sums.start(pool)

            def out(r, j, g, s):
                if r == len(runs) - 1:
                    sums.gpsimd(pool, j, g, s)
                if r % 2:
                    return
                f = hidden(r, j, s)
                pool.wait_ge(sig["h_hi"], f + 1)
                pool.tensor_tensor(at(hl, j * 2 + s), h[:, s, :], at(hh, j * 2 + s).bitcast(F32), ALU.subtract
                                   ).then_inc(sig["h_lo"], 1)
            st.follow(pool, st.lo_split, out, lambda first: norm.gpsimd(pool, first))


def ffn_run(w_up, f0, n, x=None):
    return Run(n, lambda j, s: col_strip(w_up, f0 * P + s * FF, j), *(x or (None, None)))


def ffn_phase(nc, core, name, w_up, conv, w_down):
    mem = Space(nc, name, (OFF_S, END))
    hh, hl = mem("h_hi", [P, KT, T], F32R), mem("h_lo", [P, KT, T], F32R)
    u, gate = mem("conv", [P, 2, T]), mem("h", [P, 2, T])
    taps = mem("taps", [P, 3, FF // P])
    xh, xl = x_parts(core)
    chunks = [(0, 8), (8, 8), (16, 6)]
    with ExitStack() as ctx:
        sig = ctx.enter_context(Signals(nc, name))
        runs = []
        for f0, n in chunks:
            runs.append(ffn_run(w_up, f0, n, (xh, xl)))
            runs.append(Run(KT // 2, lambda j, s, f0=f0, n=n: col_strip(w_down, s * P, j * 2, rows=n * P, row0=f0 * P),
                            lambda k: hh[:, k, :], lambda k: hl[:, k, :], nk=(n, n),
                            each=lambda k, f0=f0: (sig["h_lo"], f0 + k + 1)))
        st = Strips(core, sig, runs, fetched=True)
        sums = TileSums(core, sig, False)
        block = ctx.enter_context(nc.Block())

        @block.sync
        def _(sp):
            sp.dma_start(taps[:, :, :], conv).then_inc(sig["taps"], 16)
            st.load(sp)

        @block.tensor
        def _(pe):
            st.products(pe)

        def tile_no(r, j):
            return j + chunks[r // 2][0]

        @block.scalar
        def _(act):
            act.wait_ge(sig["taps"], 16)

            def out(r, j, g, s):
                if r % 2:
                    return
                f = tile_no(r, j)
                if s == 0:
                    act.wait_ge(sig["mm0"], g + 1)
                    act.activation(u[:, 0, :], core.slot(0), ACT.Copy, scale=colat(taps[:, 2, :], f)
                                   ).then_inc(sig["tap2"], 1)
                else:
                    act.wait_ge(sig["out0"], g + 1)
                    act.activation(u[:, 1, :], u[:, 0, :], ACT.Gelu_apprx_tanh).then_inc(sig["gelu"], 1)
                    act.wait_ge(sig["out1"], g + 1)
                    act.activation(at(hh, j), gate[:, 0, :], ACT.Copy).then_inc(sig["h_hi"], 1)
            st.follow(act, st.hi_split, out)

        @block.vector
        def _(dve):
            def out(r, j, g, s):
                if r % 2:
                    dve.wait_ge(sig[f"mm{s}"], g + 1)
                    dst = at(core.a, j * 2 + s)
                    dve.tensor_tensor(dst, dst, core.slot(s), ALU.add).then_inc(sig[f"out{s}"], 1)
                    return
                f = tile_no(r, j)
                if s == 0:
                    dve.wait_ge(sig["tap2"], f + 1)
                    dve.scalar_tensor_tensor(out=u[:, 0, 1:T], in0=core.slot(0)[:, 0:T - 1],
                                             scalar=colat(taps[:, 1, :], f), in1=u[:, 0, 1:T],
                                             op0=ALU.mult, op1=ALU.add).then_inc(sig["tap1"], 1)
                    dve.wait_ge(sig["tap1"], f + 1)
                    dve.scalar_tensor_tensor(out=u[:, 0, 2:T], in0=core.slot(0)[:, 0:T - 2],
                                             scalar=colat(taps[:, 0, :], f), in1=u[:, 0, 2:T],
                                             op0=ALU.mult, op1=ALU.add).then_inc(sig["out0"], 1)
                else:
                    dve.wait_ge(sig["mm1"], g + 1)
                    dve.wait_ge(sig["gelu"], f + 1)
                    dve.wait_ge(sig["h_lo"], f)
                    dve.tensor_tensor(gate[:, 0, :], core.slot(1), u[:, 1, :], ALU.mult).then_inc(sig["out1"], 1)
            st.follow(dve, None, out)

        @block.gpsimd
        def _(pool):
            sums.start(pool)

            def out(r, j, g, s):
                if r == len(runs) - 1:
                    sums.gpsimd(pool, j, g, s)
                if r % 2 or s == 0:
                    return
                f = tile_no(r, j)
                pool.wait_ge(sig["h_hi"], f + 1)
                pool.tensor_tensor(at(hl, j), gate[:, 0, :], at(hh, j).bitcast(F32), ALU.subtract
                                   ).then_inc(sig["h_lo"], 1)
            st.follow(pool, st.lo_split, out)


def project_phase(nc, core, name, runs, outs, w_tok=None, zv=None, tokens=None, consts=None, last_vector=None, norm=None,
                  fetched=False, ahead=None, beside=None):
    ps = core.ps
    with ExitStack() as ctx:
        sig = ctx.enter_context(Signals(nc, name))
        feat = list(runs)
        turns = sum(r.n for r in feat)
        side = beside(sig) if beside else None
        if norm:
            norm = Norm(core, sig, *norm[0], **norm[1])
            feat[0].each = norm.lo
        st = Strips(core, sig, feat + ([Run(1, lambda j, s: w_tok(s), None, None)] if w_tok else []), fetched, ahead)
        pe_st = Strips(core, sig, feat)
        block = ctx.enter_context(nc.Block())
        tokens = tokens or (lambda buf, k, j: buf[:, k, j * P:j * P + P])

        @block.sync
        def _(sp):
            if consts:
                consts[0](sp, sig)
            if side:
                side.sync(sp)
            if norm:
                norm.sync(sp)
            st.load(sp)
            if norm:
                norm.sync_end(sp)

        @block.scalar
        def _(act):
            if consts:
                act.wait_ge(sig["ready"], 1)

            def out(r, j, g, s):
                if r >= len(feat):
                    return
                if side:
                    side.scalar_out(act, r, s)
                act.wait_ge(sig[f"mm{s}"], g + 1)
                outs[r](act, j, s, core.slot(s)).then_inc(sig[f"taken{s}" if last_vector else f"out{s}"], 1)
            st.follow(act, st.hi_split, out, (lambda first: norm.scalar(act, first)) if norm else None,
                      ahead=not w_tok)
            if w_tok:
                for b in range(4):
                    act.wait_ge(sig["tok"], b + 1)
                    act.activation(zv[:, 2 * b:2 * b + 2, :], ps[:, 4 + b, :].rearrange("p (j n) -> p j n", j=2),
                                   ACT.Copy)
                if ahead:
                    st.split_hi(act, turns + 1, 0, ahead, warm=False)
            if side:
                side.scalar_end(act)

        @block.gpsimd
        def _(pool):
            st.follow(pool, st.lo_split, None, (lambda first: norm.gpsimd(pool, first)) if norm else None)

        @block.vector
        def _(dve):
            if consts:
                consts[1](dve, sig).then_inc(sig["ready"], 1)
            if norm:
                norm.vector(dve)
            if side:
                side.vector(dve)

                def tile(r, j, g, s):
                    dve.wait_ge(sig[f"out{s}"], g + 1)
                    side.vector_tile(dve, 2 * (3 - r) + s)
                pe_st.follow(dve, None, tile)
                side.vector_end(dve)
            if last_vector:
                def out(r, j, g, s):
                    dve.wait_ge(sig[f"taken{s}"], g + 1)
                    last_vector(dve, r, j, s, core.slot(s)).then_inc(sig[f"out{s}"], 1)
                pe_st.follow(dve, None, out)

        @block.tensor
        def _(pe):
            if norm:
                norm.tensor(pe)
                pe.wait_ge(sig["rstd"], 1)
            pe_st.products(pe)
            if side:
                side.tensor(pe)
            if w_tok:
                for s in range(2):
                    pe.wait_ge(sig[f"w_lo{s}"], turns + 1)
                for j in range(NC):
                    for k in range(KT):
                        for n, (x, w) in enumerate(((core.xh, core.wh), (core.xl, core.wh), (core.xh, core.wl))):
                            last = pe.matmul(ps[:, 4 + j // 2, 256 * (j % 2):256 * (j % 2) + 256],
                                             tokens(x, k, j), w[:, 0:2, k, :],
                                             start=(k == 0 and n == 0), stop=(k == KT - 1 and n == 2))
                    if j % 2:
                        last.then_inc(sig["tok"], 1)


class Shade:

    def __init__(self, core, sig, w, gates, t0, count, ahead):
        self.c, self.sig, self.w, self.gates, self.t0, self.count = core, sig, w, gates, t0, count
        self.ahead, self.chunk = ahead, 0

    def src(self, i):
        return col_strip(self.w, GATE0, self.t0 + i)

    def load_strip(self, sp, i):
        sig, s = self.sig, i % 2
        if i >= 2:
            sp.wait_ge(sig[f"w_lo{s}"], i // 2)
        if i < self.count:
            sp.dma_start(self.c.wr[:, s], self.src(i)).then_inc(sig[f"w_raw{s}"], 16)
        else:
            run = self.ahead
            sp.dma_start(self.c.wr[0:run.rows[s], s, 0:run.nk[s], 0:run.m], run.src(0, s)
                         ).then_inc(sig[f"w_raw{s}"], 16)

    def load_first(self, sp):
        self.load_strip(sp, 0)
        self.load_strip(sp, 1)

    def load_step(self, sp, i):
        self.load_strip(sp, i + 2)
        sp.wait_ge(self.sig["g_taken"], i + 1)
        row = (self.t0 + i) * P
        sp.dma_start(self.gates[row:row + P, :], self.c.gate[:, i % 2, :]).then_inc(self.sig[f"g_stored{i % 2}"], 16)

    def load_end(self, sp):
        for s in range(2):
            sp.wait_ge(self.sig[f"g_stored{s}"], 8 * self.count)
            sp.wait_ge(self.sig[f"w_raw{s}"], 8 * self.count + 16)

    def load(self, sp):
        self.load_first(sp)
        for i in range(self.count):
            self.load_step(sp, i)
        self.load_end(sp)

    def split_hi(self, act, i):
        s, run = i % 2, self.ahead
        if i > self.count:
            return
        r, nk, m = (P, KT, P) if i < self.count else (run.rows[0], run.nk[0], run.m)
        act.wait_ge(self.sig[f"w_raw{s}"], 16 * (i // 2 + 1))
        act.activation(self.c.wh[0:r, s, 0:nk, 0:m], self.c.wr[0:r, s, 0:nk, 0:m], ACT.Copy
                       ).then_inc(self.sig[f"w_hi{s}"], 1)

    def split_lo(self, pool, i):
        s, run = i % 2, self.ahead
        if i > self.count:
            return
        r, nk, m = (P, KT, P) if i < self.count else (run.rows[0], run.nk[0], run.m)
        pool.wait_ge(self.sig[f"w_hi{s}"], i // 2 + 1)
        pool.tensor_tensor(self.c.wl[0:r, s, 0:nk, 0:m], self.c.wr[0:r, s, 0:nk, 0:m],
                           self.c.wh[0:r, s, 0:nk, 0:m].bitcast(F32), ALU.subtract).then_inc(self.sig[f"w_lo{s}"], 1)

    def take(self, act, i):
        act.wait_ge(self.sig["g_mm"], i + 1)
        if i >= 2:
            act.wait_ge(self.sig[f"g_stored{i % 2}"], 16 * (i // 2))
        act.activation(self.c.gate[:, i % 2, :], self.c.slot(3), ACT.Copy).then_inc(self.sig["g_taken"], 1)

    def chunks(self, pe, n):
        for _ in range(n):
            i, k = self.chunk // 8, self.chunk % 8
            self.chunk += 1
            s = i % 2
            if k == 0:
                pe.wait_ge(self.sig[f"w_lo{s}"], i // 2 + 1)
                if i:
                    pe.wait_ge(self.sig["g_taken"], i)
            for j, (w, x) in enumerate(((self.c.wh, self.c.xh), (self.c.wh, self.c.xl), (self.c.wl, self.c.xh))):
                for h in range(2):
                    last = pe.matmul(self.c.ps[:, 6 + h, :], w[:, s, k, :], x[:, k, 512 * h:512 * h + 512],
                                     start=(k == 0 and j == 0), stop=(k == 7 and j == 2))
            if k == 7:
                last.then_inc(self.sig["g_mm"], 1)


class AttentionShade:

    def __init__(self, core, sig, w, col0, gates, count):
        self.c, self.sig, self.w, self.col0, self.gates, self.count = core, sig, w, col0, gates, count

    def fetch(self, act, i):
        act.dma_start(self.c.wr[:, i % 2], col_strip(self.w, self.col0, i)).then_inc(self.sig[f"w_raw{i % 2}"], 16)

    def split_hi(self, act, i):
        if i < self.count:
            act.wait_ge(self.sig[f"w_raw{i % 2}"], 16 * (i // 2 + 1))
            act.activation(self.c.wh[:, i % 2], self.c.wr[:, i % 2], ACT.Copy).then_inc(self.sig[f"w_hi{i % 2}"], 1)

    def start(self, act):
        for i in range(2):
            self.fetch(act, i)
        for i in range(2):
            self.split_hi(act, i)

    def store(self, act, q):
        act.wait_ge(self.sig["g_taken"], q + 1)
        i, h = q // 2, q % 2
        act.dma_start(self.gates[i * P:i * P + P, 512 * h:512 * h + 512],
                      self.c.gate[:, i % 2, 512 * h:512 * h + 512]).then_inc(self.sig[f"g_stored{q % 4}"], 16)

    def take(self, act, q):
        i, h = q // 2, q % 2
        act.wait_ge(self.sig["g_mm"], q + 1)
        if q >= 4:
            act.wait_ge(self.sig[f"g_stored{q % 4}"], 16 * (q // 4))
        act.activation(self.c.gate[:, i % 2, 512 * h:512 * h + 512], self.c.ps[:, 7, :], ACT.Copy
                       ).then_inc(self.sig["g_taken"], 1)
        if h == 0:
            if i:
                self.split_hi(act, i + 1)
        elif i + 2 < self.count:
            self.fetch(act, i + 2)
        if q:
            self.store(act, q - 1)

    def end(self, act):
        self.store(act, 2 * self.count - 1)
        for q in range(4):
            act.wait_ge(self.sig[f"g_stored{q}"], 16 * (2 * self.count // 4))

    def split_all_lo(self, pool):
        for i in range(self.count):
            pool.wait_ge(self.sig[f"w_hi{i % 2}"], i // 2 + 1)
            pool.tensor_tensor(self.c.wl[:, i % 2], self.c.wr[:, i % 2], self.c.wh[:, i % 2].bitcast(F32),
                               ALU.subtract).then_inc(self.sig[f"w_lo{i % 2}"], 1)

    def half(self, pe, q, first=0, end=KT):
        s, h = q // 2 % 2, q % 2
        if h == 0 and first == 0:
            pe.wait_ge(self.sig[f"w_lo{s}"], q // 4 + 1)
        if q and first == 0:
            pe.wait_ge(self.sig["g_taken"], q)
        for k in range(first, end):
            for j, (w, x) in enumerate(((self.c.wh, self.c.xh), (self.c.wh, self.c.xl), (self.c.wl, self.c.xh))):
                last = pe.matmul(self.c.ps[:, 7, :], w[:, s, k, :], x[:, k, 512 * h:512 * h + 512],
                                 start=(k == 0 and j == 0), stop=(k == 7 and j == 2))
        if end == KT:
            last.then_inc(self.sig["g_mm"], 1)


class Ring:

    def __init__(self, core, sig, steps, pairs, shade=None, table=None):
        self.c, self.sig, self.steps, self.pairs, self.shade, self.table = core, sig, steps, pairs, shade, table or {}
        self.place = {step: i for i, step in enumerate(steps)}

    def bank(self, name, unit):
        i = self.place[name, unit] % self.pairs
        return self.c.ps[:, 2 * i:2 * i + 2, :].rearrange("p a b -> p (a b)")

    def start(self, pe, name, unit):
        if (name, unit) in self.table:
            self.shade.chunks(pe, self.table[name, unit])
        back = self.place[name, unit] - self.pairs
        if back >= 0:
            pe.wait_ge(self.sig["out_" + self.steps[back][0]], self.steps[back][1] + 1)
        return self.bank(name, unit)

    def full(self, eng, name, unit):
        eng.wait_ge(self.sig["pe"], self.place[name, unit] + 1)
        return self.bank(name, unit)


LEVELS = (64, 32, 16, 8, 4, 2, 1)


def linear_mixer(nc, core, name, kind, mem, z, zv, yh, yl, y0, k, ahead, shaded):
    H = 512
    ret, gla, hgrn = kind == "ret", kind == "gla", kind == "hgrn"
    sc, dd = mem("scores", [P, 8, P]), mem("d", [P, 2, H])
    if ret:
        rot, sel = mem("rot", [P, 2, H]), mem("sel", [P, 4, P])
    if gla:
        sel = mem("sel", [P, 4, P])
    q, kk, c = mem("q", [P, H]), mem("k", [P, H]), None if ret else mem("c", [P, H])
    qe, ke = (mem("qe", [P, 2, H]), mem("ke", [P, 2, H])) if not ret else (mem("qe", [P, 1, H]), mem("ke", [P, 1, H]))
    kt, xs = mem("k_tok", [P, 4, P]), mem("state", [P, 5, P])
    psi = kk[:, :].rearrange("p (j t) -> p j t", t=P) if ret else mem("state_new", [P, 4, P])
    ident, bd, bdm = mem("ident", [P, P]), mem("heads", [P, P]), mem("head_mean", [P, P])
    gain, eend, epst = mem("gain", [P, 2]), mem("end", [P, 4]), mem("eps", [P, 1])
    if not ret:
        masks, onesr = mem("masks", [P, 8, P], I32), mem("ones", [P, P])
    if ret:
        dec, xz = mem("decay", [P, 2, P]), mem("xi_zeta", [P, 2, P])
        gend = mem("chunk_decay", [P, 2])
    if gla:
        w2e, bcol = mem("w2", [16, 2, P]), mem("b", [P, 2])
    units = [(u, hf) for u in range(2) for hf in range(2)]
    first = ["qs", "ks"] if ret else ["qk", "gate"] if gla else []
    levels = ["score"] if ret else [f"l{i}" for i in range(8)]
    steps = []
    for n in range(len(units) + 1):
        if ret and n:
            steps += [("mean", n - 1)]
        if n < len(units):
            steps += [(x, n) for x in first]
        if n:
            steps += [("var", n - 1)]
        if n < len(units):
            steps += [(x, n) for x in levels + ["kt", "psi", "y"]]
    nconst = 16 * {"ret": 4, "gla": 7, "hgrn": 6}[kind]
    with ExitStack() as ctx:
        sig = ctx.enter_context(Signals(nc, name))
        per_unit = 1 if ret else 2
        shade = Shade(core, sig, *shaded, per_unit * len(units), ahead)
        table = {}
        for n in range(len(units)):
            if ret:
                table |= {(x, n): 1 for x in ("ks", "score", "kt", "psi")} | {("y", n): 2, ("qs", n): 1 if n else 2}
                if n:
                    table["var", n - 1] = 1
                continue
            table |= {("l0", n): 5, ("l2", n): 1, ("l4", n): 1, ("l6", n): 1}
            if hgrn and n:
                table |= {("var", n - 1): 2, ("l0", n): 3}
            table |= {("kt", n): 2, ("psi", n): 2, ("y", n): 4}
        ring = Ring(core, sig, steps, 3, shade, table)
        t0_, t1_, sq = (nc.alloc_sbuf_tensor_at(f"{name}_tail{i}", [P, H], F32, offset=OFF_TAIL + 2 * KB * i)
                        for i in range(3))
        t0, t1, sq = t0_[:, :], t1_[:, :], sq[:, :]
        block = ctx.enter_context(nc.Block())

        def tk(buf, j):
            return buf[:, j * P:j * P + P]

        def later(x, L):
            return x.rearrange("p (n t) -> p n t", t=2 * L)[:, :, L:2 * L]

        def earlier(x, L):
            return x.rearrange("p (n t) -> p n t", t=2 * L)[:, :, 0:L]

        @block.sync
        def _(sp):
            sp.dma_start(ident[:, :], k["ident"]).then_inc(sig["consts"], 16)
            sp.dma_start(bd[:, :], k["heads"]).then_inc(sig["consts"], 16)
            sp.dma_start(bdm[:, :], k["head_mean"]).then_inc(sig["consts"], 16)
            if ret:
                sp.dma_start(gend[:, :], k["ret_end"]).then_inc(sig["consts"], 16)
            else:
                sp.dma_start(gain[:, :], k[kind + "_gain"]).then_inc(sig["consts"], 16)
                sp.dma_start(masks[:, :, :], k["levels"]).then_inc(sig["consts"], 16)
                sp.dma_start(onesr[:, :], k["ones"]).then_inc(sig["consts"], 16)
            if gla:
                sp.dma_start(sel[:, :, :], k["gla_sel"]).then_inc(sig["consts"], 16)
                sp.wait_ge(sig["zeroed"], 2)
                for h in range(4):
                    u, o = h // 2, 64 * (h % 2)
                    sp.dma_start(w2e[:, u, o:o + 32], k["gla_w2"][:, 32 * h:32 * h + 32]).then_inc(sig["w2"], 16)
                    sp.dma_start(bcol[o:o + 32, u:u + 1], k["gla_b"][32 * h:32 * h + 32, :]).then_inc(sig["w2"], 16)
            if ret:
                for n, (u, hf) in enumerate(units):
                    if n:
                        sp.wait_ge(sig["scores"], n)
                        sp.wait_ge(sig["qd"], n)
                    sp.dma_start(rot[:, :, :], k["rot"][:, :, hf * H:hf * H + H]).then_inc(sig["unit_consts"], 16)
                    sp.dma_start(sel[:, :, :], k["ret_sel"][:, 4 * u:4 * u + 4, :]).then_inc(sig["unit_consts"], 16)
                    sp.dma_start(dec[:, :, :], k["ret_decay"][:, 2 * u:2 * u + 2, :]).then_inc(sig["unit_consts"], 16)
                    sp.dma_start(xz[:, :, :], k["ret_xz"][:, 2 * u:2 * u + 2, :]).then_inc(sig["unit_consts"], 16)
                    if n == 0:
                        shade.load_first(sp)
                    else:
                        shade.load_step(sp, n - 1)
                shade.load_step(sp, len(units) - 1)
                shade.load_end(sp)
            else:
                shade.load(sp)

        @block.tensor
        def _(pe):
            pe.wait_ge(sig["consts"], nconst)
            if gla:
                pe.wait_ge(sig["w2"], 128)
            def mean(n):
                b = ring.start(pe, "mean", n)
                pe.wait_ge(sig["out_y"], n + 1)
                pe.matmul(b[:, 0:H], bdm[:, :], t0, start=True, stop=True).then_inc(sig["pe"], 1)

            def var(n):
                b = ring.start(pe, "var", n)
                pe.wait_ge(sig["sq"], n + 1)
                pe.matmul(b[:, 0:H], bdm[:, :], sq, start=True, stop=True).then_inc(sig["pe"], 1)

            for n, (u, hf) in enumerate(units):
                cols = slice(hf * H, hf * H + H)
                if ret and n:
                    mean(n - 1)
                if ret:
                    pe.wait_ge(sig["unit_consts"], 64 * (n + 1))
                    for i, s in enumerate(("qs", "ks")):
                        b = ring.start(pe, s, n)
                        pe.matmul(b[:, 0:H], sel[:, 2 * i, :], z[:, i, cols], start=True, stop=True)
                        pe.matmul(b[:, H:2 * H], sel[:, 2 * i + 1, :], z[:, i, cols], start=True, stop=True
                                  ).then_inc(sig["pe"], 1)
                if gla:
                    b = ring.start(pe, "qk", n)
                    pe.matmul(b[:, 0:H], sel[:, u, :], z[:, 0, cols], start=True, stop=True)
                    pe.matmul(b[:, H:2 * H], sel[:, 2 + u, :], z[:, 1, cols], start=True, stop=True
                              ).then_inc(sig["pe"], 1)
                    b = ring.start(pe, "gate", n)
                    pe.matmul(b[:, 0:H], w2e[:, u, :], z[0:16, 2, cols], start=True, stop=True).then_inc(sig["pe"], 1)
                if n:
                    var(n - 1)
                for i, s in enumerate(["score"] if ret else [f"l{i}" for i in range(8)]):
                    b = ring.start(pe, s, n)
                    if ret or i == 7:
                        pe.wait_ge(sig["q"], n + 1)
                        pe.wait_ge(sig["k"], n + 1)
                        qa, ka = (q[:, :], kk[:, :])
                        if hgrn:
                            qa = z[:, u, cols]
                    else:
                        pe.wait_ge(sig["level"], 7 * n + i + 1)
                        qa, ka = qe[:, i % 2, :], ke[:, i % 2, :]
                    for h in range(2):
                        for j in range(4):
                            o = (4 * h + j) * P
                            last = pe.matmul(b[:, o:o + P], tk(ka, j)[64 * h:64 * h + 64, :],
                                             tk(qa, j)[64 * h:64 * h + 64, :], start=True, stop=True)
                    last.then_inc(sig["pe"], 1)
                b = ring.start(pe, "kt", n)
                pe.wait_ge(sig["kd"], n + 1)
                for j in range(4):
                    last = pe.transpose(tk(b, j), tk(ke[:, 0, :], j), ident[:, :])
                last.then_inc(sig["pe"], 1)
                b = ring.start(pe, "psi", n)
                pe.wait_ge(sig["out_kt"], n + 1)
                for j in range(4):
                    last = pe.matmul(tk(b, j), kt[:, j, :], zv[:, 4 * hf + j, u * P:u * P + P], start=True, stop=True)
                last.then_inc(sig["pe"], 1)
                b = ring.start(pe, "y", n)
                pe.wait_ge(sig["states"], 4 * n + 4)
                pe.wait_ge(sig["scores"], n + 1)
                pe.wait_ge(sig["qd"], n + 1)
                for j in range(4):
                    for h in range(2):
                        dst = b[64 * h:64 * h + 64, j * P:j * P + P]
                        pe.matmul(dst, xs[:, j, 64 * h:64 * h + 64], tk(qe[:, 0, :], j), start=True, stop=False)
                        last = pe.matmul(dst, zv[:, 4 * hf + j, u * P + 64 * h:u * P + 64 * h + 64],
                                         sc[:, 4 * h + j, :], start=False, stop=True)
                last.then_inc(sig["pe"], 1)
            if ret:
                mean(len(units) - 1)
            var(len(units) - 1)

        @block.scalar
        def _(act):
            def deviation(n):
                if ret:
                    act.wait_ge(sig["out_mean"], n + 1)
                    act.activation(sq, t0, ACT.Square).then_inc(sig["sq"], 1)
                b = ring.full(act, "var", n)
                act.wait_ge(sig["eps"], 1)
                act.activation(t1, b[:, 0:H], ACT.Sqrt, bias=epst[:, 0:1]).then_inc(sig["out_var"], 1)

            def output_hi(n):
                u, hf = units[n]
                act.wait_ge(sig["outv"], n + 1)
                act.activation(yh[:, y0 + u, hf * H:hf * H + H], t0, ACT.Copy).then_inc(sig["yh"], 1)

            for n, (u, hf) in enumerate(units):
                cols = slice(hf * H, hf * H + H)
                if n and not ret:
                    act.wait_ge(sig["kd"], n)
                    act.wait_ge(sig["qd"], n)
                if n == 0:
                    shade.split_hi(act, 0)
                    shade.split_hi(act, 1)
                d0, d1 = dd[:, 0, :], dd[:, 1, :]
                if gla:
                    b = ring.full(act, "qk", n)
                    act.activation(q[:, :], b[:, 0:H], ACT.Copy).then_inc(sig["q"], 1)
                    act.activation(kk[:, :], b[:, H:2 * H], ACT.Copy).then_inc(sig["out_qk"], 1)
                    act.wait_ge(sig["out_qk"], n + 1)
                    act.wait_ge(sig["consts"], nconst)
                    act.wait_ge(sig["w2"], 128)
                    b = ring.full(act, "gate", n)
                    act.activation(c[:, :], b[:, 0:H], ACT.Identity, bias=bcol[:, u:u + 1]).then_inc(sig["out_gate"], 1)
                    act.wait_ge(sig["out_gate"], n + 1)
                    x = c[:, :]
                if hgrn:
                    x = z[:, 2 + u, cols]
                if not ret:
                    act.activation(d0, x, ACT.Abs).then_inc(sig["abs"], 1)
                    act.wait_ge(sig["abs"], n + 1)
                    act.activation(d0, d0, ACT.Exp, scale=-1.0).then_inc(sig["expabs"], 1)
                    act.wait_ge(sig["expabs"], n + 1)
                    act.activation(d1, d0, ACT.Ln, bias=1.0).then_inc(sig["ln"], 1)
                    if hgrn:
                        act.wait_ge(sig["lwx"], n + 1)
                        act.activation(kk[:, :], kk[:, :], ACT.Exp).then_inc(sig["k"], 1)
                if n:
                    deviation(n - 1)
                if not ret:
                    for i in range(7):
                        act.wait_ge(sig["dist"], 7 * n + i + 1)
                        act.activation(dd[:, i % 2, :], dd[:, i % 2, :], ACT.Exp).then_inc(sig["e"], 1)
                    act.wait_ge(sig["todecay"], n + 1)
                    act.activation(d0, d0, ACT.Exp).then_inc(sig["ekd"], 1)
                    act.activation(d1, c[:, :], ACT.Exp).then_inc(sig["eqd"], 1)
                    act.activation(eend[:, :], c[:, :].rearrange("p (j t) -> p j t", t=P)[:, :, P - 1], ACT.Exp
                                   ).then_inc(sig["eend"], 1)
                    shade.take(act, 2 * n)
                    shade.split_hi(act, 2 * n + 2)
                if n:
                    output_hi(n - 1)
                b = ring.full(act, "y", n)
                if n:
                    act.wait_ge(sig["unit"], n)
                act.activation(t0, b[:, 0:H], ACT.Copy).then_inc(sig["out_y"], 1)
                if not ret:
                    act.wait_ge(sig["out_y"], n + 1)
                    act.activation(sq, t0, ACT.Square).then_inc(sig["sq"], 1)
                last = per_unit * (n + 1) - 1
                shade.take(act, last)
                shade.split_hi(act, last + 2)
            deviation(len(units) - 1)
            output_hi(len(units) - 1)

        @block.vector
        def _(dve):
            dve.memset(epst[:, :], 1e-6).then_inc(sig["eps"], 1)
            if gla:
                dve.memset(w2e[:, :, :], 0.0).then_inc(sig["zeroed"], 1)
                dve.memset(bcol[:, :], 0.0).then_inc(sig["zeroed"], 1)
            dve.memset(sc[:, :, :], 0.0).then_inc(sig["sc0"], 1)
            dve.wait_ge(sig["sc0"], 1)
            dve.wait_ge(sig["consts"], nconst)
            def centre(n):
                b = ring.full(dve, "mean", n)
                dve.wait_ge(sig["out_y"], n + 1)
                dve.tensor_tensor(t0, t0, b[:, 0:H], ALU.subtract).then_inc(sig["out_mean"], 1)

            def output(n):
                u, hf = units[n]
                dve.wait_ge(sig["out_var"], n + 1)
                dve.reciprocal(t1, t1).then_inc(sig["rstd"], 1)
                dve.wait_ge(sig["rstd"], n + 1)
                dve.wait_ge(sig["sq"], n + 1)
                if ret:
                    dve.tensor_tensor(t1, t0, t1, ALU.mult).then_inc(sig["yn"], 1)
                else:
                    dve.scalar_tensor_tensor(out=t1, in0=t0, scalar=gain[:, u:u + 1], in1=t1, op0=ALU.mult,
                                             op1=ALU.mult).then_inc(sig["yn"], 1)
                dve.wait_ge(sig["yn"], n + 1)
                g = z[:, (2 if ret else 3 if gla else 4) + u, hf * H:hf * H + H]
                dve.tensor_tensor(t0, t1, g, ALU.mult).then_inc(sig["outv"], 1)

            for n, (u, hf) in enumerate(units):
                cols = slice(hf * H, hf * H + H)
                d0, d1 = dd[:, 0, :], dd[:, 1, :]
                if n and ret:
                    dve.wait_ge(sig["qd"], n)
                if ret:
                    dve.wait_ge(sig["unit_consts"], 64 * (n + 1))
                    for s, dst, nm in (("qs", q, "q"), ("ks", kk, "k")):
                        b = ring.full(dve, s, n)
                        dve.tensor_tensor(dst[:, :], b[:, 0:H], rot[:, 0, :], ALU.mult).then_inc(sig[nm + "cos"], 1)
                        if nm == "k":
                            dve.wait_ge(sig["q"], n + 1)
                        dve.tensor_tensor(d0, b[:, H:2 * H], rot[:, 1, :], ALU.mult).then_inc(sig["out_" + s], 1)
                        dve.wait_ge(sig[nm + "cos"], n + 1)
                        dve.wait_ge(sig["out_" + s], n + 1)
                        dve.tensor_tensor(dst[:, :], dst[:, :], d0, ALU.add).then_inc(sig[nm], 1)
                    if n:
                        centre(n - 1)
                        ring.full(dve, "y", n - 1)
                    b = ring.full(dve, "score", n)
                    for h in range(2):
                        last = dve.tensor_tensor(sc[:, 4 * h:4 * h + 4, :], b[:, h * H:h * H + H].rearrange(
                            "p (j t) -> p j t", t=P), bc(dec[:, h, :], 4), ALU.mult)
                        if h == 0:
                            last.then_inc(sig["score_h0"], 1)
                    last.then_inc(sig["out_score"], 1)
                    dve.wait_ge(sig["out_score"], n + 1)
                    dve.sem_inc(sig["scores"], 1)
                    if n:
                        output(n - 1)
                else:
                    if hgrn:
                        x = z[:, 2 + u, cols]
                    else:
                        dve.wait_ge(sig["out_gate"], n + 1)
                        x = c[:, :]
                    dve.wait_ge(sig["ln"], n + 1)
                    dve.scalar_tensor_tensor(out=d0, in0=x, scalar=0.0, in1=d1, op0=ALU.min,
                                             op1=ALU.subtract).then_inc(sig["lw"], 1)
                    dve.wait_ge(sig["lw"], n + 1)
                    if hgrn:
                        dve.tensor_tensor(kk[:, :], d0, x, ALU.subtract).then_inc(sig["lwx"], 1)
                    else:
                        dve.tensor_scalar(d0, d0, 1.0 / 16.0, None, ALU.mult).then_inc(sig["lw16"], 1)
                        dve.wait_ge(sig["lw16"], n + 1)
                    if n:
                        dve.wait_ge(sig["eend"], n)
                        dve.wait_ge(sig["eqd"], n)
                    for j in range(4):
                        dve.tensor_tensor_scan(out=tk(c, j), data0=onesr[:, :], data1=tk(d0, j), initial=0.0,
                                               op0=ALU.mult, op1=ALU.add).then_inc(sig["scan"], 1)
                    dve.wait_ge(sig["scan"], 4 * n + 4)
                    if hgrn:
                        dve.wait_ge(sig["lwx"], n + 1)

                    def take(i):
                        b = ring.full(dve, f"l{i}", n)
                        if n or i:
                            dve.wait_ge(sig["taken"], 8 * n + i)
                        if n and i == 0:
                            ring.full(dve, "y", n - 1)
                        dst, mask, src = sc[:, :, :], masks[:, i, :], b.rearrange("p (j t) -> p j t", t=P)
                        if i < 7:
                            L = LEVELS[i]
                            dst, src = (x.rearrange("p j (n t) -> p j n t", t=2 * L)[:, :, :, L:2 * L] for x in (dst, src))
                            mask = later(mask, L).unsqueeze(1).to_broadcast([P, 8, 64 // L, L])
                        else:
                            mask = bc(mask, 8)
                        dve.copy_predicated(dst, mask, src).then_inc(sig[f"out_l{i}"], 1)
                        dve.wait_ge(sig[f"out_l{i}"], n + 1)
                        dve.sem_inc(sig["taken"], 1)
                    for i, L in enumerate(LEVELS):
                        if i >= 2:
                            dve.wait_ge(sig["level"], 7 * n + i - 1)
                        c3 = c[:, :].rearrange("p (n t) -> p n t", t=2 * L)
                        e3 = dd[:, i % 2, :].rearrange("p (n t) -> p n t", t=2 * L)
                        ref = bcl(c3[:, :, L - 1], L)
                        dve.tensor_tensor(e3[:, :, L:2 * L], c3[:, :, L:2 * L], ref, ALU.subtract
                                          ).then_inc(sig["dist_up"], 1)
                        dve.wait_ge(sig["dist_up"], 7 * n + i + 1)
                        dve.tensor_tensor(e3[:, :, 0:L], ref, c3[:, :, 0:L], ALU.subtract
                                          ).then_inc(sig["dist"], 1)
                        if i >= 2:
                            take(i - 2)
                        if n and i == 1:
                            output(n - 1)
                    dve.wait_ge(sig["level"], 7 * n + 7)
                    c3 = c[:, :].rearrange("p (n t) -> p n t", t=P)
                    dve.tensor_tensor(d0.rearrange("p (n t) -> p n t", t=P), bcl(c3[:, :, P - 1], P), c3,
                                      ALU.subtract).then_inc(sig["todecay"], 1)
                    for i in range(5, 8):
                        take(i)
                    dve.wait_ge(sig["out_l7"], n + 1)
                    dve.sem_inc(sig["scores"], 1)
                b = ring.full(dve, "kt", n)
                dve.tensor_copy(flat(kt[:, :, :]), b[:, 0:H]).then_inc(sig["out_kt"], 1)
                b = ring.full(dve, "psi", n)
                dve.tensor_tensor(psi[:, :, :], b[:, 0:H].rearrange("p (j t) -> p j t", t=P), bc(bd[:, :], 4),
                                  ALU.mult).then_inc(sig["out_psi"], 1)
                if n:
                    ring.full(dve, "y", n - 1)
                if hf:
                    dve.tensor_copy(xs[:, 0, :], xs[:, 4, :]).then_inc(sig["carried"], 1)
                else:
                    dve.memset(xs[:, 0, :], 0.0).then_inc(sig["carried"], 1)
                dve.wait_ge(sig["out_psi"], n + 1)
                dve.wait_ge(sig["carried"], n + 1)
                if not ret:
                    dve.wait_ge(sig["eend"], n + 1)
                for j in range(4):
                    if j:
                        dve.wait_ge(sig["states"], 4 * n + j)
                    dve.scalar_tensor_tensor(out=xs[:, j + 1, :], in0=xs[:, j, :],
                                             scalar=gend[:, u:u + 1] if ret else eend[:, j:j + 1],
                                             in1=psi[:, j, :], op0=ALU.mult, op1=ALU.add).then_inc(sig["states"], 1)
            if ret:
                centre(len(units) - 1)
            output(len(units) - 1)

        @block.gpsimd
        def _(pool):
            if not ret:
                pool.memset(ke[:, :, :], 0.0).then_inc(sig["ke0"], 1)
                pool.memset(qe[:, :, :], 0.0).then_inc(sig["ke0"], 1)
                pool.wait_ge(sig["ke0"], 2)

            def output_lo(n):
                u, hf = units[n]
                cols = slice(hf * H, hf * H + H)
                pool.wait_ge(sig["yh"], n + 1)
                pool.tensor_tensor(yl[:, y0 + u, cols], t0, yh[:, y0 + u, cols].bitcast(F32), ALU.subtract
                                   ).then_inc(sig["unit"], 1)

            for n, (u, hf) in enumerate(units):
                cols = slice(hf * H, hf * H + H)
                d0, d1 = dd[:, 0, :], dd[:, 1, :]
                if n:
                    ring.full(pool, "y", n - 1)
                if n == 0:
                    shade.split_lo(pool, 0)
                    shade.split_lo(pool, 1)
                qin = z[:, u, cols] if hgrn else q[:, :]
                if gla:
                    pool.wait_ge(sig["q"], n + 1)
                    pool.wait_ge(sig["out_qk"], n + 1)
                    pool.engine_nop().then_inc(sig["k"], 1)
                if hgrn:
                    pool.wait_ge(sig["k"], n + 1)
                    pool.engine_nop().then_inc(sig["q"], 1)
                if ret:
                    pool.wait_ge(sig["unit_consts"], 64 * (n + 1))
                    pool.wait_ge(sig["q"], n + 1)
                    pool.wait_ge(sig["k"], n + 1)
                    v4 = lambda x: x.rearrange("p (j t) -> p j t", t=P)
                    pool.tensor_tensor(v4(ke[:, 0, :]), v4(kk[:, :]), bc(xz[:, 1, :], 4), ALU.mult
                                       ).then_inc(sig["kd"], 1)
                    pool.tensor_tensor(v4(qe[:, 0, :]), v4(q[:, :]), bc(xz[:, 0, :], 4), ALU.mult
                                       ).then_inc(sig["qd"], 1)
                else:
                    for i in range(7):
                        pool.wait_ge(sig["e"], 7 * n + i + 1)
                        if i >= 2:
                            ring.full(pool, f"l{i - 2}", n)
                        L = LEVELS[i]
                        pool.tensor_tensor(later(qe[:, i % 2, :], L), later(qin, L), later(dd[:, i % 2, :], L), ALU.mult
                                           ).then_inc(sig["qe"], 1)
                        pool.tensor_tensor(earlier(ke[:, i % 2, :], L), earlier(kk[:, :], L), earlier(dd[:, i % 2, :], L),
                                           ALU.mult).then_inc(sig["ke"], 1)
                        pool.wait_ge(sig["qe"], 7 * n + i + 1)
                        pool.wait_ge(sig["ke"], 7 * n + i + 1)
                        pool.sem_inc(sig["level"], 1)
                    ring.full(pool, "l6", n)
                    pool.wait_ge(sig["ekd"], n + 1)
                    pool.tensor_tensor(ke[:, 0, :], kk[:, :], d0, ALU.mult).then_inc(sig["kd"], 1)
                    pool.wait_ge(sig["eqd"], n + 1)
                    pool.tensor_tensor(qe[:, 0, :], qin, d1, ALU.mult).then_inc(sig["qd"], 1)
                if n:
                    output_lo(n - 1)
                for i in range(per_unit):
                    shade.split_lo(pool, per_unit * n + 2 + i)
            output_lo(len(units) - 1)


def rwkv_mixer(nc, core, mem, z, yh, yl, y0, k, ahead, shaded):
    H = 512
    r_, k_, v_, wa_, gl_ = 0, 2, 4, 6, 7
    cst = mem("masks", [P, 7, P])
    ident, heads, hmean, ones = (mem(n, [P, P]) for n in ("ident", "heads", "head_mean", "ones"))
    wa2, g2, pc, epst = mem("wa2", [P, 256]), mem("g2", [P, 256]), mem("params", [P, 2, 8]), mem("eps", [P, 2])
    em, ecm, eend = mem("e_mid", [P, 4]), mem("e_mid_end", [P, 4]), mem("e_end", [P, 4])
    mt, rk, rb = mem("m_t", [P, 8, P]), mem("rho_kappa", [P, 8, P]), mem("rho_beta", [P, 8, P])
    l16, l32, l64 = mem("l16", [P, 8, P]), mem("l32", [P, 8, P]), mem("l64", [P, 8, P])
    jj, jt, j2, j2t = mem("j", [P, 8, P]), mem("jt", [P, 8, P]), mem("j2", [P, 8, P]), mem("j2t", [P, 8, P])
    xx, j4, j4t = mem("x", [P, 8, P]), mem("j4", [P, 8, P]), mem("j4t", [P, 8, P])
    at_, bt, kt, vt = (mem(n, [P, 4, P]) for n in ("a_tok", "b_tok", "k_tok", "v_tok"))
    xs = mem("state", [P, 5, P])

    def halves(buf):
        f = flat(buf[:, :, :])
        return f[:, 0:H], f[:, H:2 * H]
    lw, c = halves(jj)
    a, kk = halves(jt)
    kp, e1 = halves(j2)
    e3, e2 = halves(j2t)
    tmp, _ = halves(xx)
    al, be = halves(j4)
    ka, rh = halves(j4t)
    a0f, b0f, k0f = e3, e1, e2
    xt, ww, j8t = jj, jt, j2
    ta, mv = halves(j4)
    tat, tmv = halves(j4t)
    phi, psi = halves(j2t)
    uu, _ = halves(jj)
    dg, _ = halves(mt)
    y, sq = halves(l16)
    sd, _ = halves(l32)
    bv, _ = halves(l64)
    M_JT, M_L16, M_L32, M_L64, M_J, M_SU, M_IU = range(7)
    W0, A0, K_K, K_A, R_K, LN_W, LN_B, OMKA = range(8)
    steps = ["wa", "norm", "tr1", "tr2", "L", "N", "M", "RK", "RB", "J2", "J2t", "X2", "J4", "J4t", "X4", "J8t", "X8"]
    for lv in (16, 32, 64):
        steps += [f"T{lv}", f"W{lv}", f"Y{lv}"]
    steps += ["TA", "TAt", "PP", "c0", "c1", "c2", "c3", "U", "y", "bg", "mean", "var"]
    units = [(u, hf) for u in range(2) for hf in range(2)]
    name = "rwkv"
    NCONST = 16 * 9

    def tk(buf, j):
        return buf[:, j * P:j * P + P]

    def j4v(x):
        return x.rearrange("p (j t) -> p j t", t=P)

    with ExitStack() as ctx:
        sig = ctx.enter_context(Signals(nc, name))
        shade = Shade(core, sig, *shaded, 3 * len(units), ahead)
        table = {"norm": 2, "tr1": 6, "tr2": 1, "J2": 1, "X2": 1, "J4": 1, "X4": 1, "X8": 1, "T16": 1, "W16": 1,
                 "T32": 1, "T64": 1, "TA": 1, "PP": 1, "c0": 1, "c1": 1, "c2": 1, "c3": 1}
        order = []
        for n in range(len(units) + 1):
            for x, back in (("wa", 0), ("mean", 1), ("norm", 0), ("var", 1)):
                if 0 <= n - back < len(units):
                    order.append((x, n - back))
            if n < len(units):
                order += [(x, n) for x in steps[2:-2]]
        ring = Ring(core, sig, order, 3, shade,
                    {(x, n): c for x, c in table.items() for n in range(len(units))})
        gt, fin = (nc.alloc_sbuf_tensor_at(f"rwkv_{x}", [P, H], F32, offset=OFF_TAIL + 2 * KB * i)[:, :]
                   for i, x in enumerate(("g", "out")))
        block = ctx.enter_context(nc.Block())

        def need(eng, n, *names):
            for x in names:
                eng.wait_ge(sig[x], n + 1)

        @block.sync
        def _(sp):
            for dst, src in ((cst[:, :, :], k["rwkv_masks"]), (ident[:, :], k["ident"]), (heads[:, :], k["heads"]),
                             (hmean[:, :], k["head_mean"]), (ones[:, :], k["ones"]), (wa2[0:64, :], k["w2"]),
                             (wa2[64:128, :], k["a2"]), (g2[:, :], k["g2"]), (pc[:, :, 0:7], k["params"])):
                sp.dma_start(dst, src).then_inc(sig["consts"], 16)
            shade.load(sp)

        @block.tensor
        def _(pe):
            pe.wait_ge(sig["consts"], NCONST)
            pe.wait_ge(sig["squashed"], 2)
            def mean(n):
                b = ring.start(pe, "mean", n)
                need(pe, n, "out_y")
                pe.matmul(b[:, 0:H], hmean[:, :], y, start=True, stop=True).then_inc(sig["pe"], 1)

            def var(n):
                b = ring.start(pe, "var", n)
                need(pe, n, "sqy")
                pe.matmul(b[:, 0:H], hmean[:, :], sq, start=True, stop=True).then_inc(sig["pe"], 1)

            for n, (u, hf) in enumerate(units):
                cols = slice(hf * H, hf * H + H)
                feat = slice(u * P, u * P + P)

                def step(s, *needs):
                    b = ring.start(pe, s, n)
                    need(pe, n, *needs)
                    return b

                def each(b, lhs, rhs):
                    for h in range(2):
                        for j in range(4):
                            o = (4 * h + j) * P
                            last = pe.matmul(b[:, o:o + P], lhs(h, j), rhs(h, j), start=True, stop=True)
                    last.then_inc(sig["pe"], 1)

                def mats(s, lhs, rhs, *needs):
                    each(step(s, *needs), lambda h, j: lhs[:, 4 * h + j, :], lambda h, j: rhs[:, 4 * h + j, :])

                def feats(s, lhs, rhs, *needs):
                    each(step(s, *needs), lambda h, j: tk(lhs, j)[64 * h:64 * h + 64, :],
                         lambda h, j: tk(rhs, j)[64 * h:64 * h + 64, :])

                b = step("wa")
                pe.matmul(b[:, 0:H], wa2[0:64, feat], z[0:64, wa_, cols], start=True, stop=True)
                pe.matmul(b[:, H:2 * H], wa2[64:128, feat], z[64:128, wa_, cols], start=True, stop=True
                          ).then_inc(sig["pe"], 1)
                if n:
                    mean(n - 1)
                b = step("norm", "sqk")
                pe.matmul(b[:, 0:H], heads[:, :], tmp, start=True, stop=True).then_inc(sig["pe"], 1)
                if n:
                    var(n - 1)
                for s, (x0, x1), needs in (("tr1", (a0f, b0f), ("a0f", "b0f")), ("tr2", (k0f, z[:, v_ + u, cols]), ("k0f",))):
                    b = step(s, *needs)
                    for j in range(4):
                        pe.transpose(tk(b, j), tk(x0, j), ident[:, :])
                    for j in range(4):
                        last = pe.transpose(tk(b, 4 + j), tk(x1, j), ident[:, :])
                    last.then_inc(sig["pe"], 1)
                feats("L", al, be, "al", "be")
                feats("N", be, al)
                feats("M", ka, al, "ka")
                feats("RK", ka, rh, "rh")
                feats("RB", be, rh)
                mats("J2", jt, jj, "out_L", "out_J")
                mats("J2t", jj, jt)
                mats("X2", j2t, xx, "out_J2t", "out_N")
                mats("J4", j2t, j2, "out_J2")
                mats("J4t", j2, j2t)
                mats("X4", j4t, xx, "out_J4t", "out_X2")
                mats("J8t", j4, j4t, "out_J4")
                mats("X8", j8t, xx, "out_J8t", "out_X4")
                before = "out_X8"
                for lv, lm in ((16, l16), (32, l32), (64, l64)):
                    b = step(f"T{lv}", before)
                    for i in range(8):
                        last = pe.transpose(b[:, i * P:i * P + P], xx[:, i, :], ident[:, :])
                    last.then_inc(sig["pe"], 1)
                    mats(f"W{lv}", lm, xx)
                    mats(f"Y{lv}", xt, ww, f"out_T{lv}", f"out_W{lv}")
                    before = f"out_Y{lv}"

                def heads64(b, half, lhs, rhs):
                    for j in range(4):
                        for h in range(2):
                            o = half * H + j * P + 64 * h
                            last = pe.matmul(b[:, o:o + 64], lhs[:, 4 * h + j, :], rhs(j, h), start=True, stop=True)
                    return last
                b = step("TA", before, "out_tr1", "out_tr2", "out_M")
                heads64(b, 0, xx, lambda j, h: at_[:, j, 64 * h:64 * h + 64])
                heads64(b, 1, mt, lambda j, h: vt[:, j, 64 * h:64 * h + 64]).then_inc(sig["pe"], 1)
                b = step("TAt", "out_TA")
                for j in range(4):
                    for h in range(2):
                        pe.matmul(b[64 * h:64 * h + 64, j * P:j * P + P], at_[:, j, 64 * h:64 * h + 64],
                                  xx[:, 4 * h + j, :], start=True, stop=True)
                heads64(b, 1, xx, lambda j, h: tk(mv, j)[:, 64 * h:64 * h + 64]).then_inc(sig["pe"], 1)
                b = step("PP", "out_TAt")
                for j in range(4):
                    pe.matmul(tk(b, j), tk(ta, j), bt[:, j, :], start=True, stop=True)
                for j in range(4):
                    pe.matmul(tk(b, 4 + j), kt[:, j, :], vt[:, j, :], start=True, stop=False)
                    last = pe.matmul(tk(b, 4 + j), bt[:, j, :], tk(tmv, j), start=False, stop=True)
                last.then_inc(sig["pe"], 1)
                for j in range(4):
                    b = step(f"c{j}", "phi", "psi", "carried" if j == 0 else f"out_c{j - 1}")
                    pe.matmul(b[:, 0:P], tk(phi, j), xs[:, j, :], start=True, stop=True).then_inc(sig["pe"], 1)
                b = step("U")
                for j in range(4):
                    last = pe.matmul(tk(b, j), tk(tat, j), xs[:, j, :], start=True, stop=True)
                last.then_inc(sig["pe"], 1)
                b = step("y", "out_U", "out_RK", "out_RB", "r0")
                for j in range(4):
                    for h in range(2):
                        dst = b[64 * h:64 * h + 64, j * P:j * P + P]
                        hc = slice(64 * h, 64 * h + 64)
                        pe.matmul(dst, xs[:, j, hc], tk(z[:, k_ + u, cols], j), start=True, stop=False)
                        pe.matmul(dst, vt[:, j, hc], rk[:, 4 * h + j, :], start=False, stop=False)
                        last = pe.matmul(dst, tk(uu, j)[:, hc], rb[:, 4 * h + j, :], start=False, stop=True)
                last.then_inc(sig["pe"], 1)
                b = step("bg", "bonus")
                pe.matmul(b[:, 0:H], heads[:, :], z[:, r_ + u, cols], start=True, stop=True)
                pe.matmul(b[:, H:2 * H], g2[:, feat], z[:, gl_, cols], start=True, stop=True).then_inc(sig["pe"], 1)
            mean(len(units) - 1)
            var(len(units) - 1)

        @block.scalar
        def _(act):
            act.activation(z[0:64, wa_, :], z[0:64, wa_, :], ACT.Tanh).then_inc(sig["squashed"], 1)
            act.activation(z[:, gl_, :], z[:, gl_, :], ACT.Sigmoid).then_inc(sig["squashed"], 1)
            act.wait_ge(sig["consts"], NCONST)
            act.wait_ge(sig["eps"], 2)
            def output_squares(n):
                need(act, n, "out_mean")
                act.activation(sq, y, ACT.Square).then_inc(sig["sqy"], 1)

            def output_deviation(n):
                b = ring.full(act, "var", n)
                act.activation(sd, b[:, 0:H], ACT.Sqrt, bias=epst[:, 1:2]).then_inc(sig["out_var"], 1)

            def output_hi(n):
                u, hf = units[n]
                need(act, n, "fin")
                act.activation(yh[:, y0 + u, hf * H:hf * H + H], fin, ACT.Copy).then_inc(sig["yh"], 1)

            for n, (u, hf) in enumerate(units):
                if n == 0:
                    shade.split_hi(act, 0)
                    shade.split_hi(act, 1)

                def copy(s, dst, lo=0, hi=2 * H, signal=None, scale=1.0):
                    b = ring.full(act, s, n)
                    act.activation(dst, b[:, lo:hi], ACT.Copy, scale=scale).then_inc(sig[signal or "out_" + s], 1)

                b = ring.full(act, "wa", n)
                act.activation(lw, b[:, 0:H], ACT.Sigmoid, bias=pc[:, u, W0:W0 + 1]).then_inc(sig["w_sig"], 1)
                act.activation(a, b[:, H:2 * H], ACT.Sigmoid, bias=pc[:, u, A0:A0 + 1]).then_inc(sig["out_wa"], 1)
                if n:
                    output_squares(n - 1)
                need(act, n, "kk0")
                act.activation(tmp, kk, ACT.Square).then_inc(sig["sqk"], 1)
                b = ring.full(act, "norm", n)
                act.activation(tmp, b[:, 0:H], ACT.Sqrt, bias=epst[:, 0:1]).then_inc(sig["out_norm"], 1)
                if n:
                    output_deviation(n - 1)
                need(act, n, "d1", "d3", "dm")
                act.activation(e1, e1, ACT.Exp).then_inc(sig["e1"], 1)
                act.activation(e2, e3, ACT.Exp, scale=-1.0).then_inc(sig["e2"], 1)
                act.wait_ge(sig["e2"], n + 1)
                act.activation(e3, e3, ACT.Exp).then_inc(sig["e3"], 1)
                c3 = j4v(c)
                act.activation(em[:, :], c3[:, :, P // 2 - 1], ACT.Exp).then_inc(sig["em"], 1)
                act.activation(ecm[:, :], ecm[:, :], ACT.Exp).then_inc(sig["ecm"], 1)
                act.activation(eend[:, :], c3[:, :, P - 1], ACT.Exp).then_inc(sig["eend"], 1)
                shade.take(act, 3 * n)
                copy("tr1", flat(at_[:, :, :]), 0, H, "at")
                copy("tr1", flat(bt[:, :, :]), H, 2 * H, scale=-1.0)
                copy("tr2", flat(kt[:, :, :]), 0, H, "kt")
                copy("tr2", flat(vt[:, :, :]), H, 2 * H)
                shade.split_hi(act, 3 * n + 2)
                if n:
                    output_hi(n - 1)
                copy("J2", flat(j2[:, :, :]))
                copy("J2t", flat(j2t[:, :, :]))
                copy("J4", flat(j4[:, :, :]))
                copy("J4t", flat(j4t[:, :, :]))
                copy("J8t", flat(j8t[:, :, :]))
                for lv in (16, 32, 64):
                    copy(f"T{lv}", flat(xt[:, :, :]))
                    copy(f"W{lv}", flat(ww[:, :, :]))
                    if lv == 16:
                        shade.take(act, 3 * n + 1)
                        shade.split_hi(act, 3 * n + 3)
                copy("TA", flat(j4[:, :, :]))
                copy("TAt", flat(j4t[:, :, :]))
                copy("y", y, 0, H)
                copy("bg", gt, H, 2 * H, "gate")
                shade.take(act, 3 * n + 2)
                shade.split_hi(act, 3 * n + 4)
            output_squares(len(units) - 1)
            output_deviation(len(units) - 1)
            output_hi(len(units) - 1)

        @block.vector
        def _(dve):
            dve.memset(epst[:, 0:1], 1e-12).then_inc(sig["eps"], 1)
            dve.memset(epst[:, 1:2], 64e-5).then_inc(sig["eps"], 1)
            dve.wait_ge(sig["consts"], NCONST)
            dve.tensor_scalar(pc[:, :, OMKA], pc[:, :, K_A], -1.0, 1.0, ALU.mult, ALU.add).then_inc(sig["omka"], 1)
            dve.wait_ge(sig["omka"], 1)

            def centre(n):
                need(dve, n, "out_y")
                b = ring.full(dve, "mean", n)
                dve.tensor_tensor(y, y, b[:, 0:H], ALU.subtract).then_inc(sig["out_mean"], 1)

            def output(n):
                par = lambda i: pc[:, units[n][0], i:i + 1]
                need(dve, n, "out_var", "out_mean")
                dve.reciprocal(sd, sd).then_inc(sig["rsd"], 1)
                need(dve, n, "sqy", "rsd")
                dve.tensor_tensor(y, y, sd, ALU.mult).then_inc(sig["yn"], 1)
                need(dve, n, "yn")
                dve.tensor_scalar(y, y, par(LN_W), par(LN_B), ALU.mult, ALU.add).then_inc(sig["yw"], 1)
                need(dve, n, "yw", "bv")
                dve.tensor_tensor(y, y, bv, ALU.add).then_inc(sig["yb"], 1)
                need(dve, n, "yb", "gate")
                if n:
                    dve.wait_ge(sig["unit"], n)
                dve.tensor_tensor(fin, y, gt, ALU.mult).then_inc(sig["fin"], 1)

            for n, (u, hf) in enumerate(units):
                cols = slice(hf * H, hf * H + H)
                r, kin, v = z[:, r_ + u, cols], z[:, k_ + u, cols], z[:, v_ + u, cols]

                def par(i):
                    return pc[:, u, i:i + 1]

                def mul(out, x, y_, signal, *needs):
                    need(dve, n, *needs)
                    dve.tensor_tensor(out, x, y_, ALU.mult).then_inc(sig[signal], 1)

                if n:
                    ring.full(dve, "y", n - 1)
                if hf:
                    dve.tensor_copy(xs[:, 0, :], xs[:, 4, :]).then_inc(sig["carried"], 1)
                else:
                    dve.memset(xs[:, 0, :], 0.0).then_inc(sig["carried"], 1)
                dve.tensor_scalar(kk, kin, par(K_K), None, ALU.mult).then_inc(sig["kk0"], 1)
                if n:
                    centre(n - 1)
                need(dve, n, "w_sig", "out_wa")
                dve.tensor_scalar(lw, lw, -RWKV_DECAY, None, ALU.mult).then_inc(sig["lw"], 1)
                dve.tensor_scalar(kp, a, par(K_A), par(OMKA), ALU.mult, ALU.add).then_inc(sig["ka_"], 1)
                need(dve, n, "lw")
                for j in range(4):
                    last = dve.tensor_tensor_scan(out=tk(c, j), data0=ones[:, :], data1=tk(lw, j), initial=0.0,
                                                  op0=ALU.mult, op1=ALU.add)
                    last.then_inc(sig["scan"], 1)
                mul(kp, kp, kin, "kp", "ka_")
                dve.wait_ge(sig["scan"], 4 * n + 4)
                c3 = j4v(c)
                mid = bcl(c3[:, :, P // 2 - 1], P)
                dve.tensor_tensor(e1, c, lw, ALU.subtract).then_inc(sig["d1_"], 1)
                dve.tensor_tensor(j4v(e3), c3, mid, ALU.subtract).then_inc(sig["d3"], 1)
                dve.tensor_tensor(ecm[:, :], c3[:, :, P - 1], c3[:, :, P // 2 - 1], ALU.subtract).then_inc(sig["dm"], 1)
                need(dve, n, "d1_")
                dve.tensor_tensor(j4v(e1), j4v(e1), mid, ALU.subtract).then_inc(sig["d1"], 1)
                need(dve, n, "out_norm")
                dve.reciprocal(tmp, tmp).then_inc(sig["rn"], 1)
                mul(kk, kk, tmp, "kk", "rn")
                mul(al, kk, e1, "al", "kk", "e1")
                mul(a, kk, a, "kka")
                mul(be, a, e2, "be", "kka", "e2")
                mul(ka, kp, e2, "ka", "kp")
                mul(rh, r, e3, "rh", "e3")
                need(dve, n, "ecm", "be", "ka", "al")
                dve.tensor_tensor(j4v(b0f), j4v(be), bcl(ecm[:, :], P), ALU.mult).then_inc(sig["b0f"], 1)
                dve.tensor_tensor(j4v(k0f), j4v(ka), bcl(ecm[:, :], P), ALU.mult).then_inc(sig["k0f"], 1)
                need(dve, n, "em", "rh")
                dve.tensor_tensor(j4v(a0f), j4v(al), bcl(em[:, :], P), ALU.mult).then_inc(sig["a0f"], 1)
                if n:
                    output(n - 1)

                def masked(s, dst, m, signal=None):
                    b = ring.full(dve, s, n)
                    dve.tensor_tensor(dst[:, :, :], b.rearrange("p (j t) -> p j t", t=P), bc(cst[:, m, :], 8),
                                      ALU.mult).then_inc(sig[signal or "out_" + s], 1)
                need(dve, n, "a0f", "b0f", "k0f", "bonus", "eend")
                if n:
                    need(dve, n - 1, "fin")
                masked("L", l16, M_L16, "l16")
                masked("L", l32, M_L32, "l32")
                masked("L", l64, M_L64, "l64")
                masked("L", jt, M_JT)
                masked("N", jj, M_J, "out_J")
                need(dve, n, "out_J")
                dve.tensor_tensor(xx[:, :, :], bc(ident[:, :], 8), jj[:, :, :], ALU.subtract).then_inc(sig["out_N"], 1)
                masked("M", mt, M_SU)
                masked("RK", rk, M_IU)
                masked("RB", rb, M_IU)
                need(dve, n, "out_N")
                x = flat(xx[:, :, :])

                def update(s, op):
                    b = ring.full(dve, s, n)
                    dve.tensor_tensor(x, x, b, op).then_inc(sig["out_" + s], 1)
                    need(dve, n, "out_" + s)
                for s in ("X2", "X4", "X8"):
                    update(s, ALU.add)
                for lv in (16, 32, 64):
                    update(f"Y{lv}", ALU.subtract)
                b = ring.full(dve, "PP", n)
                dve.tensor_tensor(j4v(phi), j4v(b[:, 0:H]), bc(heads[:, :], 4), ALU.mult).then_inc(sig["phi_"], 1)
                dve.tensor_tensor(j4v(psi), j4v(b[:, H:2 * H]), bc(heads[:, :], 4), ALU.mult).then_inc(sig["psi"], 1)
                need(dve, n, "phi_", "psi", "dg")
                dve.tensor_tensor(phi, phi, dg, ALU.add).then_inc(sig["phi"], 1)
                need(dve, n, "phi")
                dve.sem_inc(sig["out_PP"], 1)
                for j in range(4):
                    b = ring.full(dve, f"c{j}", n)
                    dve.tensor_tensor(xs[:, j + 1, :], b[:, 0:P], tk(psi, j), ALU.add).then_inc(sig[f"out_c{j}"], 1)
                b = ring.full(dve, "U", n)
                need(dve, n, "out_TAt")
                dve.scalar_tensor_tensor(out=uu, in0=b[:, 0:H], scalar=-1.0, in1=tmv, op0=ALU.mult,
                                         op1=ALU.subtract).then_inc(sig["out_U"], 1)
                b = ring.full(dve, "bg", n)
                dve.tensor_tensor(bv, b[:, 0:H], v, ALU.mult).then_inc(sig["bv"], 1)
                need(dve, n, "bv", "gate")
                dve.sem_inc(sig["out_bg"], 1)
            centre(len(units) - 1)
            output(len(units) - 1)

        @block.gpsimd
        def _(pool):
            def output_lo(n):
                u, hf = units[n]
                cols = slice(hf * H, hf * H + H)
                need(pool, n, "yh")
                pool.tensor_tensor(yl[:, y0 + u, cols], fin, yh[:, y0 + u, cols].bitcast(F32), ALU.subtract
                                   ).then_inc(sig["unit"], 1)

            for n, (u, hf) in enumerate(units):
                cols = slice(hf * H, hf * H + H)
                r = z[:, r_ + u, cols]
                if n == 0:
                    shade.split_lo(pool, 0)
                    shade.split_lo(pool, 1)
                need(pool, n, "rh", "em", "kp", "kk0")
                pool.tensor_tensor(j4v(z[:, k_ + u, cols]), j4v(rh), bcl(em[:, :], P), ALU.mult).then_inc(sig["r0"], 1)
                pool.tensor_scalar(r, r, pc[:, u, R_K:R_K + 1], None, ALU.mult).then_inc(sig["rrk"], 1)
                need(pool, n, "rrk")
                pool.tensor_tensor(r, r, kp, ALU.mult).then_inc(sig["bonus"], 1)
                if n:
                    output_lo(n - 1)
                shade.split_lo(pool, 3 * n + 2)
                ring.full(pool, "TA", n)
                need(pool, n, "eend")
                pool.tensor_tensor(j4v(dg), bc(ident[:, :], 4), bcl(eend[:, :], P), ALU.mult).then_inc(sig["dg"], 1)
                shade.split_lo(pool, 3 * n + 3)
                shade.split_lo(pool, 3 * n + 4)
            output_lo(len(units) - 1)


def attention_phase(nc, core, mem, qks, vs, scratch, k, shaded):
    ob, bias = mem("out", [P, 2, NC, 4, 66]), mem("bias", [P, 2, 2, P])
    sb, pt = mem("scores", [P, 2, 4, 2 * P]), mem("probs_t", [P, 2, 8, P])
    ident, neg = mem("ident", [P, P]), mem("neg_max", [P, 2, 4])
    ps = core.ps
    units = [(g, h, hf) for g in range(3) for h in range(4) for hf in range(2)]
    N = len(units)

    def before(g, j):
        return (g == 0 and j > 0) or (g == 1 and j % 2 == 1)

    def spans(g, hf):
        return {0: [(slice(1, 4), slice(0, 1)), (slice(0, 4), None)][hf], 1: (slice(1, 4, 2), slice(0, 4, 2)),
                2: (None, slice(0, 4))}[g]

    def blocks(g, hf):
        return [(i, b) for i in range(4) for b in range(2) if b or before(g, 4 * hf + i)]

    def tokens(g, buf, tile, row, first, n=1):
        x = buf[row:row + 64, tile, :]
        if g == 0:
            return x[:, first * P:(first + n) * P]
        if g == 1:
            z, nb = first // 2, first % 2
            return x.rearrange("p (l z) -> p z l", z=4)[:, z, nb * P:(nb + n) * P]
        return x.rearrange("p (l z) -> p z l", z=8)[:, first, :]

    with ExitStack() as ctx:
        sig = ctx.enter_context(Signals(nc, "att"))
        shade = AttentionShade(core, sig, *shaded)
        early = [n + n // 3 for n in range(N)]
        late = [n + n // 3 + 1 if n % 3 == 2 else None for n in range(N)]
        block = ctx.enter_context(nc.Block())

        def s_bank(n):
            return ps[:, 2 * (n % 2):2 * (n % 2) + 2, :].rearrange("p a (b c) -> p (a b) c", b=2)

        t_bank = ps[:, 4:6, :].rearrange("p a (b c) -> p (a b) c", b=4)

        def o_bank(n):
            return ps[:, 6, 256 * (n % 2):256 * (n % 2) + 256].rearrange("p (j e) -> p j e", j=4)

        @block.sync
        def _(sp):
            sp.dma_start(ident[:, :], k["ident"]).then_inc(sig["ident"], 16)
            for h in range(14):
                if h >= 2:
                    sp.wait_ge(sig["scored"], 2 * min(h - 1, 12))
                if h < 12:
                    sp.dma_start(bias[:, h % 2], k["att_bias"][:, h]).then_inc(sig[f"bias{h % 2}"], 16)
                if h % 4 == 1 and h > 1:
                    g = h // 4 - 1
                    sp.wait_ge(sig["o_out"], 8 * (g + 1))
                    sp.wait_ge(sig["exp"], 8 * (g + 1))
                    src = ob[:, g % 2].rearrange("p j h e -> p j (h e)")
                    dst = scratch[:, g, :]
                    if g == 0:
                        sp.dma_start(dst.rearrange("(j p) c -> p j c", p=P), src).then_inc(sig["stored0"], 16)
                    elif g == 1:
                        v = dst.rearrange("(b p z) c -> z b p c", b=2, z=4)
                        for j in range(NC):
                            sp.dma_start(v[j // 2, j % 2], src[:, j]).then_inc(sig["stored1"], 16)
                    else:
                        sp.dma_start(dst.rearrange("(p j) c -> p j c", j=NC), src).then_inc(sig["stored2"], 16)
            sp.wait_ge(sig["stored0"], 16)
            sp.wait_ge(sig["stored1"], 16 * NC)
            sp.wait_ge(sig["stored2"], 16)

        @block.tensor
        def _(pe):
            def scores(n):
                g, h, hf = units[n]
                row, tile = 64 * (h % 2), h // 2
                if n >= 2:
                    pe.wait_ge(sig["scored"], n - 1)
                b = s_bank(n)
                for i in range(4):
                    j = 4 * hf + i
                    q = tokens(g, qks[g], tile, row, j)
                    if before(g, j):
                        last = pe.matmul(b[:, i, :], q, tokens(g, qks[g], 2 + tile, row, j - 1, 2), start=True, stop=True)
                    else:
                        last = pe.matmul(b[:, i, P:2 * P], q, tokens(g, qks[g], 2 + tile, row, j), start=True, stop=True)
                last.then_inc(sig["s"], 1)

            pe.wait_ge(sig["ident"], 16)
            scores(0)
            for n, (g, h, hf) in enumerate(units):
                if n + 1 < N:
                    scores(n + 1)
                shade.half(pe, early[n], 0, 4)
                pe.wait_ge(sig["exp"], n + 1)
                if n:
                    pe.wait_ge(sig["t_out"], n)
                for i, b in blocks(g, hf):
                    last = pe.transpose(t_bank[:, 2 * i + b, :], sb[:, n % 2, i, b * P:b * P + P], ident[:, :])
                last.then_inc(sig["t"], 1)
                shade.half(pe, early[n], 4)
                if late[n] is not None:
                    shade.half(pe, late[n])
                pe.wait_ge(sig["t_out"], n + 1)
                if n:
                    pe.wait_ge(sig["o_out"], n)
                for i in range(4):
                    j = 4 * hf + i
                    have = [b for ii, b in blocks(g, hf) if ii == i]
                    for b in have:
                        last = pe.matmul(o_bank(n)[:, i, :], pt[:, n % 2, 2 * i + b, :],
                                         vs[g][:, j - 1 + b, 64 * h:64 * h + 64], start=(b == have[0]), stop=(b == 1))
                last.then_inc(sig["o"], 1)

        def tout(dve, n):
            g, h, hf = units[n]
            full, own = spans(g, hf)
            dve.wait_ge(sig["t"], n + 1)
            if n >= 2:
                dve.wait_ge(sig["o"], n - 1)
            tb = t_bank.rearrange("p (i b) c -> p i b c", b=2)
            pv = pt[:, n % 2].rearrange("p (i b) c -> p i b c", b=2)
            if full is not None:
                last = dve.tensor_copy(pv[:, full], tb[:, full])
                if own is not None:
                    last.then_inc(sig["t_part"], 1)
            if own is not None:
                last = dve.tensor_copy(pv[:, own, 1, :], tb[:, own, 1, :])
            last.then_inc(sig["t_out"], 1)

        @block.vector
        def _(dve):
            for n, (g, h, hf) in enumerate(units):
                head = 4 * g + h
                full, own = spans(g, hf)
                dve.wait_ge(sig[f"bias{head % 2}"], 16 * (head // 2 + 1))
                dve.wait_ge(sig["s"], n + 1)
                if n >= 2:
                    dve.wait_ge(sig["t"], n - 1)
                if own is not None and g < 2:
                    dve.memset(sb[:, n % 2, own, 0:P], NEG).then_inc(sig["filled"], 1)
                else:
                    dve.sem_inc(sig["filled"], 1)
                b = s_bank(n)
                bi = bias[:, head % 2].rearrange("p a b -> p (a b)")
                last = None
                for part, c0 in ((full, 0), (own, P)):
                    if part is None:
                        continue
                    if last is not None:
                        last.then_inc(sig["scored_part"], 1)
                    m = len(range(*part.indices(4)))
                    last = dve.scalar_tensor_tensor(out=sb[:, n % 2, part, c0:2 * P], in0=b[:, part, c0:2 * P],
                                                    scalar=0.125, in1=bc(bi[:, c0:2 * P], m), op0=ALU.mult, op1=ALU.add)
                last.then_inc(sig["scored"], 1)
                dve.wait_ge(sig["scored"], n + 1)
                dve.wait_ge(sig["filled"], n + 1)
                c0 = P if g == 2 else 0
                if g == 2 and h == 0 and hf == 0:
                    dve.wait_ge(sig["stored0"], 16)
                mx = ob[:, g % 2, 4 * hf:4 * hf + 4, h, 64]
                dve.tensor_reduce(mx, sb[:, n % 2, :, c0:2 * P], AX, ALU.max).then_inc(sig["max"], 1)
                dve.wait_ge(sig["max"], n + 1)
                dve.tensor_scalar(neg[:, n % 2, :], mx, -1.0, None, ALU.mult).then_inc(sig["neg"], 1)
                if n:
                    tout(dve, n - 1)
            tout(dve, N - 1)

        @block.scalar
        def _(act):
            def o_out(n):
                g, h, hf = units[n]
                act.wait_ge(sig["o"], n + 1)
                act.activation(ob[:, g % 2, 4 * hf:4 * hf + 4, h, 0:64], o_bank(n), ACT.Copy).then_inc(sig["o_out"], 1)

            shade.start(act)
            for n, (g, h, hf) in enumerate(units):
                act.wait_ge(sig["neg"], n + 1)
                c0 = P if g == 2 else 0
                for i in range(4):
                    ins = act.activation(sb[:, n % 2, i, c0:2 * P], sb[:, n % 2, i, c0:2 * P], ACT.Exp,
                                         bias=neg[:, n % 2, i:i + 1], accum_out=ob[:, g % 2, 4 * hf + i, h, 65:66])
                    ins.then_inc(sig["exp" if i == 3 else "exp_part"], 1)
                if n:
                    o_out(n - 1)
                    if late[n - 1] is not None:
                        shade.take(act, late[n - 1])
                shade.take(act, early[n])
            shade.take(act, late[N - 1])
            o_out(N - 1)
            shade.end(act)

        @block.gpsimd
        def _(pool):
            shade.split_all_lo(pool)


class Chain:

    def __init__(self, dve, sem):
        self.dve, self.sem, self.count = dve, sem, 0

    def __call__(self, ins):
        self.count += 1
        ins.then_inc(self.sem, 1)
        self.dve.wait_ge(self.sem, self.count)


class MergeAndPool:

    def __init__(self, core, sig, mem, scratch, ah, al, pz, k):
        self.core, self.sig, self.scratch, self.ah, self.al, self.pz, self.k = core, sig, scratch, ah, al, pz, k
        self.groups = mem("groups", [P, NC, 3, 4 * 66])
        self.w, self.r = mem("weights", [P, 3, NC, 4]), mem("sums", [P, 3, NC, 4])
        self.acc, self.tmp, self.ident = mem("merged", [P, NC, 256]), mem("term", [P, NC, 256]), mem("ident", [P, P])
        self.fix = mem("fix", [PG, 4, 16])

    def sync(self, sp):
        sp.dma_start(self.groups[:, :, :, :], self.scratch.rearrange("(j p) g c -> p j g c", p=P)
                     ).then_inc(self.sig["in"], 16)
        sp.dma_start(self.ident[:, :], self.k["ident"]).then_inc(self.sig["in"], 16)
        sp.dma_start(self.fix[:, :, :], self.k["pool_fix"]).then_inc(self.sig["in"], 16)

    def vector(self, dve):
        sig, w, r, acc, tmp = self.sig, self.w, self.r, self.acc, self.tmp
        self.link = link = Chain(dve, sig["chain"])
        grp = self.groups[:, :, :, :].rearrange("p j g (h e) -> p j g h e", e=66)
        dve.wait_ge(sig["in"], 48)
        m = [grp[:, :, g, :, 64] for g in range(3)]
        s = [grp[:, :, g, :, 65] for g in range(3)]
        top = r[:, 0]
        link(dve.tensor_tensor(top, m[0], m[1], ALU.max))
        link(dve.tensor_tensor(top, top, m[2], ALU.max))
        for g in range(3):
            ins = dve.tensor_tensor(w[:, g], m[g], top, ALU.subtract)
            if g < 2:
                link(ins)
        ins.then_inc(sig["diff"], 1)
        dve.wait_ge(sig["e"], 1)
        link(dve.tensor_tensor(r[:, 0], w[:, 0], s[0], ALU.mult))
        for g in (1, 2):
            link(dve.tensor_tensor(r[:, 1], w[:, g], s[g], ALU.mult))
            link(dve.tensor_tensor(r[:, 0], r[:, 0], r[:, 1], ALU.add))
        link(dve.reciprocal(r[:, 2], r[:, 0]))
        for g in range(3):
            link(dve.tensor_tensor(w[:, g], w[:, g], r[:, 2], ALU.mult))
        for g in range(3):
            for j in range(NC):
                dst = (acc if g == 0 else tmp)[:, j, :].rearrange("p (h e) -> p h e", e=64)
                link(dve.tensor_tensor(dst, grp[:, j, g, :, 0:64], bcl(w[:, g, j, :], 64), ALU.mult))
            if g:
                link(dve.tensor_tensor(acc[:, :, :], acc[:, :, :], tmp[:, :, :], ALU.add))
        dve.sem_inc(sig["merged"], 1)

    def vector_tile(self, dve, tile):
        win, pz, link = POOL_WIN[tile // 2], self.pz, self.link
        src, d, b = pz[:, tile, :], 1, 0
        while d < win:
            dst = self.core.gate[0:PG, b, :]
            link(dve.tensor_tensor(dst[:, d:T], src[:, d:T], src[:, 0:T - d], ALU.add))
            link(dve.tensor_copy(dst[:, 0:d], src[:, 0:d]))
            src, d, b = dst, 2 * d, 1 - b
        link(dve.tensor_tensor(src[:, 0:16], src[:, 0:16], self.fix[:, tile // 2, :], ALU.mult))
        link(dve.scalar_tensor_tensor(out=pz[:, tile, :], in0=src, scalar=1.0 / win, in1=pz[:, tile, :],
                                      op0=ALU.mult, op1=ALU.subtract))

    def vector_end(self, dve):
        dve.wait_ge(self.sig["hi"], 1)
        for h in range(2):
            dve.tensor_tensor(self.al[:, h, :], self.core.slot(2 + h), self.ah[:, h, :].bitcast(F32), ALU.subtract)

    def scalar_out(self, act, r, s):
        if (r, s) == (0, 1):
            act.wait_ge(self.sig["diff"], 1)
            act.activation(self.w[:, :, :, :], self.w[:, :, :, :], ACT.Exp).then_inc(self.sig["e"], 1)

    def scalar_end(self, act):
        act.wait_ge(self.sig["t"], 1)
        act.activation(self.ah[:, :, :], self.core.ps[:, 4:8, :].rearrange("p (h a) b -> p h (a b)", h=2), ACT.Copy
                       ).then_inc(self.sig["hi"], 1)

    def tensor(self, pe):
        pe.wait_ge(self.sig["merged"], 1)
        for h in range(2):
            for j in range(NC):
                last = pe.transpose(self.core.ps[:, 4 + 2 * h + j // 4, (j % 4) * P:(j % 4) * P + P],
                                    self.acc[:, j, h * P:h * P + P], self.ident[:, :])
        last.then_inc(self.sig["t"], 1)


def pool_phase(nc, core, mem, pz, ph, pl, a, ahead):
    wg, sc = mem("w_grp", [PG, 8, 2 * PG]), mem("scale", [PG, 8])
    with ExitStack() as ctx:
        sig = ctx.enter_context(Signals(nc, "pool"))
        fetch = Strips(core, sig, [], ahead=ahead)
        block = ctx.enter_context(nc.Block())

        @block.sync
        def _(sp):
            sp.dma_start(wg[:, :, :], a["w_pool_grp_2"]).then_inc(sig["consts"], 16)
            sp.dma_start(sc[:, :], a["pool_scale_2"]).then_inc(sig["consts"], 16)
            fetch.load(sp)

        @block.gpsimd
        def _(pool):
            fetch.split_ahead(pool=pool)

        @block.vector
        def _(dve):
            for o in range(8):
                dve.wait_ge(sig["hi"], o + 1)
                dve.scalar_tensor_tensor(out=pl[0:PG, o, :], in0=core.slot(o % 2)[0:PG, :], scalar=sc[:, o:o + 1],
                                         in1=ph[0:PG, o, :].bitcast(F32), op0=ALU.mult, op1=ALU.subtract
                                         ).then_inc(sig["lo"], 1)

        @block.scalar
        def _(act):
            fetch.split_ahead(act=act)
            act.wait_ge(sig["consts"], 32)
            for o in range(8):
                act.wait_ge(sig["mixed"], o + 1)
                act.activation(ph[0:PG, o, :], core.slot(o % 2)[0:PG, :], ACT.Copy, scale=sc[:, o:o + 1]
                               ).then_inc(sig["hi"], 1)

        @block.tensor
        def _(pe):
            pe.wait_ge(sig["consts"], 32)
            for o in range(8):
                g, half = o // 2, o % 2
                if o >= 2:
                    pe.wait_ge(sig["lo"], o - 1)
                for h in range(2):
                    for kk in range(2):
                        last = pe.matmul(core.ps[0:PG, 2 * (o % 2) + h, :], wg[:, 2 * g + kk, half * PG:half * PG + PG],
                                         pz[:, 2 * g + kk, 512 * h:512 * h + 512], start=(kk == 0), stop=(kk == 1))
                last.then_inc(sig["mixed"], 1)


def second_block(nc, core, a, k, out, gates):
    xh, xl = x_parts(core)
    w = a["w_in_2"]
    qks = [nc.alloc_sbuf_tensor_at(f"qk{g}", [P, 4, T], F32, offset=OFF_S + 16 * KB * g) for g in range(3)]
    vs = [nc.alloc_sbuf_tensor_at(f"v{g}", [P, NC, 256], F32, offset=OFF_S + (48 + 8 * g) * KB) for g in range(3)]

    def order(g):
        def tokens(buf, kt, j):
            x = buf[:, kt, :]
            if g == 0:
                return x[:, j * P:j * P + P]
            if g == 1:
                return x.rearrange("p (l z) -> p z l", z=4)[:, j // 2, (j % 2) * P:(j % 2) * P + P]
            return x.rearrange("p (l z) -> p z l", z=8)[:, j, :]
        return tokens
    residual = nc.dram_tensor("residual", (D, T), F32, kind="Internal").ap()
    norm = (Space(nc, "rms_mix", (OFF_S + 32 * KB, OFF_S + 64 * KB)), k["mean"], a["norm_mix_g_2"], None, 1e-6)
    qk_runs = [Run(2, lambda j, s, g=g: col_strip(w, g * 256 + s * P, j * (ATT_W // P)), xh, xl) for g in range(3)]
    pool_runs = [Run(1, lambda j, s, g=g: col_strip(w, 3 * ATT_W + s * PG, 2 * g, width=PG), xh, xl, m=PG)
                 for g in reversed(range(4))]
    for g in range(3):
        project_phase(nc, core, f"qkv{g}",
                      [qk_runs[g]],
                      [into(qks[g], 0)], w_tok=lambda s, g=g: col_strip(w, 2 * ATT_W + g * 256, s), zv=vs[g],
                      tokens=order(g), norm=(norm, dict(keep=False, spill=residual)) if g == 0 else None,
                      fetched=g > 0, ahead=qk_runs[g + 1] if g < 2 else None)
    gate0 = 3 * ATT_W + 768
    scratch = nc.dram_tensor("attention", (T, 3, 4 * 66), F32, kind="Internal").ap()
    attention_phase(nc, core, Space(nc, "att", (OFF_A, OFF_A + 32 * KB), (OFF_T + 8 * KB, END)), qks, vs, scratch, k,
                    (w, gate0, gates, 2 * KT))
    ah = nc.alloc_sbuf_tensor_at("a_hi", [P, 2, T], F32R, offset=OFF_S)
    al = nc.alloc_sbuf_tensor_at("a_lo", [P, 2, T], F32R, offset=OFF_S + 8 * KB)
    pz = nc.alloc_sbuf_tensor_at("pool_z", [PG, 8, T], F32, offset=OFF_A)
    ph = nc.alloc_sbuf_tensor_at("pool_hi", [PG, 8, T], F32R, offset=OFF_S + 16 * KB)
    pl = nc.alloc_sbuf_tensor_at("pool_lo", [PG, 8, T], F32R, offset=OFF_S + 48 * KB)
    beside = lambda sig: MergeAndPool(core, sig, Space(nc, "beside", (OFF_S + 16 * KB, END)), scratch, ah, al, pz, k)
    project_phase(nc, core, "pool_in", pool_runs,
                  [lambda act, j, s, psum, g=g: act.activation(pz[:, 2 * g + s, :], psum[0:PG, :], ACT.Copy)
                   for g in reversed(range(4))], beside=beside)
    branches = [(a["w_att_out_2"], lambda kt: ah[:, kt, :], lambda kt: al[:, kt, :]),
                (a["w_pool_out_2"], lambda kt: ph[0:PG, kt, :], lambda kt: pl[0:PG, kt, :], PG)]
    pool_phase(nc, core, Space(nc, "pool", (OFF_S + 80 * KB, END)), pz, ph, pl, a, branch_run(*branches[0]))
    merge_phase(nc, core, "merge2", Space(nc, "merge2", (OFF_XH, OFF_A)), branches, gates, True,
                mix_out_run(a["w_out_2"]))
    mix_out_phase(nc, core, "out2", a["w_out_2"], residual=residual)
    mlp_phase(nc, core, "mlp", a["w_mlp_in_2"], a["w_mlp_out_2"], (k["mean"], a["norm_mlp_g_2"], None, 1e-6))
    norm_phase(nc, core, "rms_out", k["mean"], a["norm_final_g_2"], None, 1e-6, out=out)


def constants():
    i = np.arange(P)
    f = np.float32
    k = {"ident": np.eye(P, dtype=f), "ones": np.ones((P, P), f), "mean": np.full((P, P), 1.0 / D, f)}
    heads = (i[:, None] // 64 == i[None, :] // 64).astype(f)
    k["heads"], k["head_mean"] = heads, heads / f(64)
    s, t = i[:, None], i[None, :]
    lv = [((s // (2 * L) == t // (2 * L)) & (s % (2 * L) < L) & (t % (2 * L) >= L)) for L in LEVELS] + [s == t]
    k["levels"] = np.stack(lv, 1).astype(np.int32)
    slopes = np.exp2(-8.0 * (np.arange(12) + 1.0) / 12.0)
    bias = np.full((P, 12, 2, P), NEG)
    for h in range(12):
        dil = DIL[h // 4]
        if h < 8:
            for b in range(2):
                dist = s - t + P * (1 - b)
                bias[:, h, b] = np.where((dist >= 0) & (dist <= P), -slopes[h] * dist * dil, NEG)
        else:
            dist = s // 2 - t // 2
            bias[:, h, 1] = np.where((dist >= 0) & (s % 2 == t % 2), -slopes[h] * dist * dil, NEG)
    k["att_bias"] = bias.astype(f)
    k["pool_fix"] = np.broadcast_to(np.stack([w / np.minimum(np.arange(16) + 1.0, w) for w in POOL_WIN]), (PG, 4, 16)).astype(f)
    b16 = s // 16 == t // 16

    def low(L):
        return (s // (2 * L) == t // (2 * L)) & (s % (2 * L) >= L) & (t % (2 * L) < L)
    k["rwkv_masks"] = np.stack([(s > t) & b16, low(16), low(32), low(64), (s < t) & b16, s < t, s <= t], 1).astype(f)
    sel = np.zeros((2, P, P), f)
    swap = np.zeros((P, P), f)
    for h in range(4):
        for e in range(32):
            sel[h // 2, 32 * h + e, 64 * (h % 2) + e] = 1
    for e in range(0, P, 2):
        swap[e + 1, e], swap[e, e + 1] = -1, 1
    sc = f(32.0 ** -0.5)
    k["gla_sel"] = np.stack([sel[0] * sc, sel[1] * sc, sel[0], sel[1]], 1)
    k["ret_sel"] = np.stack([m for u in range(2) for m in (sel[u], swap @ sel[u], sel[u] * sc, swap @ sel[u] * sc)], 1)
    theta = (1.0 / (f(10000.0) ** np.linspace(0.0, 1.0, 16, dtype=f))).astype(f)
    ang = (np.arange(T, dtype=f)[:, None] * theta[None, :]).astype(f)
    rot = np.zeros((P, 2, T), f)
    for p in range(P):
        if p % 64 < 32:
            rot[p, 0], rot[p, 1] = np.cos(ang[:, p % 64 // 2]), np.sin(ang[:, p % 64 // 2])
    k["rot"] = rot
    lg = np.log1p(-np.exp2(-5.0 - np.arange(4)))
    k["ret_decay"] = np.stack([np.where(s <= t, np.exp(lg[h] * np.maximum(t - s, 0)), 0) for h in range(4)], 1).astype(f)
    lgp = np.stack([lg[2 * u + i // 64] for u in range(2)], 1)
    k["ret_xz"] = np.stack([np.exp(lgp[:, u:u + 1] * e) for u in range(2) for e in (t + 1.0, P - 1.0 - t)], 1).astype(f)
    k["ret_end"] = np.exp(lgp * P).astype(f)
    return k


def into(z, z0, func=ACT.Copy, rows=P):
    def out(act, j, s, psum):
        return act.activation(at(z, j * 2 + (z0 + s)), psum, func)
    return out


def program(nc, a, out):
    core = Core(nc)
    k = {n[2:]: v for n, v in a.items() if n.startswith("k_")}
    xh, xl = x_parts(core)
    w = a["w_in"]

    ln_in = ((Space(nc, "ln_in", (OFF_S, OFF_T)), k["mean"], a["ln_in_w"], a["ln_in_b"], 1e-5),
             dict(x_in=a["x"], keep=False))
    hgrn_run = Run(2, lambda j, s: col_strip(w, HGRN0 + s * P, j * 2), xh, xl)
    gla_run = Run(1, lambda j, s: col_strip(w, GLA0, s), xh, xl)
    ret_run = Run(1, lambda j, s: col_strip(w, RET0, s), xh, xl)
    yh = nc.alloc_sbuf_tensor_at("y_hi", [P, KT, T], F32R, offset=OFF_S)
    yl = nc.alloc_sbuf_tensor_at("y_lo", [P, KT, T], F32R, offset=OFF_S + 32 * KB)
    y_free = lambda lo, hi: [(OFF_S + 4 * KB * lo, OFF_S + 4 * KB * hi), (OFF_S + (32 + 4 * lo) * KB, OFF_S + (32 + 4 * hi) * KB)]

    gates = nc.dram_tensor("gates", (4 * D, T), F32, kind="Internal").ap()

    z = nc.alloc_sbuf_tensor_at("rwkv_z", [P, 8, T], F32, offset=OFF_A)
    mem = Space(nc, "rwkv", (OFF_S, OFF_S + 8 * KB), (OFF_S + 16 * KB, OFF_S + 40 * KB), (OFF_S + 48 * KB, END))
    mu, om = (nc.alloc_sbuf_tensor_at(n, [P, 8], F32, offset=OFF_T + 32 * i) for i, n in enumerate(("mu", "one_mu")))

    def mu_load(sp, sig):
        sp.dma_start(mu[:, :], a["rwkv_mu"]).then_inc(sig["mu"], 16)

    def mu_prepare(dve, sig):
        dve.wait_ge(sig["mu"], 16)
        return dve.tensor_scalar(om[:, :], mu[:, :], -1.0, 1.0, ALU.mult, ALU.add)

    def shifted(dve, r, j, s, psum):
        dst = at(z, j * 2 + s)[:, 1:T]
        return dve.scalar_tensor_tensor(out=dst, in0=psum[:, 0:T - 1], scalar=colat(mu, j * 2 + s), in1=dst,
                                        op0=ALU.mult, op1=ALU.add)
    project_phase(nc, core, "rwkv_in", [Run(4, lambda j, s: col_strip(w, RWKV0 + s * P, j * 2), xh, xl)],
                  [lambda act, j, s, psum: act.activation(at(z, j * 2 + s), psum, ACT.Copy, scale=colat(om, j * 2 + s))],
                  consts=(mu_load, mu_prepare), last_vector=shifted, norm=ln_in)
    rwkv_mixer(nc, core, mem, z, yh, yl, 2,
               dict(k, w2=a["rwkv_w2"], a2=a["rwkv_a2"], g2=a["rwkv_g2"], params=a["rwkv_params"]), hgrn_run, (w, gates, 0))

    z = nc.alloc_sbuf_tensor_at("hgrn_z", [P, 6, T], F32, offset=OFF_A)
    zv = nc.alloc_sbuf_tensor_at("hgrn_v", [P, NC, 256], F32, offset=OFF_A + 24 * KB)
    project_phase(nc, core, "hgrn_in",
                  [hgrn_run,
                   Run(1, lambda j, s: col_strip(w, HGRN0 + 768, s), xh, xl)],
                  [into(z, 0), into(z, 4, ACT.Silu)], w_tok=lambda s: col_strip(w, HGRN0 + 512, s), zv=zv, fetched=True)
    linear_mixer(nc, core, "hgrn", "hgrn", Space(nc, "hgrn", (OFF_T, END), *y_free(0, 2), *y_free(4, 6)),
                 z, zv, yh, yl, 6, k, gla_run, (w, gates, 12))
    z = nc.alloc_sbuf_tensor_at("gla_z", [P, 6, T], F32, offset=OFF_A)
    zv = nc.alloc_sbuf_tensor_at("gla_v", [P, NC, 256], F32, offset=OFF_A + 24 * KB)
    project_phase(nc, core, "gla_in",
                  [gla_run,
                   Run(1, lambda j, s: col_strip(w, GLA0 + 512, 0, rows=(D, P)[s]), xh, xl, nk=(KT, 1)),
                   Run(1, lambda j, s: col_strip(w, GLA0 + 528, s), xh, xl)],
                  [into(z, 0), lambda act, j, s, psum: act.activation(z[:, 2 + 3 * s, :], psum, ACT.Copy),
                   into(z, 3, ACT.Silu)],
                  w_tok=lambda s: col_strip(w, GLA0 + 256, s), zv=zv, fetched=True)
    linear_mixer(nc, core, "gla", "gla", Space(nc, "gla", (OFF_T, END), *y_free(0, 2)), z, zv, yh, yl, 4,
                 dict(k, gla_w2=a["gla_w2"], gla_b=a["gla_b"]), ret_run, (w, gates, 20))
    z = nc.alloc_sbuf_tensor_at("ret_z", [P, 4, T], F32, offset=OFF_A)
    zv = nc.alloc_sbuf_tensor_at("ret_v", [P, NC, 256], F32, offset=OFF_A + 16 * KB)
    project_phase(nc, core, "ret_in",
                  [ret_run,
                   Run(1, lambda j, s: col_strip(w, RET0 + 512, s), xh, xl)],
                  [into(z, 0), into(z, 2, ACT.Silu)], w_tok=lambda s: col_strip(w, RET0 + 256, s), zv=zv, fetched=True)
    ytile = lambda buf, n: (lambda k: buf[:, 2 * n + k, :])
    branches = [(a["w_branch"][n], ytile(yh, n), ytile(yl, n)) for n in range(4)]
    linear_mixer(nc, core, "ret", "ret", Space(nc, "ret", (OFF_T, END), (OFF_A + 24 * KB, OFF_A + 32 * KB)),
                 z, zv, yh, yl, 0, k, branch_run(*branches[0]), (w, gates, 28))
    merge_phase(nc, core, "merge", Space(nc, "merge", (OFF_T, END)), branches, gates, True,
                mix_out_run(a["w_mix_out"]))
    mix_out_phase(nc, core, "mix_out", a["w_mix_out"])
    ple_phase(nc, core, "ple", a["p"], a["w_ple_gate"], a["w_ple_proj"], (k["mean"], a["ln_mix_w"], a["ln_mix_b"], 1e-5),
              ffn_run(a["w_ffn_up"], 0, 8))
    ffn_phase(nc, core, "ffn", a["w_ffn_up"], a["ffn_conv"], a["w_ffn_down"])
    norm_phase(nc, core, "ln_ffn", k["mean"], a["ln_ffn_w"], a["ln_ffn_b"], 1e-5, split=False, sum_squares=True)
    second_block(nc, core, a, k, out, gates)


def tiles_of(v, m=P):
    return np.ascontiguousarray(v.reshape(-1, m).T)


def layout(i):
    c = np.ascontiguousarray
    a = {"x": c(i["x"][0].T), "w_in": i["w_in"][0]}
    for n in ("ln_in_w", "ln_in_b", "norm_final_g_2"):
        a[n] = tiles_of(i[n])
    for n in ("ln_mix_w", "ln_mix_b", "ln_ffn_w", "ln_ffn_b", "norm_mix_g_2", "norm_mlp_g_2"):
        a[n] = tiles_of(i[n][0])
    for n in ("w_branch", "w_mix_out", "w_ffn_up", "w_ffn_down", "w_ple_gate", "w_ple_proj", "w_in_2", "w_att_out_2",
              "w_pool_out_2", "w_out_2", "w_mlp_in_2", "w_mlp_out_2"):
        a[n] = i[n][0]
    a["p"] = c(i["p"][0, 0].T)
    a["ffn_conv"] = c(i["ffn_conv"][0].reshape(3, FF // P, P).transpose(2, 0, 1))
    a["w_pool_grp_2"] = c(i["w_pool_grp_2"][0].reshape(8, PG, 2 * PG).transpose(1, 0, 2))
    a["pool_scale_2"] = tiles_of(i["pool_scale_2"][0], PG)
    for n in ("w2", "a2", "g2"):
        a["rwkv_" + n] = i["rwkv_" + n][0]
    a["rwkv_mu"] = tiles_of(i["rwkv_mu"][0])
    names = ("w0", "a0", "k_k", "k_a", "r_k", "ln_w", "ln_b")
    a["rwkv_params"] = c(np.stack([tiles_of(i["rwkv_" + n][0].reshape(-1)) for n in names], 2))
    a["gla_w2"], a["gla_b"] = i["gla_w2"][0], c(i["gla_b"][0].reshape(-1, 1))
    for n in ("gla", "hgrn"):
        g = i[n + "_norm_w"][0]
        a["k_" + n + "_gain"] = c(np.stack([np.concatenate([g, g])] * 2, 1))
    a.update({"k_" + n: v for n, v in constants().items()})
    return a


def kernel(**inputs):
    import concourse.bacc as bacc
    from concourse.bass_utils import run_bass_kernel_spmd

    arrays = {n: np.ascontiguousarray(v) for n, v in layout({n: np.asarray(v) for n, v in inputs.items()}).items()}
    nc = bacc.Bacc("TRN2", target_bir_lowering=False, num_devices=1, dynamic_dma_scratch_size=KB)
    a = {n: nc.dram_tensor("in_" + n, v.shape, mybir.dt.from_np(v.dtype), kind="ExternalInput").ap()
         for n, v in arrays.items()}
    out = nc.dram_tensor("out", (D, T), F32, kind="ExternalOutput").ap()
    program(nc, a, out)
    r = run_bass_kernel_spmd(nc, [{"in_" + n: v for n, v in arrays.items()}], core_ids=[0])
    return r.results[0]["out"].T.reshape(1, T, D)
```
